# Optimizing a Trainium2 kernel written in Bass

```python
import math
import jax, jax.numpy as jnp
from jax import lax
import numpy as np

D_MODEL = 1024
BATCH = 1
SEQ = 256
DEPTH = 1

MIX_WIDTH = D_MODEL
ATTN_HEAD_DIM = 64
ATTN_WIDTH = MIX_WIDTH // 2
ATTN_HEADS = ATTN_WIDTH // ATTN_HEAD_DIM
RWKV_HEAD_DIM = 64
RWKV_WIDTH = MIX_WIDTH - ATTN_WIDTH
RWKV_HEADS = RWKV_WIDTH // RWKV_HEAD_DIM
DILATED_PATTERNS = ((128, 1), (512, 4), (2048, 16))
ATTN_BLOCK = 128
DECAY_LORA = 64
ICLR_LORA = 64
GATE_LORA = 128
N_EXPERTS = 32
TOP_K = 4
D_FF = D_MODEL
SWIGLU_LIMIT = 7.0
SWIGLU_ALPHA = 1.702
MOE_BLOCK = 256
RMS_EPS = 1e-5
GN_EPS = 64e-5
SHIFT_WIDTH = 3 * RWKV_WIDTH + DECAY_LORA + ICLR_LORA + GATE_LORA
IN_WIDTH = 3 * ATTN_WIDTH + SHIFT_WIDTH

kernel_name = "hybrid_dilated_attn_rwkv7_moe"

F32 = jnp.float32

def rmsnorm(x, g):
    x32 = x.astype(F32)
    y = x32 * lax.rsqrt(jnp.mean(x32 * x32, axis=-1, keepdims=True) + RMS_EPS)
    return (y * g.astype(F32)).astype(x.dtype)

def token_shift(z):
    return jnp.pad(z[:, :-1], ((0, 0), (1, 0), (0, 0)))

def alibi_slopes(n_heads):
    return jnp.exp2(-8.0 / n_heads * jnp.arange(1, n_heads + 1, dtype=F32))

def dilated_window(q, k, v, slopes, window, dil):
    B, S, H, Dh = q.shape
    steps = window // dil
    C = ATTN_BLOCK
    n_sub = -(-S // dil)
    nb = -(-n_sub // C)
    Sp = nb * C * dil
    pad = ((0, 0), (0, Sp - S), (0, 0), (0, 0))

    def to_blocks(t):
        t = jnp.pad(t, pad).reshape(B, nb, C, dil, H, Dh)
        return t.transpose(0, 3, 4, 1, 2, 5)

    qb, kb, vb = to_blocks(q), to_blocks(k), to_blocks(v)
    shift = lambda t: jnp.pad(t[:, :, :, :-1], ((0, 0), (0, 0), (0, 0), (1, 0), (0, 0), (0, 0)))
    kk = jnp.concatenate([shift(kb), kb], axis=4)
    vv = jnp.concatenate([shift(vb), vb], axis=4)

    scale = 1.0 / math.sqrt(Dh)
    s = jnp.einsum('brhnqe,brhnke->brhnqk', qb, kk, preferred_element_type=F32) * scale
    diff = (jnp.arange(C)[:, None] + C) - jnp.arange(2 * C)[None, :]
    band = (diff >= 0) & (diff <= steps)
    first_ok = (jnp.arange(nb)[:, None, None] > 0) | (jnp.arange(2 * C)[None, None, :] >= C)
    valid = band[None] & first_ok
    bias = -slopes[:, None, None] * (dil * diff).astype(F32)[None]
    s = s + bias[None, None, :, None]
    s = jnp.where(valid[None, None, None], s, -jnp.inf)
    m = jnp.max(s, axis=-1, keepdims=True)
    p = jnp.exp(s - m)
    den = jnp.sum(p, axis=-1, keepdims=True)
    o = jnp.einsum('brhnqk,brhnke->brhnqe', p, vv.astype(F32)) / den
    lse = (m + jnp.log(den))[..., 0]
    o = o.transpose(0, 3, 4, 1, 2, 5).reshape(B, Sp, H, Dh)[:, :S]
    lse = lse.transpose(0, 3, 4, 1, 2).reshape(B, Sp, H)[:, :S]
    return o, lse

def dilated_attention(q, k, v):
    slopes = alibi_slopes(q.shape[2])
    outs, lses = [], []
    for window, dil in DILATED_PATTERNS:
        o, l = dilated_window(q, k, v, slopes, window, dil)
        outs.append(o)
        lses.append(l)
    wts = jax.nn.softmax(jnp.stack(lses, 0), axis=0)
    return jnp.sum(wts[..., None] * jnp.stack(outs, 0), axis=0)

def rwkv7_mix(r, k, v, wd, ad, gd, decay_w0, w_decay_up, iclr_a0, w_iclr_up, w_gate_lr_up,
              k_k, k_a, r_k, gn_w, gn_b):
    B, S, W = r.shape
    H, N = RWKV_HEADS, RWKV_HEAD_DIM
    w = -jax.nn.softplus(-(decay_w0 + jnp.tanh(wd) @ w_decay_up)) - 0.5
    decay = jnp.exp(-jnp.exp(w))
    a = jax.nn.sigmoid(iclr_a0 + ad @ w_iclr_up)
    g = jax.nn.sigmoid(gd) @ w_gate_lr_up
    heads = lambda t: t.reshape(B, S, H, N)
    kk = heads(k * k_k)
    kk = kk / jnp.maximum(jnp.sqrt(jnp.sum(kk * kk, -1, keepdims=True)), 1e-12)
    k = k * (1.0 + (a - 1.0) * k_a)
    rh, wh, kh, vh, ah = heads(r), heads(decay), heads(k), heads(v), heads(a)

    def step(state, inp):
        r_t, w_t, k_t, v_t, kk_t, a_t = inp
        sa = jnp.einsum('bhij,bhj->bhi', state, kk_t)
        state = (state * w_t[:, :, None, :]
                 - sa[..., None] * (kk_t * a_t)[:, :, None, :]
                 + v_t[..., None] * k_t[:, :, None, :])
        return state, jnp.einsum('bhij,bhj->bhi', state, r_t)

    xs = tuple(jnp.moveaxis(t, 1, 0) for t in (rh, wh, kh, vh, kk, ah))
    state0 = jnp.zeros((B, H, N, N), F32)
    _, ys = lax.scan(step, state0, xs)
    y = jnp.moveaxis(ys, 0, 1)
    mu = jnp.mean(y, -1, keepdims=True)
    var = jnp.mean(jnp.square(y - mu), -1, keepdims=True)
    yn = ((y - mu) * lax.rsqrt(var + GN_EPS)).reshape(B, S, W) * gn_w + gn_b
    bonus = (jnp.sum(rh * kh * r_k, -1, keepdims=True) * vh).reshape(B, S, W)
    return (yn + bonus) * g

def moe_ffn(xn, w_router, b_router, w_gate_up, b_gate_up, w_down, b_down):
    Bsz, S, D = xn.shape
    n_tok = Bsz * S
    xf = xn.reshape(n_tok, D)
    logits = jnp.matmul(xf, w_router, preferred_element_type=F32) + b_router.astype(F32)
    top_val, top_idx = lax.top_k(logits, TOP_K)
    gates = jax.nn.softmax(top_val, axis=-1)
    n_assign = n_tok * TOP_K
    e_flat = top_idx.reshape(n_assign).astype(jnp.int32)
    g_flat = gates.reshape(n_assign)
    t_flat = jnp.repeat(jnp.arange(n_tok, dtype=jnp.int32), TOP_K)
    order = jnp.argsort(e_flat)
    e_s, t_s, g_s = e_flat[order], t_flat[order], g_flat[order]
    counts = jnp.bincount(e_flat, length=N_EXPERTS)
    padded = (counts + MOE_BLOCK - 1) // MOE_BLOCK * MOE_BLOCK
    start = jnp.cumsum(counts) - counts
    pend = jnp.cumsum(padded)
    pstart = pend - padded
    dest = pstart[e_s] + (jnp.arange(n_assign, dtype=jnp.int32) - start[e_s])
    n_blocks = (n_assign + N_EXPERTS * (MOE_BLOCK - 1) + MOE_BLOCK - 1) // MOE_BLOCK
    n_rows = n_blocks * MOE_BLOCK
    row_tok = jnp.full((n_rows,), n_tok, jnp.int32).at[dest].set(t_s)
    row_gate = jnp.zeros((n_rows,), F32).at[dest].set(g_s)
    blk_expert = jnp.minimum(
        jnp.searchsorted(pend, jnp.arange(n_blocks, dtype=pend.dtype) * MOE_BLOCK, side='right'),
        N_EXPERTS - 1)
    xpad = jnp.concatenate([xf, jnp.zeros((1, D), xf.dtype)], axis=0)

    def expert_block(args):
        tok, gate, e = args
        hb = xpad[tok]
        gu = hb @ w_gate_up[e] + b_gate_up[e]
        g_lin = jnp.minimum(gu[:, :D_FF], SWIGLU_LIMIT)
        u_lin = jnp.clip(gu[:, D_FF:], -SWIGLU_LIMIT, SWIGLU_LIMIT)
        act = (u_lin + 1.0) * (g_lin * jax.nn.sigmoid(SWIGLU_ALPHA * g_lin))
        out = act @ w_down[e] + b_down[e]
        return out.astype(F32) * gate[:, None]

    outs = lax.map(expert_block, (row_tok.reshape(n_blocks, MOE_BLOCK),
                                  row_gate.reshape(n_blocks, MOE_BLOCK), blk_expert))
    y = jnp.zeros((n_tok + 1, D), F32).at[row_tok].add(outs.reshape(n_rows, D))
    return y[:n_tok].reshape(Bsz, S, D).astype(xn.dtype)

def setup_inputs(seed: int = 0) -> dict:
    key = jax.random.key(seed)
    ks = jax.random.split(key, 24)
    L = DEPTH
    nrm = lambda k, shape, scale: jax.random.normal(k, shape, F32) * scale
    return {
        "x": nrm(ks[0], (BATCH, SEQ, D_MODEL), 1.0),
        "norm_mix_g": 1.0 + nrm(ks[1], (L, D_MODEL), 0.02),
        "w_in": nrm(ks[2], (L, D_MODEL, IN_WIDTH), D_MODEL ** -0.5),
        "shift_mu": jax.random.uniform(ks[3], (L, SHIFT_WIDTH), F32, 0.2, 0.8),
        "decay_w0": -0.6 + nrm(ks[4], (L, RWKV_WIDTH), 0.3),
        "w_decay_up": nrm(ks[5], (L, DECAY_LORA, RWKV_WIDTH), 0.1),
        "iclr_a0": nrm(ks[6], (L, RWKV_WIDTH), 0.1),
        "w_iclr_up": nrm(ks[7], (L, ICLR_LORA, RWKV_WIDTH), 0.1),
        "w_gate_lr_up": nrm(ks[8], (L, GATE_LORA, RWKV_WIDTH), GATE_LORA ** -0.5),
        "k_k": 0.85 + nrm(ks[9], (L, RWKV_WIDTH), 0.02),
        "k_a": 1.0 + nrm(ks[10], (L, RWKV_WIDTH), 0.02),
        "r_k": nrm(ks[11], (L, RWKV_HEADS, RWKV_HEAD_DIM), 0.1),
        "gn_w": 1.0 + nrm(ks[12], (L, RWKV_WIDTH), 0.02),
        "gn_b": nrm(ks[13], (L, RWKV_WIDTH), 0.01),
        "w_out": nrm(ks[14], (L, MIX_WIDTH, D_MODEL), MIX_WIDTH ** -0.5),
        "norm_ffn_g": 1.0 + nrm(ks[15], (L, D_MODEL), 0.02),
        "w_router": nrm(ks[16], (L, D_MODEL, N_EXPERTS), D_MODEL ** -0.5),
        "b_router": nrm(ks[17], (L, N_EXPERTS), 0.01),
        "w_gate_up": nrm(ks[18], (L, N_EXPERTS, D_MODEL, 2 * D_FF), D_MODEL ** -0.5),
        "b_gate_up": nrm(ks[19], (L, N_EXPERTS, 2 * D_FF), 0.01),
        "w_down": nrm(ks[20], (L, N_EXPERTS, D_FF, D_MODEL), D_FF ** -0.5),
        "b_down": nrm(ks[21], (L, N_EXPERTS, D_MODEL), 0.01),
        "norm_final_g": 1.0 + nrm(ks[22], (D_MODEL,), 0.02),
    }

def reference(x, norm_mix_g, w_in, shift_mu, decay_w0, w_decay_up, iclr_a0, w_iclr_up,
              w_gate_lr_up, k_k, k_a, r_k, gn_w, gn_b, w_out, norm_ffn_g, w_router, b_router,
              w_gate_up, b_gate_up, w_down, b_down, norm_final_g):
    B, S, _ = x.shape
    h = x
    for l in range(DEPTH):
        xn = rmsnorm(h, norm_mix_g[l])
        proj = xn @ w_in[l]
        qa, ka, va = jnp.split(proj[..., :3 * ATTN_WIDTH], 3, axis=-1)
        rest = proj[..., 3 * ATTN_WIDTH:].astype(F32)
        rest = rest + (token_shift(rest) - rest) * shift_mu[l]
        o1 = RWKV_WIDTH
        r_, k_, v_ = rest[..., :o1], rest[..., o1:2 * o1], rest[..., 2 * o1:3 * o1]
        wd = rest[..., 3 * o1:3 * o1 + DECAY_LORA]
        ad = rest[..., 3 * o1 + DECAY_LORA:3 * o1 + DECAY_LORA + ICLR_LORA]
        gd = rest[..., 3 * o1 + DECAY_LORA + ICLR_LORA:]

        hd = lambda t: t.reshape(B, S, ATTN_HEADS, ATTN_HEAD_DIM)
        attn = dilated_attention(hd(qa), hd(ka), hd(va)).reshape(B, S, ATTN_WIDTH)
        rw = rwkv7_mix(r_, k_, v_, wd, ad, gd,
                       decay_w0[l].astype(F32), w_decay_up[l].astype(F32), iclr_a0[l].astype(F32),
                       w_iclr_up[l].astype(F32), w_gate_lr_up[l].astype(F32), k_k[l].astype(F32),
                       k_a[l].astype(F32), r_k[l].astype(F32), gn_w[l].astype(F32), gn_b[l].astype(F32))
        mixed = jnp.concatenate([attn.astype(h.dtype), rw.astype(h.dtype)], axis=-1) @ w_out[l]
        h = h + mixed
        h = h + moe_ffn(rmsnorm(h, norm_ffn_g[l]), w_router[l], b_router[l], w_gate_up[l],
                        b_gate_up[l], w_down[l], b_down[l])
    return rmsnorm(h, norm_final_g)


_drawn_inputs = setup_inputs


def setup_inputs(seed=0):
    import zlib

    import numpy as np

    out = dict(_drawn_inputs(seed))
    spreads = {}
    factors = {'k_k': 6.081, 'b_gate_up': 8.0, 'b_down': 8.0, 'norm_final_g': 2.819}
    for name, (base, spread) in spreads.items():
        noise = np.random.default_rng([zlib.crc32(name.encode()), seed]).standard_normal(out[name].shape)
        drawn = base * np.exp(spread * noise) if base else spread * noise
        out[name] = __import__('jax').numpy.asarray(drawn.astype(out[name].dtype))
    for name, factor in factors.items():
        out[name] = (out[name] * factor).astype(out[name].dtype)
    return out
```

```python
from contextlib import ExitStack

import numpy as np
import concourse.bass as bass
from concourse import mybir

F32 = mybir.dt.float32
BF16 = mybir.dt.bfloat16
I32 = mybir.dt.int32
U32 = mybir.dt.uint32
ALU = mybir.AluOpType
ACT = mybir.ActivationFunctionType
AX = mybir.AxisListType

P = 128
D = 1024
SEQ = 256
NT = SEQ // P
KT = D // P
AW = 512
RW = 512
HD = 64
H = 8
FT = RW // P
LORA = 256
IN_W = 3 * AW + 3 * RW + LORA
CH = 64
NCH = SEQ // CH
LEVELS = 6
E = 32
TOPK = 4
FF = 1024
SLOTS = 64
EXTRA = 16
ITEMS = E + EXTRA
CHUNK = 4096
RING = 6
LIMIT = 7.0
ALPHA = 1.702
RMS_EPS = 1e-5
GN_EPS = 64e-5
DECAY_C = float(np.exp(-0.5))
NV = 14 + 7 * FT
PATTERNS = ((128, 1), (512, 4), (2048, 16))

C_IDENT, C_ONES, C_MEAN, C_SCAN = 0, 128, 256, 384
C_EYE2 = 640
C_MASK4 = 704
C_LEVEL = C_MASK4 + 512
C_A = C_LEVEL + LEVELS * 128
C_IOTA2, C_TRI, C_ONE, C_IOTA32, C_ECOL, C_J = 0, 128, 256, 384, 416, 417
C_B = 440


def shape_constants():
    a = np.zeros((P, C_A), np.float32)
    t = np.arange(P)
    same = (t[:, None] // CH) == (t[None, :] // CH)
    a[:, C_IDENT:C_IDENT + P] = np.eye(P)
    a[:, C_ONES:C_ONES + P] = (t[:, None] // HD) == (t[None, :] // HD)
    a[:, C_MEAN:C_MEAN + P] = a[:, C_ONES:C_ONES + P] / HD
    a[:, C_SCAN:C_SCAN + SEQ] = (np.arange(SEQ) % CH) != 0
    a[:, C_EYE2:C_EYE2 + HD] = np.tile(np.eye(HD), (2, 1))

    def level(n):
        return ((t[:, None] >> n) == (t[None, :] >> n)) & (((t[:, None] >> (n - 1)) & 1) == 1) & (((t[None, :] >> (n - 1)) & 1) == 0)

    strict = (t[:, None] < t[None, :]) & same
    incl = (t[:, None] <= t[None, :]) & same
    for n, m in enumerate((level(1).T, incl, strict, incl)):
        a[:, C_MASK4 + n * P:C_MASK4 + (n + 1) * P] = m
    for n in range(LEVELS):
        a[:, C_LEVEL + n * P:C_LEVEL + (n + 1) * P] = level(n + 1)

    dist = P + t[:, None] - np.arange(SEQ)[None, :]
    times = np.zeros(dist.shape, np.float64)
    for window, dil in PATTERNS:
        times += (dist >= 0) & (dist <= window) & (dist % dil == 0)
    bias = np.empty((P, H, SEQ), np.float32)
    for h in range(H):
        slope = 2.0 ** (-8.0 / H * (h + 1))
        bias[:, h] = np.where(times > 0, -slope * dist + np.log(np.maximum(times, 1)), -1e30)

    b = np.zeros((P, C_B), np.float32)
    b[:, C_IOTA2:C_IOTA2 + P] = np.tile(np.arange(SLOTS), 2)
    b[:, C_TRI:C_TRI + P] = t[:, None] < t[None, :]
    b[:, C_ONE:C_ONE + P] = 1.0
    b[:, C_IOTA32:C_IOTA32 + E] = np.arange(E)
    b[:, C_ECOL] = t
    b[:, C_J:C_J + EXTRA] = np.arange(EXTRA)
    return a, bias.reshape(P, H * SEQ), b


def program(nc, x, g_mix, w_in, mu, w0, w_dec, a0, w_icl, w_gat, k_k, k_a, r_k, gn_w, gn_b, w_out, g_ffn, w_router,
            b_router, w_gu, b_gu, w_dn, b_dn, g_fin, const_a, const_bias, const_b, out):
    with ExitStack() as ctx:
        def sb(name, shape, dt=F32):
            return ctx.enter_context(nc.sbuf_tensor(name, shape, dt))

        def sem(name):
            return ctx.enter_context(nc.semaphore(name))

        ring = sb("ring", [P, RING, CHUNK])
        resid = sb("resid", [P, NT, D])
        arena = sb("arena", [P, 12, 1024])
        attn = sb("attn", [P, 3, 1024])
        stage = sb("stage", [P, 4, 1024])
        zpad = sb("zpad", [P, 2, 2, SEQ + 1])
        lora = sb("lora", [P, 2, SEQ])
        mixT = sb("mixT", [P, KT, SEQ])
        ca = sb("ca", [P, C_A])
        cb = sb("cb", [P, C_B])
        vrow = sb("vrow", [NV, P])
        vcol = sb("vcol", [P, NV])
        gmix = sb("gmix", [P, KT])
        gffn = sb("gffn", [P, KT])
        st = sb("st", [P, 96])
        wrt = sb("wrt", [P, KT, E])
        brt = sb("brt", [P, E])

        bank = [ctx.enter_context(nc.psum_tensor(f"bank{i}", [P, 512], F32)) for i in range(8)]

        ident = ca[:, C_IDENT:C_IDENT + P]
        head_ones = ca[:, C_ONES:C_ONES + P]
        head_mean = ca[:, C_MEAN:C_MEAN + P]
        scan_keep = ca[:, C_SCAN:C_SCAN + SEQ]
        eye2 = ca[:, C_EYE2:C_EYE2 + HD]
        mask4 = ca[:, C_MASK4:C_MASK4 + 512]

        def level_mask(n):
            return ca[:, C_LEVEL + (n - 1) * P:C_LEVEL + n * P].unsqueeze(1).to_broadcast([P, 4, P])

        def blk(i, n=1):
            return arena[:, i:i + n, :].rearrange("p b c -> p (b c)")

        def tiles(ap):
            return ap.rearrange("p (f t) -> p f t", t=SEQ)

        B_R, B_S, B_I, B_X, B_KK, B_G, B_C, B_AR, B_A, B_K, B_V = 0, 1, 2, 3, 4, 5, 6, 7, 9, 10, 11
        rT, kT, vT = blk(B_R), blk(B_K), blk(B_V)
        sw = blk(B_S)
        cum = blk(B_C)
        pinv = blk(B_I)
        tmp = blk(B_X)
        kkT = blk(B_KK)
        gT = blk(B_G)
        aT = blk(B_A)
        ar = blk(B_AR, 2).rearrange("p (f w t) -> p f w t", w=2, t=SEQ)
        xn = arena[:, B_R:B_R + 2, :]
        xT = stage[:, 0:2, :].rearrange("p b c -> p (b c)").rearrange("p (k t) -> p k t", t=SEQ)
        wlo = stage[:, 2:4, :].rearrange("p b c -> p (b c)").rearrange("p (k n) -> p k n", n=LORA)
        qA, kA = tiles(attn[:, 0, :]), tiles(attn[:, 1, :])
        vA = attn[:, 2, :].rearrange("p (t n) -> p t n", n=AW)

        slot = [ring[:, i, :].rearrange("p (k n) -> p k n", k=KT) for i in range(RING)]
        work = ring[:, 2:4, :].rearrange("p b c -> p (b c)")
        amv = work[:, 0:2048].rearrange("p (t h w j) -> p t h w j", t=NT, h=H, w=2)
        btok = work[:, 2048:3072].rearrange("p (t n) -> p t n", t=NT)
        ktok = work[:, 3072:4096].rearrange("p (t n) -> p t n", t=NT)
        vtok = work[:, 4096:5120].rearrange("p (t n) -> p t n", t=NT)
        abias = work[:, 5120:7168].rearrange("p (h s) -> p h s", h=H)
        ux = [work[:, 5120 + 1024 * g:6144 + 1024 * g].rearrange("p (i w s) -> p i w s", i=4, w=2) for g in range(2)]
        low = [work[:, 7168 + 512 * g:7680 + 512 * g].rearrange("p (i s) -> p i s", i=4) for g in range(2)]
        mflat = mixT[:, :, :].rearrange("p k t -> p (k t)")
        wlor_d = mflat[:, 0:RW]
        wgt = mflat[:, RW:2 * RW]
        wo = ring[:, 4:6, :].rearrange("p b c -> p (b c)").rearrange("p (m n) -> p m n", m=KT)

        sflat = stage[:, :, :].rearrange("p b c -> p (b c)")
        sc_s = [sflat[:, 384 * i:384 * i + 384] for i in range(2)]
        sc_e = [sflat[:, 768 + 384 * i:1152 + 384 * i] for i in range(2)]
        sc_t = [sflat[:, 1536 + 384 * i:1920 + 384 * i] for i in range(2)]
        nm = [sflat[:, 2048 * g:2048 * g + 2048].rearrange("p (i w s) -> p i w s", i=4, w=4) for g in range(2)]
        t1s = [blk(B_S)[:, 512 * g:512 * g + 512].rearrange("p (i s) -> p i s", i=4) for g in range(2)]
        lml = [blk(B_R)[:, 512 * g:512 * g + 512].rearrange("p (i s) -> p i s", i=4) for g in range(2)]
        nzw = [blk(B_I)[:, 512 * g:512 * g + 512].rearrange("p (i s) -> p i s", i=4) for g in range(2)]
        gg = tiles(blk(B_X))
        yT = tiles(zpad[:, :, :, :].rearrange("p a b c -> p (a b c)")[:, 0:1024])
        tt = attn[:, 1, :].rearrange("p (c f j) -> p c f j", c=NCH, f=FT)
        state = attn[:, 2, :].rearrange("p (c f i) -> p c f i", c=NCH, f=FT)
        stmp = attn[:, 0, 0:FT * HD].rearrange("p (f i) -> p f i", f=FT)
        yc = blk(B_S)
        ysq = blk(B_R)

        xs = arena[:, B_R:B_R + 2, :]
        xsplit = attn[:, :, :].rearrange("p b c -> p (b c)").bitcast(BF16).rearrange("p (t s n) -> p t s n", t=NT, s=3)
        hT = stage[:, 0:2, :].rearrange("p b c -> p (b c)").rearrange("p (k t) -> p k t", t=SEQ)
        gfin = stage[:, 2, :]
        yout = arena[:, B_R:B_R + 2, :]
        braw = blk(B_AR, 3)
        bsp = blk(B_K, 2).bitcast(BF16)[:, 0:3 * D]
        bmid = stage[0:E, 0:2, :].rearrange("p b c -> p (b c)").bitcast(BF16)[:, 0:3 * D]
        mz = blk(B_I, 5)
        m_g, m_u, m_t, m_s, m_a, m_at, m_os, m_xg = (mz[:, 512 * i:512 * i + 512] for i in range(8))
        m_gt, m_g2 = mz[:, 4096:4352], mz[:, 4352:4608].rearrange("p (t c) -> p t c", t=NT)
        m_p = mz[:, 4608:4672].bitcast(BF16).rearrange("p (t c) -> p t c", t=NT)
        m_sel = mz[:, 4672:4704].bitcast(BF16)
        rs = stage[:, 3, :]
        rint = sb("rint", [P, 80], I32)
        idx8 = sb("idx8", [P, NT, 8], U32)
        lg = rs[:, 0:64].rearrange("p (t e) -> p t e", t=NT)
        mx8 = rs[:, 64:80].rearrange("p (t e) -> p t e", t=NT)
        idxf = rs[:, 80:96].rearrange("p (t e) -> p t e", t=NT)
        ex4 = rs[:, 96:104].rearrange("p (t e) -> p t e", t=NT)
        gt4 = rs[:, 104:112].rearrange("p (t e) -> p t e", t=NT)
        onehot = rs[:, 112:368].rearrange("p (t j e) -> p t j e", t=NT, j=TOPK)
        picked = rs[:, 368:432].rearrange("p (t e) -> p t e", t=NT)
        gates = rs[:, 432:496].rearrange("p (t e) -> p t e", t=NT)
        slotv = rs[:, 496:560].rearrange("p (t e) -> p t e", t=NT)
        extra = rs[0:E, 560:563]
        cnt = rs[0:E, 563:564]
        startc = rs[0:E, 564:565]
        dj = rs[0:E, 566:566 + EXTRA]
        oh = rs[0:E, 584:584 + ITEMS]
        back = rs[0:E, 632:632 + ITEMS]
        colv = rs[:, 680:680 + 2 * (ITEMS + 2)].rearrange("p (t i) -> p t i", t=NT)
        gcol = rs[:, 780:780 + 2 * (ITEMS + 2)].rearrange("p (t i) -> p t i", t=NT)
        oh3 = sb("oh3", [P, ITEMS + 2], BF16)
        svT = mz[0:E, 512:1024].rearrange("p (w t) -> p w t", w=2)

        names = ("x_in ca_in vec_in wlo_in up_in bias_in cb_in wo_in braw_in route_in gfin_in out_done "
                 "v_chain a_chain p_chain xn_done xt_pe xt_done vt_pe vt_done proj_pe zcopy zshift zpad0 tanh_done sgd_done "
                 "dec_pe icl_pe gat_pe sdec_done sicl_done gat_done exps_done sq_done ss_pe nrm_done bprod_done bsum_pe "
                 "bonus_done tilde_done tok_pe tok_done s_pe s_max e_done en_done et_pe et_done pv_pe attn_done "
                 "gram_pe nm_done low_pe low_done ux_done lml_done t1_pe t1_done d_pe mv_pe mv_done zw_pe zw_done gc_pe gc_done "
                 "q_pe q_done u_pe u_done st_pe st_done yp_pe y_done mu_pe yc_done ysq_done var_pe sd_done mix_done wo_pe h_done "
                 "xs_done ht_pe ht_done lg_pe lg_done ex_done pick_done rank_pe slot_done extra_done start_pe oh_done svt_pe "
                 "svt_done col_pe col_done items_done split_done bsp_done moe_zero yinit_pe hsq_done "
                 "p_ready ga_pe xg_ready sel_ready gu_pe gm_done sg_done act_done tr_pe at_done g2_ready gtt_pe gt_done dn_pe os_done "
                 "sc_pe scf_pe fsq_done fin_done v_fs um_done t_done").split()
        s = {n: sem(n) for n in names}
        s_win = [sem(f"win_in{i}") for i in range(RING)]
        s_ring = [sem(f"ring_in{i}") for i in range(RING)]
        s_free = [sem(f"ring_free{i}") for i in range(RING)]

        block = ctx.enter_context(nc.Block())

        groups = [(t, q) for t in range(NT) for q in range(2)]
        VL = dict(mu=0, w0=14, a0=18, kk=22, ka=26, rk=30, gw=34, gb=38)

        def vec(name, f):
            c = VL[name] + f
            return vcol[:, c:c + 1]

        def expert_chunk(e, c):
            if c < 4:
                return w_gu[0, e].rearrange("(p c t) n -> c p (t n)", c=4, t=2)[c]
            return w_dn[0, e].rearrange("(h p t) n -> h p (t n)", h=2, t=4)[c - 4]

        @block.sync
        def _(sp):
            for t in range(NT):
                sp.dma_start(resid[:, t, :], x[0, P * t:P * t + P, :]).then_inc(s["x_in"], 16)
            sp.dma_start(gmix[:, :], g_mix[0].rearrange("(p k) -> p k", k=KT)).then_inc(s["ca_in"], 16)
            sp.dma_start(ca[:, :], const_a).then_inc(s["ca_in"], 16)
            sp.dma_start(wlo, w_in[0].rearrange("(p k) n -> p k n", k=KT)[:, :, 3 * AW + 3 * RW:IN_W]).then_inc(s["wlo_in"], 16)
            rows = [(mu[0], 14), (w0[0], FT), (a0[0], FT), (k_k[0], FT), (k_a[0], FT),
                    (r_k[0].rearrange("h j -> (h j)"), FT), (gn_w[0], FT), (gn_b[0], FT)]
            at = 0
            for src, n in rows:
                sp.dma_start(vrow[at:at + n, :], src.rearrange("(r c) -> r c", c=P)).then_inc(s["vec_in"], 16)
                at += n
            order = [3, 4, 5, 0, 1, 2]
            for c in range(RING):
                cols = slice(AW * order[c], AW * order[c] + AW)
                sp.dma_start(slot[c], w_in[0].rearrange("(p k) n -> p k n", k=KT)[:, :, cols]).then_inc(s_win[c], 16)
                if c == 0:
                    sp.dma_start(wlor_d[0:64, :], w_dec[0]).then_inc(s["up_in"], 16)
                    sp.dma_start(wlor_d[64:128, :], w_icl[0]).then_inc(s["up_in"], 16)
                    sp.dma_start(wgt[:, :], w_gat[0]).then_inc(s["up_in"], 16)
            sp.dma_start(cb[:, :], const_b).then_inc(s["cb_in"], 16)
            sp.dma_start(gffn[:, :], g_ffn[0].rearrange("(p k) -> p k", k=KT)).then_inc(s["cb_in"], 16)
            sp.dma_start(wrt[:, :, :], w_router[0].rearrange("(p k) e -> p k e", k=KT)).then_inc(s["route_in"], 16)
            sp.dma_start(brt[:, :], b_router[0:1, :].to_broadcast([P, E])).then_inc(s["route_in"], 16)
            sp.wait_ge(s["proj_pe"], 9)
            sp.dma_start(abias, const_bias.rearrange("p (h s) -> p h s", h=H)).then_inc(s["bias_in"], 16)
            for c in (0, 1):
                sp.dma_start(ring[:, c, :], expert_chunk(0, c)).then_inc(s_ring[c], 16)
            sp.wait_ge(s["proj_pe"], 13)
            sp.dma_start(wo, w_out[0].rearrange("(m p) n -> p m n", p=P)).then_inc(s["wo_in"], 16)
            sp.wait_ge(s["q_done"], 4)
            sp.wait_ge(s["gc_done"], 4)
            sp.dma_start(braw[0:E, 0:2 * FF], b_gu[0]).then_inc(s["braw_in"], 16)
            sp.dma_start(braw[0:E, 2 * FF:3 * FF], b_dn[0]).then_inc(s["braw_in"], 16)
            sp.wait_ge(s["u_done"], 3)
            for c in (2, 3):
                sp.dma_start(ring[:, c, :], expert_chunk(0, c)).then_inc(s_ring[c], 16)
            sp.dma_start(gfin, g_fin.unsqueeze(0).to_broadcast([P, D])).then_inc(s["gfin_in"], 16)
            sp.wait_ge(s["wo_pe"], 4)
            for c in (4, 5):
                sp.dma_start(ring[:, c, :], expert_chunk(0, c)).then_inc(s_ring[c], 16)
            sp.wait_ge(s["items_done"], 1)
            n_items = sp.value_load(rint[0:1, ITEMS:ITEMS + 1], min_val=E, max_val=ITEMS)
            with sp.Fori(1, n_items) as i:
                e = sp.value_load(rint[0:1, bass.ds(i, 1)], min_val=0, max_val=E - 1)
                gu = w_gu[0, bass.ds(e, 1)].rearrange("e (p c t) n -> c p (e t n)", c=4, t=2)
                dn = w_dn[0, bass.ds(e, 1)].rearrange("e (h p t) n -> h p (e t n)", h=2, t=4)
                for c in range(RING):
                    sp.wait_ge(s_free[c], i)
                    sp.dma_start(ring[:, c, :], gu[c] if c < 4 else dn[c - 4]).then_inc(s_ring[c], 16)
            for t in range(NT):
                sp.wait_ge(s["fin_done"], t + 1)
                sp.dma_start(out[0, P * t:P * t + P, :], yout[:, t, :]).then_inc(s["out_done"], 16)
            sp.wait_ge(s["out_done"], 16 * NT)

        @block.tensor
        def _(pe):
            def mm(o, l, r, start=True, stop=True):
                return pe.matmul(o, l, r, start=start, stop=stop, skip_group_check=True)

            def model_transposes(src, ready, done):
                for u in range(4):
                    t, k0 = u // 2, 4 * (u % 2)
                    pe.wait_ge(ready, t + 1)
                    v = src[:, t, :].rearrange("p (q k) -> p k q", k=KT)
                    for k in range(4):
                        m = pe.transpose(bank[4 + u][:, P * k:P * k + P], v[:, k0 + k, :], ident)
                    m.then_inc(done, 1)

            pe.wait_ge(s["ca_in"], 32)
            model_transposes(xn, s["xn_done"], s["xt_pe"])
            pe.wait_ge(s["vec_in"], 16 * 8)
            pe.transpose(bank[3][:, 0:NV], vrow[:, :], ident[0:NV, 0:NV]).then_inc(s["vt_pe"], 1)
            pe.wait_ge(s["xt_done"], 4)
            pe.wait_ge(s["vt_done"], 1)

            def project(u):
                if u >= 4:
                    pe.wait_ge(s["zcopy"], u - 3)
                if u == 0:
                    pe.wait_ge(s["wlo_in"], 16)
                else:
                    pe.wait_ge(s_win[(u - 1) // 2], 16)
                b = bank[u % 4]
                if u >= 11:
                    t = u - 11
                    for k in range(KT):
                        m = mm(b[:, :], xT[:, k, P * t:P * t + P], slot[5][:, k, :], k == 0, k == KT - 1)
                else:
                    w, c0 = (wlo, 0) if u == 0 else (slot[(u - 1) // 2], 2 * P * ((u - 1) % 2))
                    for j in range(2):
                        for k in range(KT):
                            m = mm(b[:, SEQ * j:SEQ * j + SEQ], w[:, k, c0 + P * j:c0 + P * j + P], xT[:, k, :],
                                   k == 0, k == KT - 1)
                m.then_inc(s["proj_pe"], 1)

            project(0)
            project(1)
            pe.wait_ge(s["up_in"], 48)
            pe.wait_ge(s["tanh_done"], 1)
            for f in range(FT):
                m = mm(bank[4 + f // 2][:, SEQ * (f % 2):SEQ * (f % 2) + SEQ], wlor_d[0:64, P * f:P * f + P], lora[0:64, 0, :])
                if f % 2:
                    m.then_inc(s["dec_pe"], 1)
            for f in range(FT):
                m = mm(bank[6 + f // 2][:, SEQ * (f % 2):SEQ * (f % 2) + SEQ], wlor_d[64:128, P * f:P * f + P], lora[64:128, 0, :])
                if f % 2:
                    m.then_inc(s["icl_pe"], 1)
            project(2)
            project(3)
            pe.wait_ge(s["sgd_done"], 1)
            pe.wait_ge(s["sdec_done"], FT)
            for f in range(FT):
                m = mm(bank[4 + f // 2][:, SEQ * (f % 2):SEQ * (f % 2) + SEQ], wgt[:, P * f:P * f + P], lora[:, 1, :])
                if f % 2:
                    m.then_inc(s["gat_pe"], 1)
            for u in range(4, 7):
                project(u)
            pe.wait_ge(s["sq_done"], 1)
            pe.wait_ge(s["sicl_done"], FT)
            for j in range(2):
                mm(bank[6 + j][:, :], head_ones, tmp[:, 512 * j:512 * j + 512]).then_inc(s["ss_pe"], 1)
            for u in range(7, 13):
                project(u)
            pe.wait_ge(s["bprod_done"], 1)
            pe.wait_ge(s["gat_done"], 2)
            for j in range(2):
                mm(bank[4 + j][:, :], head_ones, tmp[:, 512 * j:512 * j + 512]).then_inc(s["bsum_pe"], 1)

            pe.wait_ge(s["tilde_done"], 4)
            pe.wait_ge(s["zcopy"], 13)
            for n in range(8):
                arr, t = n // 2, n % 2
                if n >= 4:
                    pe.wait_ge(s["tok_done"], n - 3)
                for f in range(FT):
                    src = (tiles(vT)[:, f, :], ar[:, f, 0, :], tiles(aT)[:, f, :], tiles(kT)[:, f, :])[arr]
                    m = pe.transpose(bank[n % 4][:, P * f:P * f + P], src[:, P * t:P * t + P], ident)
                m.then_inc(s["tok_pe"], 1)

            def scores(h):
                f, p0 = h // 2, HD * (h % 2)
                b = bank[4 + h % 2]
                if h >= 2:
                    pe.wait_ge(s["s_max"], 2 * (h - 1))
                mm(b[:, 0:P], qA[p0:p0 + HD, f, 0:P], kA[p0:p0 + HD, f, 0:P])
                mm(b[:, P:3 * P], qA[p0:p0 + HD, f, P:SEQ], kA[p0:p0 + HD, f, :]).then_inc(s["s_pe"], 1)

            def values(h):
                f, p0 = h // 2, HD * (h % 2)
                pe.wait_ge(s["en_done"], h + 1)
                if h >= 2:
                    pe.wait_ge(s["et_done"], h - 1)
                b = bank[6 + h % 2]
                for n in range(3):
                    m = pe.transpose(b[:, P * n:P * n + P], sc_e[h % 2][:, (0, P, 2 * P)[n]:(0, P, 2 * P)[n] + P], ident)
                m.then_inc(s["et_pe"], 1)
                pe.wait_ge(s["et_done"], h + 1)
                o = bank[f][p0:p0 + HD, 0:SEQ]
                mm(o, vA[:, 0, HD * h:HD * h + HD], sc_t[h % 2][:, 0:SEQ], True, False)
                mm(bank[f][p0:p0 + HD, P:SEQ], vA[:, 1, HD * h:HD * h + HD], sc_t[h % 2][:, SEQ:3 * P], False, True).then_inc(s["pv_pe"], 1)

            pe.wait_ge(s["bonus_done"], 1)
            pe.wait_ge(s["nrm_done"], 2)
            pe.wait_ge(s["tok_done"], 8)
            scores(0)
            scores(1)
            for h in range(H):
                values(h)
                if h + 2 < H:
                    scores(h + 2)

            pe.wait_ge(s["attn_done"], FT)
            pe.wait_ge(s["et_done"], H)
            for pair in range(2):
                for g in range(2):
                    n, (t, q) = 2 * pair + g, groups[2 * pair + g]
                    ts = slice(P * t, P * t + P)
                    for i in range(4):
                        f, p0, c = 2 * q + i // 2, HD * (i % 2), 4 * n + i
                        if c >= 2:
                            pe.wait_ge(s["nm_done"], c - 1)
                        if c == 8:
                            pe.wait_ge(s["y_done"], 1)
                            pe.wait_ge(s["st_done"], 1)
                        b = bank[c % 2]
                        mm(b[:, 0:2 * P], tiles(aT)[p0:p0 + HD, f, ts], ar[p0:p0 + HD, f, :, ts])
                        mm(b[:, 2 * P:4 * P], tiles(kT)[p0:p0 + HD, f, ts], ar[p0:p0 + HD, f, :, ts]).then_inc(s["gram_pe"], 1)
                        if pair == 1 and i == 0:
                            pe.wait_ge(s["zw_done"], g + 1)
                            pe.wait_ge(s["gc_done"], g + 1)
                        m = mm(bank[4 + 2 * g + i % 2][:, P * (i // 2):P * (i // 2) + P], ar[p0:p0 + HD, f, 0, ts],
                               tiles(aT)[p0:p0 + HD, f, ts])
                    m.then_inc(s["low_pe"], 1)
                for lv in range(2, LEVELS + 1):
                    for g in range(2):
                        n = 2 * pair + g
                        if lv == 2:
                            pe.wait_ge(s["q_done"], 2 * pair) if pair else None
                        pe.wait_ge(s["lml_done"], 10 * pair + 2 * (lv - 2) + g + 1)
                        pe.wait_ge(s["low_done"], 2 * n + 2)
                        pe.wait_ge(s["ux_done"], 24 * pair + (4 if lv == 2 else 4 + 4 * (lv - 2)) if g == 1 else
                                   24 * pair + (2 if lv == 2 else 2 + 4 * (lv - 2)))
                        for i in range(4):
                            m = mm(bank[2 + g][:, P * i:P * i + P], lml[g][:, i, :], ux[g][:, i, 0, :])
                        m.then_inc(s["t1_pe"], 1)
                    for g in range(2):
                        pe.wait_ge(s["t1_done"], 10 * pair + 2 * (lv - 2) + g + 1)
                        for i in range(4):
                            b = bank[4 + 2 * g + i // 2][:, 2 * P * (i % 2):2 * P * (i % 2) + 2 * P]
                            m = mm(b[:, 0:P], ux[g][:, i, 1, :], t1s[g][:, i, :])
                            if lv < LEVELS:
                                m = mm(b[:, P:2 * P], t1s[g][:, i, :], ux[g][:, i, 1, :])
                            if i % 2:
                                m.then_inc(s["d_pe"], 1)
                for g in range(2):
                    n, (t, q) = 2 * pair + g, groups[2 * pair + g]
                    for i in range(4):
                        h = 4 * q + i
                        m = mm(bank[2 + g][:, HD * i:HD * i + HD], nm[g][:, i, 2, :], vtok[:, t, HD * h:HD * h + HD])
                    m.then_inc(s["mv_pe"], 1)
                for g in range(2):
                    n, (t, q) = 2 * pair + g, groups[2 * pair + g]
                    pe.wait_ge(s["mv_done"], n + 1)
                    pe.wait_ge(s["ux_done"], 24 * pair + 22 + 2 * g)
                    for i in range(4):
                        m = mm(bank[4 + 2 * g][:, P * i:P * i + P], ux[g][:, i, 0, :], amv[:, t, 4 * q + i, :, :])
                    m.then_inc(s["zw_pe"], 1)
                for g in range(2):
                    n, (t, q) = 2 * pair + g, groups[2 * pair + g]
                    pe.wait_ge(s["zw_done"], n + 1)
                    b = bank[5 + 2 * g]
                    for i in range(4):
                        h, p0, c0 = 4 * q + i, HD * (i % 2), P * (i // 2)
                        mm(b[p0:p0 + HD, c0:c0 + P], nzw[g][:, i, 0:HD], nm[g][:, i, 1, :])
                        o = b[p0:p0 + HD, 2 * P + c0:3 * P + c0]
                        mm(o, vtok[:, t, HD * h:HD * h + HD], nm[g][:, i, 3, :], True, False)
                        m = mm(o, nzw[g][:, i, HD:2 * HD], nm[g][:, i, 1, :], False, True)
                    m.then_inc(s["gc_pe"], 1)
                t = pair
                for c in range(2):
                    rows = slice(HD * c, HD * c + HD)
                    for h in range(H):
                        f, p0 = h // 2, HD * (h % 2)
                        m = mm(bank[2 + c][p0:p0 + HD, HD * f:HD * f + HD], nzw[h // 4][rows, h % 4, 0:HD],
                               btok[rows, t, HD * h:HD * h + HD])
                m.then_inc(s["q_pe"], 1)
                pe.wait_ge(s["nm_done"], 8 * (pair + 1))
                for c in range(2 - pair):
                    rows = slice(HD * c, HD * c + HD)
                    for h in range(H):
                        f, p0 = h // 2, HD * (h % 2)
                        o = bank[c][p0:p0 + HD, HD * f:HD * f + HD]
                        mm(o, ktok[rows, t, HD * h:HD * h + HD], vtok[rows, t, HD * h:HD * h + HD], True, False)
                        m = mm(o, btok[rows, t, HD * h:HD * h + HD], nzw[h // 4][rows, h % 4, HD:2 * HD], False, True)
                    m.then_inc(s["u_pe"], 1)
                for cc in range(max(1, 2 * pair), 2 * pair + 2):
                    pe.wait_ge(s["u_done"], 2 + pair)
                    if cc >= 2:
                        pe.wait_ge(s["st_done"], cc - 1)
                        pe.wait_ge(s["y_done"], cc - 1)
                    pe.wait_ge(s["gc_done"], 2 * (pair + 1))
                    for h in range(H):
                        f, p0 = h // 2, HD * (h % 2)
                        m = mm(bank[1][p0:p0 + HD, HD * f:HD * f + HD], state[p0:p0 + HD, cc - 1, f, :],
                               gg[p0:p0 + HD, f, CH * cc:CH * cc + CH])
                    m.then_inc(s["yp_pe"], 1)
                    if cc < NCH - 1:
                        pe.wait_ge(s["q_done"], 2 * (pair + 1))
                        for h in range(H):
                            f, p0 = h // 2, HD * (h % 2)
                            m = mm(bank[0][p0:p0 + HD, HD * f:HD * f + HD], tt[p0:p0 + HD, cc, f, :], state[p0:p0 + HD, cc - 1, f, :])
                        m.then_inc(s["st_pe"], 1)

            pe.wait_ge(s["y_done"], 3)
            yflat = yT.rearrange("p f t -> p (f t)")
            for j in range(2):
                mm(bank[4 + j][:, :], head_mean, yflat[:, 512 * j:512 * j + 512]).then_inc(s["mu_pe"], 1)
            pe.wait_ge(s["ysq_done"], 1)
            for j in range(2):
                mm(bank[6 + j][:, :], head_mean, ysq[:, 512 * j:512 * j + 512]).then_inc(s["var_pe"], 1)
            pe.wait_ge(s["wo_in"], 16)
            pe.wait_ge(s["mix_done"], 1)
            for n in range(4):
                t, half = n // 2, n % 2
                for k in range(KT):
                    m = mm(bank[n][:, :], mixT[:, k, P * t:P * t + P], wo[:, k, 512 * half:512 * half + 512], k == 0, k == KT - 1)
                m.then_inc(s["wo_pe"], 1)

            pe.wait_ge(s["sd_done"], 2)
            model_transposes(xs, s["xs_done"], s["ht_pe"])
            pe.wait_ge(s["ht_done"], 4)
            pe.wait_ge(s["route_in"], 32)
            pe.wait_ge(s["h_done"], 4)
            for t in range(NT):
                for k in range(KT):
                    m = mm(bank[4][:, E * t:E * t + E], hT[:, k, P * t:P * t + P], wrt[:, k, :], k == 0, k == KT - 1)
            m.then_inc(s["lg_pe"], 1)
            for n in range(4):
                m = mm(bank[n][:, :], ident, resid[:, n // 2, 512 * (n % 2):512 * (n % 2) + 512], True, False)
            m.then_inc(s["yinit_pe"], 1)
            pe.wait_ge(s["cb_in"], 32)
            pe.wait_ge(s["pick_done"], 1)
            tri, ones = cb[:, C_TRI:C_TRI + P], cb[:, C_ONE:C_ONE + P]
            mm(bank[5][:, 0:E], tri, picked[:, 0, :])
            mm(bank[5][:, E:2 * E], ones, picked[:, 0, :], True, False)
            mm(bank[5][:, E:2 * E], tri, picked[:, 1, :], False, True)
            mm(bank[5][0:E, 64:65], picked[:, 0, :], ones[:, 0:1], True, False)
            mm(bank[5][0:E, 64:65], picked[:, 1, :], ones[:, 0:1], False, True).then_inc(s["rank_pe"], 1)
            pe.wait_ge(s["extra_done"], 1)
            mm(bank[6][0:E, 0:1], tri[0:E, 0:E], extra[:, 2:3])
            mm(bank[6][0:1, 64:65], extra[:, 2:3], ones[0:E, 0:1]).then_inc(s["start_pe"], 1)
            pe.wait_ge(s["slot_done"], 1)
            for t in range(NT):
                pe.transpose(bank[7][0:E, P * t:P * t + P], slotv[:, t, :], ident)
                m = pe.transpose(bank[7][0:E, SEQ + P * t:SEQ + P * t + P], gates[:, t, :], ident)
            m.then_inc(s["svt_pe"], 1)
            pe.wait_ge(s["oh_done"], 1)
            pe.wait_ge(s["svt_done"], 1)
            for t in range(NT):
                mm(bank[4][:, 64 * t:64 * t + ITEMS], svT[:, 0, P * t:P * t + P], oh, True, False)
                mm(bank[4][:, 64 * t:64 * t + ITEMS], ones[0:E, :], back, False, True)
                mm(bank[4][:, P + 64 * t:P + 64 * t + ITEMS], svT[:, 1, P * t:P * t + P], oh)
            mm(bank[4][0:1, SEQ:SEQ + ITEMS], cb[0:E, C_ECOL:C_ECOL + 1], oh).then_inc(s["col_pe"], 1)

            y = bank[0:4]
            b_g, b_u, b_x, b_d = bank[4], bank[5], bank[6], bank[7]
            xg = m_xg.rearrange("p (k c) -> p k c", k=KT)
            act_v = m_a.rearrange("p (q t) -> p t q", t=4)
            actT = m_at.rearrange("p (t c) -> p t c", t=4)

            def gather():
                for k in range(KT):
                    for n in range(6):
                        t, part = n // 3, n % 3
                        w = xsplit[:, t, part, :].rearrange("p (q k) -> p k q", k=KT)[:, k, :]
                        m = mm(b_x[:, SLOTS * k:SLOTS * k + SLOTS], w, m_p[:, t, :], n == 0, n == 5)
                m.then_inc(s["ga_pe"], 1)

            def scatter(done):
                for half in range(2):
                    r0 = slice(SLOTS * half, SLOTS * half + SLOTS)
                    for t in range(NT):
                        m = mm(y[2 * t + half][:, :], m_gt[r0, P * t:P * t + P], m_os[r0, :], False, False)
                m.then_inc(done, 1)

            pe.wait_ge(s["split_done"], 1)
            pe.wait_ge(s["p_ready"], 1)
            gather()
            pe.wait_ge(s["bsp_done"], 1)
            pe.wait_ge(s["items_done"], 1)
            n_items = pe.value_load(rint[0:1, ITEMS:ITEMS + 1], min_val=E, max_val=ITEMS)
            with pe.Fori(0, n_items) as i:
                pe.wait_ge(s["xg_ready"], i + 1)
                pe.wait_ge(s["gt_done"], i + 1)
                for c in range(4):
                    pe.wait_ge(s_ring[c], 16 * i + 16)
                    for k in range(2):
                        for col, b in ((0, b_g), (FF, b_u)):
                            for half in range(2):
                                c0 = 2 * FF * k + col + 512 * half
                                m = mm(b[SLOTS * half:SLOTS * half + SLOTS, :], xg[:, 2 * c + k, :], ring[:, c, c0:c0 + 512],
                                       c == 0 and k == 0, False)
                    m.then_inc(s_free[c], 1)
                pe.wait_ge(s["sel_ready"], i + 1)
                for col, b in ((0, b_g), (FF, b_u)):
                    for half in range(2):
                        m = mm(b[SLOTS * half:SLOTS * half + SLOTS, :], m_sel[0:3 * E, :],
                               bsp[0:3 * E, col + 512 * half:col + 512 * half + 512], False, True)
                m.then_inc(s["gu_pe"], 1)
                pe.wait_ge(s["os_done"], i + 1)
                scatter(s["sc_pe"])
                pe.wait_ge(s["p_ready"], i + 2)
                gather()
                pe.wait_ge(s["act_done"], i + 1)
                for t in range(4):
                    m = pe.transpose(b_d[:, P * t:P * t + P], act_v[:, t, :], ident)
                m.then_inc(s["tr_pe"], 1)
                pe.wait_ge(s["g2_ready"], i + 1)
                for t in range(NT):
                    m = pe.transpose(b_g[:, P * t:P * t + P], m_g2[:, t, :], ident)
                m.then_inc(s["gtt_pe"], 1)
                pe.wait_ge(s["at_done"], i + 1)
                for h in range(2):
                    pe.wait_ge(s_ring[4 + h], 16 * i + 16)
                    for t in range(4):
                        for half in range(2):
                            m = mm(b_d[SLOTS * half:SLOTS * half + SLOTS, :], actT[:, t, SLOTS * h:SLOTS * h + SLOTS],
                                   ring[:, 4 + h, FF * t + 512 * half:FF * t + 512 * half + 512], h == 0 and t == 0, False)
                    m.then_inc(s_free[4 + h], 1)
                for half in range(2):
                    m = mm(b_d[SLOTS * half:SLOTS * half + SLOTS, :], m_sel[0:3 * E, :],
                           bsp[0:3 * E, 2 * FF + 512 * half:2 * FF + 512 * half + 512], False, True)
                m.then_inc(s["dn_pe"], 1)
            pe.wait_ge(s["os_done"], n_items + 1)
            pe.wait_ge(s["gt_done"], n_items + 1)
            scatter(s["scf_pe"])

        @block.scalar
        def _(act):
            def sqrt_of(o, i, scale, bias, done=None):
                ins = nc.scalar.activation(o, i, ACT.Sqrt, bias=bias, scale=scale)
                if done is not None:
                    ins.then_inc(done, 1)
                return ins

            for t in range(NT):
                act.wait_ge(s["x_in"], 32)
                act.activation(xn[:, t, :], resid[:, t, :], ACT.Square, accum_out=st[:, t:t + 1]).then_inc(s["a_chain"], 1)
            act.wait_ge(s["a_chain"], 2)
            act.wait_ge(s["zpad0"], 1)
            act.activation(st[:, 2:4], st[:, 0:2], ACT.Sqrt, scale=1.0 / D, bias=st[:, 6:7]).then_inc(s["hsq_done"], 1)

            def copy_unit(u):
                act.wait_ge(s["proj_pe"], u + 1)
                if 2 <= u < 7:
                    act.wait_ge(s["zshift"], 2 * (u - 1))
                src = bank[u % 4][:, :].rearrange("p (j t) -> p j t", j=2)
                if u < 7:
                    act.copy(zpad[:, u % 2, :, 1:], src).then_inc(s["zcopy"], 1)
                elif u < 9:
                    act.mul(qA[:, 2 * (u - 7):2 * (u - 7) + 2, :], src, HD ** -0.5).then_inc(s["zcopy"], 1)
                elif u < 11:
                    act.copy(kA[:, 2 * (u - 9):2 * (u - 9) + 2, :], src).then_inc(s["zcopy"], 1)
                else:
                    act.copy(vA[:, u - 11, :], bank[u % 4][:, :]).then_inc(s["zcopy"], 1)

            act.wait_ge(s["zpad0"], 1)
            copy_unit(0)
            copy_unit(1)
            act.wait_ge(s["zshift"], 2)
            act.activation(lora[0:64, 0, :], lora[0:64, 0, :], ACT.Tanh).then_inc(s["tanh_done"], 1)
            act.activation(lora[:, 1, :], lora[:, 1, :], ACT.Sigmoid).then_inc(s["sgd_done"], 1)
            for f in range(FT):
                act.wait_ge(s["dec_pe"], f // 2 + 1)
                act.activation(tiles(sw)[:, f, :], bank[4 + f // 2][:, SEQ * (f % 2):SEQ * (f % 2) + SEQ], ACT.Sigmoid,
                               bias=vec("w0", f)).then_inc(s["sdec_done"], 1)
            for f in range(FT):
                act.wait_ge(s["icl_pe"], f // 2 + 1)
                act.activation(tiles(aT)[:, f, :], bank[6 + f // 2][:, SEQ * (f % 2):SEQ * (f % 2) + SEQ], ACT.Sigmoid,
                               bias=vec("a0", f)).then_inc(s["sicl_done"], 1)
            copy_unit(2)
            copy_unit(3)
            for j in range(2):
                act.wait_ge(s["gat_pe"], j + 1)
                act.copy(gT[:, 512 * j:512 * j + 512], bank[4 + j][:, :]).then_inc(s["gat_done"], 1)
            copy_unit(4)
            copy_unit(5)
            copy_unit(6)
            act.wait_ge(s["exps_done"], 1)
            act.activation(pinv, cum, ACT.Exp, scale=DECAY_C).then_inc(s["a_chain"], 1)
            act.activation(sw, sw, ACT.Exp, scale=-DECAY_C).then_inc(s["a_chain"], 1)
            act.wait_ge(s["a_chain"], 4)
            act.activation(cum, cum, ACT.Exp, scale=-DECAY_C).then_inc(s["a_chain"], 1)
            for j in range(2):
                act.wait_ge(s["ss_pe"], j + 1)
                act.activation(tmp[:, 512 * j:512 * j + 512], bank[6 + j][:, :], ACT.Sqrt).then_inc(s["nrm_done"], 1)
            for u in range(7, 13):
                copy_unit(u)
            for n in range(8):
                arr, t = n // 2, n % 2
                act.wait_ge(s["tok_pe"], n + 1)
                src = bank[n % 4][:, :]
                dst = (vtok[:, t, :], amv[:, t, :, 0, :], btok[:, t, :], ktok[:, t, :])[arr]
                if arr == 1:
                    src = src.rearrange("p (h j) -> p h j", h=H)
                act.copy(dst, src).then_inc(s["tok_done"], 1)

            def exps(h):
                act.wait_ge(s["s_max"], 2 * h + 2)
                if h >= 2:
                    act.wait_ge(s["et_pe"], h - 1)
                for j, (c0, n) in enumerate(((0, P), (P, SEQ))):
                    c = 16 + 2 * h + j
                    act.activation(sc_e[h % 2][:, c0:c0 + n], sc_s[h % 2][:, c0:c0 + n], ACT.Exp,
                                   bias=st[:, c:c + 1], accum_out=st[:, c + 16:c + 17]).then_inc(s["e_done"], 1)

            def et_copy(h):
                act.wait_ge(s["et_pe"], h + 1)
                if h >= 2:
                    act.wait_ge(s["pv_pe"], h - 1)
                act.copy(sc_t[h % 2], bank[6 + h % 2][:, 0:3 * P]).then_inc(s["et_done"], 1)

            exps(0)
            for h in range(H):
                if h + 1 < H:
                    exps(h + 1)
                et_copy(h)
                if h % 2:
                    act.wait_ge(s["pv_pe"], h + 1)
                    act.copy(mixT[:, h // 2, :], bank[h // 2][:, 0:SEQ]).then_inc(s["attn_done"], 1)

            for pair in range(2):
                for g in range(2):
                    act.wait_ge(s["low_pe"], 2 * pair + g + 1)
                    for j in range(2):
                        act.copy(low[g].rearrange("p (f j) s -> p j f s", j=2)[:, j], bank[4 + 2 * g + j][:, 0:2 * P].rearrange(
                            "p (f s) -> p f s", f=2)).then_inc(s["low_done"], 1)
                for lv in range(2, LEVELS + 1):
                    for g in range(2):
                        act.wait_ge(s["t1_pe"], 10 * pair + 2 * (lv - 2) + g + 1)
                        if lv > 2:
                            act.wait_ge(s["d_pe"], 20 * pair + 4 * (lv - 3) + 2 * g + 2)
                        act.copy(t1s[g], bank[2 + g][:, :].rearrange("p (i s) -> p i s", i=4)).then_inc(s["t1_done"], 1)
                for g in range(2):
                    t, q = groups[2 * pair + g]
                    act.wait_ge(s["mv_pe"], 2 * pair + g + 1)
                    act.copy(amv[:, t, 4 * q:4 * q + 4, 1, :],
                             bank[2 + g][:, 0:4 * HD].rearrange("p (i j) -> p i j", i=4)).then_inc(s["mv_done"], 1)
                for g in range(2):
                    act.wait_ge(s["zw_pe"], 2 * pair + g + 1)
                    act.mul(nzw[g], bank[4 + 2 * g][:, :].rearrange("p (i s) -> p i s", i=4), -1.0).then_inc(s["zw_done"], 1)
            act.wait_ge(s["yc_done"], 2)
            act.activation(ysq, yc, ACT.Square).then_inc(s["ysq_done"], 1)
            for j in range(2):
                act.wait_ge(s["var_pe"], j + 1)
                act.activation(yT.rearrange("p f t -> p (f t)")[:, 512 * j:512 * j + 512], bank[6 + j][:, :], ACT.Sqrt,
                               bias=st[:, 7:8]).then_inc(s["sd_done"], 1)
            for t in range(NT):
                act.wait_ge(s["h_done"], 2 * t + 2)
                act.activation(xs[:, t, :], resid[:, t, :], ACT.Square, accum_out=st[:, 8 + t:9 + t]).then_inc(s["a_chain"], 1)
                act.wait_ge(s["a_chain"], 6 + t)
                act.activation(st[:, 10 + t:11 + t], st[:, 8 + t:9 + t], ACT.Sqrt, scale=1.0 / D, bias=st[:, 6:7]).then_inc(s["hsq_done"], 1)
            act.wait_ge(s["lg_done"], 1)
            for t in range(NT):
                act.activation(ex4[:, t, :], mx8[:, t, 0:TOPK], ACT.Exp, bias=st[:, 48 + t:49 + t],
                               accum_out=st[:, 50 + t:51 + t]).then_inc(s["ex_done"], 1)
            act.wait_ge(s["svt_pe"], 1)
            act.copy(svT, bank[7][0:E, :].rearrange("p (w t) -> p w t", w=2)).then_inc(s["svt_done"], 1)

            act.wait_ge(s["items_done"], 1)
            n_items = act.value_load(rint[0:1, ITEMS:ITEMS + 1], min_val=E, max_val=ITEMS)
            with act.Fori(0, n_items) as i:
                act.wait_ge(s["gm_done"], i + 1)
                act.activation(m_s, m_g, ACT.Sigmoid, scale=ALPHA).then_inc(s["sg_done"], 1)
                act.wait_ge(s["tr_pe"], i + 1)
                act.copy(m_at, bank[7][:, :]).then_inc(s["at_done"], 1)
                act.wait_ge(s["gtt_pe"], i + 1)
                act.copy(m_gt, bank[4][:, 0:SEQ]).then_inc(s["gt_done"], 1)
                act.wait_ge(s["dn_pe"], i + 1)
                act.copy(m_os, bank[7][:, :]).then_inc(s["os_done"], 1)
            act.wait_ge(s["scf_pe"], 1)
            for n in range(4):
                act.activation(m_g if n % 2 else m_u, bank[n][:, :], ACT.Square, accum_out=st[:, 52 + n:53 + n]).then_inc(s["fsq_done"], 1)
                if n % 2:
                    act.wait_ge(s["fsq_done"], n + 1)
            act.wait_ge(s["v_fs"], 1)
            act.activation(st[:, 58:60], st[:, 56:58], ACT.Sqrt, scale=1.0 / D, bias=st[:, 6:7]).then_inc(s["fsq_done"], 1)

        @block.gpsimd
        def _(pool):
            for pair in range(2):
                for lv in range(2, LEVELS + 1):
                    for g in range(2):
                        pool.wait_ge(s["low_done"], 4 * pair + 2 * g + 2)
                        if lv == 2 and pair == 0 and g == 0:
                            pool.wait_ge(s["tilde_done"], 4)
                            pool.wait_ge(s["bprod_done"], 1)
                        n = 10 * pair + 2 * (lv - 2) + g
                        if n >= 2:
                            pool.wait_ge(s["t1_pe"], n - 1)
                        pool.tensor_tensor(lml[g], low[g], level_mask(lv), ALU.mult).then_inc(s["lml_done"], 1)
            pool.wait_ge(s["braw_in"], 32)
            raw = braw[0:E, :]
            steps = [0]

            def link(ins):
                ins.then_inc(s["p_chain"], 1)
                steps[0] += 1
                pool.wait_ge(s["p_chain"], steps[0])

            link(pool.tensor_copy(bsp[0:E, :], raw))
            link(pool.tensor_tensor(raw, raw, bsp[0:E, :], ALU.subtract))
            link(pool.tensor_copy(bmid, raw))
            link(pool.tensor_tensor(raw, raw, bmid, ALU.subtract))
            pool.tensor_copy(bsp[E:2 * E, :], bmid)
            pool.tensor_copy(bsp[2 * E:3 * E, :], raw).then_inc(s["bsp_done"], 1)

        @block.vector
        def _(v):
            steps = [0]

            def link(ins):
                ins.then_inc(s["v_chain"], 1)
                steps[0] += 1
                v.wait_ge(s["v_chain"], steps[0])

            def bc(col, n):
                return col.unsqueeze(2).to_broadcast([P, col.shape[1], n])

            def rows(ap):
                return ap.rearrange("p f t -> p (f t)")

            v.memset(st[:, 6:7], RMS_EPS)
            v.memset(st[:, 7:8], GN_EPS)
            v.memset(oh3[:, :], 0.0)
            v.memset(zpad[:, :, :, 0:1], 0.0).then_inc(s["zpad0"], 1)
            v.wait_ge(s["hsq_done"], 1)
            link(v.reciprocal(st[:, 4:6], st[:, 2:4]))
            for t in range(NT):
                v.tensor_scalar(xn[:, t, :], resid[:, t, :], st[:, 4 + t:5 + t], None, ALU.mult).then_inc(s["xn_done"], 1)

            def feature_major(dst, g, ready, done):
                for u in range(4):
                    t, k0 = u // 2, 4 * (u % 2)
                    v.wait_ge(ready, u + 1)
                    v.tensor_tensor(dst[:, k0:k0 + 4, P * t:P * t + P], bank[4 + u][:, :].rearrange("p (k t) -> p k t", k=4),
                                    bc(g[:, k0:k0 + 4], P), ALU.mult).then_inc(done, 1)

            v.wait_ge(s["ca_in"], 32)
            feature_major(xT, gmix, s["xt_pe"], s["xt_done"])
            v.wait_ge(s["vt_pe"], 1)
            v.tensor_copy(vcol[:, :], bank[3][:, 0:NV]).then_inc(s["vt_done"], 1)
            v.wait_ge(s["vt_done"], 1)

            def shift(u):
                v.wait_ge(s["zcopy"], u + 1)
                z = zpad[:, u % 2, :, :]
                if u == 0:
                    dst, m0 = lora[:, :, :], 12
                else:
                    dst = tiles((rT, kT, vT)[(u - 1) // 2])[:, 2 * ((u - 1) % 2):2 * ((u - 1) % 2) + 2, :]
                    m0 = 2 * (u - 1)
                if u == 1:
                    v.wait_ge(s["xt_pe"], 4)
                v.tensor_tensor(dst, z[:, :, 0:SEQ], z[:, :, 1:SEQ + 1], ALU.subtract).then_inc(s["zshift"], 1)
                v.wait_ge(s["zshift"], 2 * u + 1)
                for j in range(2):
                    ins = v.scalar_tensor_tensor(out=dst[:, j, :], in0=dst[:, j, :], scalar=vcol[:, m0 + j:m0 + j + 1],
                                                 in1=z[:, j, 1:SEQ + 1], op0=ALU.mult, op1=ALU.add)
                ins.then_inc(s["zshift"], 1)

            for u in range(3):
                shift(u)
            v.wait_ge(s["sdec_done"], FT)
            for f in range(FT):
                ins = v.tensor_tensor_scan(tiles(cum)[:, f, :], scan_keep, tiles(sw)[:, f, :], 0.0, ALU.mult, ALU.add)
            link(ins)
            v.tensor_tensor(sw, cum, sw, ALU.subtract).then_inc(s["exps_done"], 1)
            shift(3)
            shift(4)
            v.wait_ge(s["zshift"], 10)
            for f in range(FT):
                ins = v.tensor_scalar(tiles(kkT)[:, f, :], tiles(kT)[:, f, :], vec("kk", f), None, ALU.mult)
            link(ins)
            v.tensor_tensor(tmp, kkT, kkT, ALU.mult).then_inc(s["sq_done"], 1)
            shift(5)
            shift(6)
            v.wait_ge(s["nrm_done"], 2)
            link(v.tensor_scalar(tmp, tmp, 1e-12, None, ALU.max))
            link(v.reciprocal(tmp, tmp))
            link(v.tensor_tensor(kkT, kkT, tmp, ALU.mult))
            v.wait_ge(s["sicl_done"], FT)
            for f in range(FT):
                ins = v.tensor_scalar(tiles(tmp)[:, f, :], tiles(aT)[:, f, :], -1.0, vec("ka", f), ALU.add, ALU.mult)
            link(ins)
            link(v.scalar_tensor_tensor(out=kT, in0=tmp, scalar=1.0, in1=kT, op0=ALU.add, op1=ALU.mult))
            v.wait_ge(s["zshift"], 14)
            for f in range(FT):
                ins = v.scalar_tensor_tensor(out=tiles(tmp)[:, f, :], in0=tiles(rT)[:, f, :], scalar=vec("rk", f),
                                             in1=tiles(kT)[:, f, :], op0=ALU.mult, op1=ALU.mult)
            ins.then_inc(s["bprod_done"], 1)
            v.wait_ge(s["a_chain"], 5)
            link(v.tensor_tensor(aT, aT, kkT, ALU.mult))
            v.tensor_tensor(ar[:, :, 0, :], tiles(kkT), tiles(sw), ALU.mult).then_inc(s["tilde_done"], 1)
            v.tensor_tensor(aT, aT, pinv, ALU.mult).then_inc(s["tilde_done"], 1)
            v.wait_ge(s["bprod_done"], 1)
            v.tensor_tensor(kT, kT, pinv, ALU.mult).then_inc(s["tilde_done"], 1)
            v.tensor_tensor(ar[:, :, 1, :], tiles(rT), tiles(cum), ALU.mult).then_inc(s["tilde_done"], 1)
            v.wait_ge(s["bsum_pe"], 2)
            v.wait_ge(s["tilde_done"], 4)
            for j in range(2):
                ins = v.tensor_tensor(kkT[:, 512 * j:512 * j + 512], bank[4 + j][:, :], vT[:, 512 * j:512 * j + 512], ALU.mult)
            ins.then_inc(s["bonus_done"], 1)

            v.wait_ge(s["bias_in"], 16)

            def biased(h):
                v.wait_ge(s["s_pe"], h + 1)
                if h >= 2:
                    v.wait_ge(s["e_done"], 2 * (h - 1))
                b = bank[4 + h % 2]
                c = 16 + 2 * h
                v.tensor_tensor_reduce(sc_s[h % 2][:, 0:P], b[:, 0:P], abias[:, h, P:SEQ], 1.0, -3e38,
                                       ALU.add, ALU.max, st[:, 60:61])
                link(v.tensor_tensor_reduce(sc_s[h % 2][:, P:3 * P], b[:, P:3 * P], abias[:, h, :], 1.0, -3e38,
                                            ALU.add, ALU.max, st[:, 61:62]))
                v.tensor_scalar(st[:, c:c + 2], st[:, 60:62], -1.0, None, ALU.mult).then_inc(s["s_max"], 2)
                v.wait_ge(s["s_max"], 2 * h + 2)

            def normalise(h):
                v.wait_ge(s["e_done"], 2 * h + 2)
                c = 32 + 2 * h
                link(v.reciprocal(st[:, 62:64], st[:, c:c + 2]))
                v.tensor_scalar(sc_e[h % 2][:, 0:P], sc_e[h % 2][:, 0:P], st[:, 62:63], None, ALU.mult)
                v.tensor_scalar(sc_e[h % 2][:, P:3 * P], sc_e[h % 2][:, P:3 * P], st[:, 63:64], None,
                                ALU.mult).then_inc(s["en_done"], 1)
                v.wait_ge(s["en_done"], h + 1)

            biased(0)
            for h in range(H):
                if h + 1 < H:
                    biased(h + 1)
                normalise(h)

            v.wait_ge(s["attn_done"], FT)
            v.wait_ge(s["pv_pe"], H)
            for pair in range(2):
                for g in range(2):
                    n, (t, q) = 2 * pair + g, groups[2 * pair + g]
                    if pair == 1:
                        v.wait_ge(s["gc_pe"], g + 1)
                    for i in range(4):
                        v.wait_ge(s["gram_pe"], 4 * n + i + 1)
                        v.tensor_tensor(nm[g][:, i, :, :].rearrange("p w s -> p (w s)"), bank[(4 * n + i) % 2][:, :], mask4,
                                        ALU.mult).then_inc(s["nm_done"], 1)
                    v.wait_ge(s["nm_done"], 4 * n + 4)
                    v.wait_ge(s["low_done"], 2 * n + 2)
                    if pair == 1:
                        v.wait_ge(s["zw_pe"], g + 1)
                    link(v.tensor_tensor(ux[g][:, :, 1, :], low[g], level_mask(1), ALU.mult))
                    eye = ident.unsqueeze(1).to_broadcast([P, 4, P])
                    v.tensor_tensor(ux[g][:, :, 1, :], eye, ux[g][:, :, 1, :], ALU.subtract).then_inc(s["ux_done"], 1)
                    v.tensor_tensor(ux[g][:, :, 0, :], eye, nm[g][:, :, 0, :], ALU.subtract).then_inc(s["ux_done"], 1)
                for lv in range(2, LEVELS + 1):
                    for g in range(2):
                        for j in range(2):
                            v.wait_ge(s["d_pe"], 20 * pair + 4 * (lv - 2) + 2 * g + 2)
                            u2 = ux[g][:, 2 * j:2 * j + 2, :, :]
                            d2 = bank[4 + 2 * g + j][:, :].rearrange("p (i w s) -> p i w s", i=2, w=2)
                            if lv == LEVELS:
                                u2, d2 = u2[:, :, 0, :], d2[:, :, 0, :]
                            else:
                                u2, d2 = u2.rearrange("p i w s -> p (i w s)"), d2.rearrange("p i w s -> p (i w s)")
                            if lv == 2 and j == 0:
                                v.wait_ge(s["ux_done"], 24 * pair + 4)
                            elif j == 0:
                                v.wait_ge(s["ux_done"], 24 * pair + 4 * (lv - 2) + 2 * g + 2)
                            v.tensor_tensor(u2, u2, d2, ALU.subtract).then_inc(s["ux_done"], 1)
                for g in range(2):
                    n, (t, q) = 2 * pair + g, groups[2 * pair + g]
                    ts = slice(P * t, P * t + P)
                    v.wait_ge(s["gc_pe"], n + 1)
                    b = bank[5 + 2 * g]
                    v.tensor_tensor(gg[:, 2 * q:2 * q + 2, ts], b[:, 0:SEQ].rearrange("p (f t) -> p f t", f=2),
                                    ar[:, 2 * q:2 * q + 2, 1, ts], ALU.add)
                    v.tensor_copy(yT[:, 2 * q:2 * q + 2, ts], b[:, SEQ:512].rearrange("p (f t) -> p f t", f=2)).then_inc(s["gc_done"], 1)
                v.wait_ge(s["q_pe"], pair + 1)
                for c in range(2):
                    v.tensor_tensor(tt[:, 2 * pair + c, :, :], bank[2 + c][:, 0:SEQ].rearrange("p (f j) -> p f j", f=FT),
                                    eye2.unsqueeze(1).to_broadcast([P, FT, HD]), ALU.add).then_inc(s["q_done"], 1)
                for c in range(2 - pair):
                    cc = 2 * pair + c
                    v.wait_ge(s["u_pe"], cc + 1)
                    v.tensor_tensor(state[:, cc, :, :], bank[c][:, 0:FT * HD].rearrange("p (f i) -> p f i", f=FT),
                                    bc(tiles(cum)[:, :, CH * cc + CH - 1], HD), ALU.mult).then_inc(s["u_done"], 1)
                for cc in range(max(1, 2 * pair), 2 * pair + 2):
                    if cc < NCH - 1:
                        v.wait_ge(s["st_pe"], cc)
                        link(v.tensor_tensor(stmp, bank[0][:, 0:FT * HD].rearrange("p (f i) -> p f i", f=FT),
                                             bc(tiles(cum)[:, :, CH * cc + CH - 1], HD), ALU.mult))
                        v.wait_ge(s["u_done"], 2 + pair)
                        v.tensor_tensor(state[:, cc, :, :], state[:, cc, :, :], stmp, ALU.add).then_inc(s["st_done"], 1)
                    v.wait_ge(s["yp_pe"], cc)
                    v.wait_ge(s["gc_done"], 2 * pair + 2)
                    o = yT[:, :, CH * cc:CH * cc + CH]
                    v.tensor_tensor(o, bank[1][:, 0:FT * HD].rearrange("p (f t) -> p f t", f=FT), o, ALU.add).then_inc(s["y_done"], 1)

            v.wait_ge(s["y_done"], 3)
            for j in range(2):
                v.wait_ge(s["mu_pe"], j + 1)
                v.tensor_tensor(yc[:, 512 * j:512 * j + 512], rows(yT)[:, 512 * j:512 * j + 512], bank[4 + j][:, :],
                                ALU.subtract).then_inc(s["yc_done"], 1)
            v.wait_ge(s["sd_done"], 2)
            link(v.reciprocal(rows(yT), rows(yT)))
            link(v.tensor_tensor(yc, yc, rows(yT), ALU.mult))
            for f in range(FT):
                ins = v.tensor_scalar(tiles(yc)[:, f, :], tiles(yc)[:, f, :], vec("gw", f), vec("gb", f), ALU.mult, ALU.add)
            link(ins)
            link(v.tensor_tensor(yc, yc, kkT, ALU.add))
            v.tensor_tensor(rows(mixT[:, FT:KT, :]), yc, gT, ALU.mult).then_inc(s["mix_done"], 1)
            for n in range(4):
                o = resid[:, n // 2, 512 * (n % 2):512 * (n % 2) + 512]
                v.wait_ge(s["wo_pe"], n + 1)
                v.tensor_tensor(o, bank[n][:, :], o, ALU.add).then_inc(s["h_done"], 1)
            for t in range(NT):
                v.wait_ge(s["hsq_done"], 2 + t)
                link(v.reciprocal(st[:, 12 + t:13 + t], st[:, 10 + t:11 + t]))
                v.tensor_scalar(xs[:, t, :], resid[:, t, :], st[:, 12 + t:13 + t], None, ALU.mult).then_inc(s["xs_done"], 1)
            v.wait_ge(s["cb_in"], 32)
            v.wait_ge(s["bsp_done"], 1)
            feature_major(hT, gffn, s["ht_pe"], s["ht_done"])
            v.wait_ge(s["lg_pe"], 1)
            v.wait_ge(s["route_in"], 32)
            link(v.tensor_tensor(lg, bank[4][:, 0:2 * E].rearrange("p (t e) -> p t e", t=NT),
                                 brt[:, :].unsqueeze(1).to_broadcast([P, NT, E]), ALU.add))
            for t in range(NT):
                link(v.max(mx8[:, t, :], lg[:, t, :]))
            v.tensor_scalar(st[:, 48:50], mx8[:, :, 0], -1.0, None, ALU.mult).then_inc(s["lg_done"], 1)
            for t in range(NT):
                link(v.max_index(idx8[:, t, :], mx8[:, t, :], lg[:, t, :]))
            link(v.tensor_copy(idxf, idx8[:, :, :]))
            iota = cb[:, C_IOTA32:C_IOTA32 + E]
            for t in range(NT):
                ins = v.tensor_tensor(onehot[:, t, :, :], iota.unsqueeze(1).to_broadcast([P, TOPK, E]),
                                      bc(idxf[:, t, 0:TOPK], E), ALU.is_equal)
            link(ins)
            for t in range(NT):
                ins = v.tensor_reduce(picked[:, t, :], onehot[:, t, :, :].rearrange("p j e -> p e j"), AX.X, ALU.add)
            ins.then_inc(s["pick_done"], 1)
            v.wait_ge(s["ex_done"], 2)
            link(v.reciprocal(st[:, 54:56], st[:, 50:52]))
            link(v.tensor_tensor(gt4, ex4, bc(st[:, 54:56], TOPK), ALU.mult))
            for t in range(NT):
                ins = v.tensor_tensor(onehot[:, t, :, :], onehot[:, t, :, :], bc(gt4[:, t, :], E), ALU.mult)
            link(ins)
            for t in range(NT):
                ins = v.tensor_reduce(gates[:, t, :], onehot[:, t, :, :].rearrange("p j e -> p e j"), AX.X, ALU.add)
            link(ins)
            v.wait_ge(s["rank_pe"], 1)
            v.wait_ge(s["pick_done"], 1)
            link(v.tensor_copy(cnt, bank[5][0:E, 64:65]))
            link(v.tensor_scalar(extra[:, 0:1], cnt, 1.0 * SLOTS, None, ALU.is_gt))
            link(v.scalar_tensor_tensor(out=extra[:, 1:2], in0=cnt, scalar=2.0 * SLOTS, in1=extra[:, 0:1], op0=ALU.is_gt, op1=ALU.add))
            v.scalar_tensor_tensor(out=extra[:, 2:3], in0=cnt, scalar=3.0 * SLOTS, in1=extra[:, 1:2], op0=ALU.is_gt,
                                   op1=ALU.add).then_inc(s["extra_done"], 1)
            link(v.scalar_tensor_tensor(out=slotv, in0=bank[5][:, 0:2 * E].rearrange("p (t e) -> p t e", t=NT), scalar=1.0,
                                        in1=picked, op0=ALU.add, op1=ALU.mult))
            v.tensor_scalar(slotv, slotv, -1.0, None, ALU.add).then_inc(s["slot_done"], 1)
            v.memset(back, 0.0)
            v.memset(colv, 0.0)
            v.memset(gcol, 0.0)
            v.tensor_copy(oh[:, 0:E], ident[0:E, 0:E])
            v.wait_ge(s["extra_done"], 1)
            v.wait_ge(s["start_pe"], 1)
            link(v.tensor_copy(startc, bank[6][0:E, 0:1]))
            link(v.tensor_scalar(dj, cb[0:E, C_J:C_J + EXTRA], startc, None, ALU.subtract))
            link(v.tensor_scalar(oh[:, E:ITEMS], dj, 0.0, None, ALU.is_ge))
            link(v.scalar_tensor_tensor(out=oh[:, E:ITEMS], in0=dj, scalar=extra[:, 2:3], in1=oh[:, E:ITEMS],
                                        op0=ALU.is_lt, op1=ALU.mult))
            link(v.tensor_scalar(dj, dj, 1.0, -1.0 * SLOTS, ALU.add, ALU.mult))
            link(v.tensor_tensor(back[:, E:ITEMS], dj, oh[:, E:ITEMS], ALU.mult))
            for part in range(3):
                ins = v.tensor_copy(oh3[E * part:E * part + E, 0:ITEMS], oh)
            ins.then_inc(s["oh_done"], 1)
            v.wait_ge(s["col_pe"], 1)
            v.tensor_copy(colv[:, :, 0:ITEMS], bank[4][:, 0:P].rearrange("p (t i) -> p t i", t=NT)[:, :, 0:ITEMS])
            v.tensor_copy(gcol[:, :, 0:ITEMS], bank[4][:, P:2 * P].rearrange("p (t i) -> p t i", t=NT)[:, :, 0:ITEMS])
            v.tensor_copy(rint[0:1, 0:ITEMS], bank[4][0:1, SEQ:SEQ + ITEMS])
            v.tensor_scalar(rint[0:1, ITEMS:ITEMS + 1], bank[6][0:1, 64:65], float(E), None, ALU.add).then_inc(s["items_done"], 1)
            v.wait_ge(s["items_done"], 1)
            n_items = v.value_load(rint[0:1, ITEMS:ITEMS + 1], min_val=E, max_val=ITEMS)

            v.wait_ge(s["ht_pe"], 4)
            for t in range(NT):
                for part in range(3):
                    link(v.tensor_copy(xsplit[:, t, part, :], xs[:, t, :]))
                    if part < 2:
                        link(v.tensor_tensor(xs[:, t, :], xs[:, t, :], xsplit[:, t, part, :], ALU.subtract))
            v.memset(m_os, 0.0).then_inc(s["os_done"], 1)
            v.memset(m_gt, 0.0).then_inc(s["gt_done"], 1)
            v.memset(m_sel, 0.0).then_inc(s["split_done"], 1)
            v.wait_ge(s["split_done"], 1)

            iota2 = cb[:, C_IOTA2:C_IOTA2 + P]

            def one_hot(i):
                for t in range(NT):
                    ins = v.tensor_scalar(m_p[:, t, :], iota2[:, 0:SLOTS], colv[:, t, bass.ds(i, 1)], None, ALU.is_equal)
                ins.then_inc(s["p_ready"], 1)

            def gate_matrix(i):
                for t in range(NT):
                    ins = v.tensor_scalar(m_g2[:, t, :], iota2, colv[:, t, bass.ds(i, 1)], gcol[:, t, bass.ds(i, 1)],
                                          ALU.is_equal, ALU.mult)
                ins.then_inc(s["g2_ready"], 1)

            def select(i):
                v.tensor_copy(m_sel[0:3 * E, :], oh3[0:3 * E, bass.ds(i, 1)].to_broadcast([3 * E, SLOTS])).then_inc(s["sel_ready"], 1)

            def gathered():
                v.tensor_tensor(m_xg.rearrange("p (k c) -> p k c", k=KT), bank[6][:, :].rearrange("p (k c) -> p k c", k=KT),
                                bc(gffn[:, :], SLOTS), ALU.mult).then_inc(s["xg_ready"], 1)

            one_hot(0)
            gate_matrix(0)
            select(0)
            v.wait_ge(s["ga_pe"], 1)
            gathered()
            one_hot(1)
            with v.Fori(0, n_items) as i:
                v.wait_ge(s["gu_pe"], i + 1)
                v.tensor_scalar(m_g, bank[4][:, :], LIMIT, None, ALU.min).then_inc(s["gm_done"], 1)
                v.tensor_scalar(m_u, bank[5][:, :], LIMIT, -LIMIT, ALU.min, ALU.max).then_inc(s["um_done"], 1)
                v.wait_ge(s["gm_done"], i + 1)
                v.wait_ge(s["um_done"], i + 1)
                v.scalar_tensor_tensor(out=m_t, in0=m_u, scalar=1.0, in1=m_g, op0=ALU.add, op1=ALU.mult).then_inc(s["t_done"], 1)
                v.wait_ge(s["t_done"], i + 1)
                v.wait_ge(s["sg_done"], i + 1)
                v.tensor_tensor(m_a, m_t, m_s, ALU.mult).then_inc(s["act_done"], 1)
                v.wait_ge(s["ga_pe"], i + 2)
                gathered()
                one_hot(i + 2)
                v.wait_ge(s["gtt_pe"], i + 1)
                gate_matrix(i + 1)
                v.wait_ge(s["dn_pe"], i + 1)
                select(i + 1)
            v.wait_ge(s["fsq_done"], 4)
            v.tensor_tensor(st[:, 56:58], st[:, 52:56:2], st[:, 53:56:2], ALU.add).then_inc(s["v_fs"], 1)
            v.wait_ge(s["fsq_done"], 5)
            link(v.reciprocal(st[:, 64:66], st[:, 58:60]))
            v.wait_ge(s["gfin_in"], 16)
            for n in range(4):
                t, half = n // 2, 512 * (n % 2)
                ins = v.scalar_tensor_tensor(out=yout[:, t, half:half + 512], in0=bank[n][:, :], scalar=st[:, 64 + t:65 + t],
                                             in1=gfin[:, half:half + 512], op0=ALU.mult, op1=ALU.mult)
                if n % 2:
                    ins.then_inc(s["fin_done"], 1)


_INS = ["x", "norm_mix_g", "w_in", "shift_mu", "decay_w0", "w_decay_up", "iclr_a0", "w_iclr_up", "w_gate_lr_up", "k_k", "k_a",
        "r_k", "gn_w", "gn_b", "w_out", "norm_ffn_g", "w_router", "b_router", "w_gate_up", "b_gate_up", "w_down", "b_down",
        "norm_final_g"]


def kernel(**inputs):
    import concourse.bacc as _bacc
    from concourse.bass_utils import run_bass_kernel_spmd as _run

    nc = _bacc.Bacc("TRN2", target_bir_lowering=False, num_devices=1)
    arrays, args = {}, []
    named = [(n, np.ascontiguousarray(inputs[n])) for n in _INS]
    named += list(zip(("const_a", "const_bias", "const_b"), shape_constants()))
    for name, a in named:
        arrays[f"in_{name}"] = a
        args.append(nc.dram_tensor(f"in_{name}", a.shape, mybir.dt.from_np(a.dtype), kind="ExternalInput").ap())
    args.append(nc.dram_tensor("out_0", (1, SEQ, D), F32, kind="ExternalOutput").ap())
    program(nc, *args)
    r = _run(nc, [arrays], core_ids=[0])
    return r.results[0]["out_0"]
```

```python
from contextlib import ExitStack

import numpy as np
import concourse.bass as bass
from concourse import mybir

F32 = mybir.dt.float32
BF16 = mybir.dt.bfloat16
I32 = mybir.dt.int32
U32 = mybir.dt.uint32
ALU = mybir.AluOpType
ACT = mybir.ActivationFunctionType
AX = mybir.AxisListType

P = 128
D = 1024
SEQ = 256
NT = SEQ // P
KT = D // P
AW = 512
RW = 512
HD = 64
H = 8
FT = RW // P
LORA = 256
IN_W = 3 * AW + 3 * RW + LORA
CH = 64
NCH = SEQ // CH
LEVELS = 6
E = 32
TOPK = 4
FF = 1024
SLOTS = 64
EXTRA = 16
ITEMS = E + EXTRA
CHUNK = 4096
RING = 6
LIMIT = 7.0
ALPHA = 1.702
RMS_EPS = 1e-5
GN_EPS = 64e-5
DECAY_C = float(np.exp(-0.5))
NV = 14 + 7 * FT
PATTERNS = ((128, 1), (512, 4), (2048, 16))

C_IDENT, C_ONES, C_MEAN, C_SCAN = 0, 128, 256, 384
C_EYE2 = 640
C_MASK4 = 704
C_LEVEL = C_MASK4 + 4 * CH
C_A = C_LEVEL + LEVELS * CH
C_IOTA2, C_TRI, C_ONE, C_IOTA32, C_ECOL, C_J = 0, 128, 256, 384, 416, 417
C_B = 440


def shape_constants():
    a = np.zeros((P, C_A), np.float32)
    t = np.arange(P)
    a[:, C_IDENT:C_IDENT + P] = np.eye(P)
    a[:, C_ONES:C_ONES + P] = (t[:, None] // HD) == (t[None, :] // HD)
    a[:, C_MEAN:C_MEAN + P] = a[:, C_ONES:C_ONES + P] / HD
    a[:, C_SCAN:C_SCAN + SEQ] = (np.arange(SEQ) % CH) != 0
    a[:, C_EYE2:C_EYE2 + HD] = np.tile(np.eye(HD), (2, 1))

    c = np.arange(CH)

    def level(n):
        return ((c[:, None] >> n) == (c[None, :] >> n)) & (((c[:, None] >> (n - 1)) & 1) == 1) & (((c[None, :] >> (n - 1)) & 1) == 0)

    masks = [level(1).T, c[:, None] <= c[None, :], c[:, None] < c[None, :], c[:, None] <= c[None, :]]
    masks += [level(n + 1) for n in range(LEVELS)]
    for n, m in enumerate(masks):
        a[:, C_MASK4 + n * CH:C_MASK4 + (n + 1) * CH] = np.tile(m, (2, 1))

    dist = P + t[:, None] - np.arange(SEQ)[None, :]
    times = np.zeros(dist.shape, np.float64)
    for window, dil in PATTERNS:
        times += (dist >= 0) & (dist <= window) & (dist % dil == 0)
    bias = np.empty((P, H, SEQ), np.float32)
    for h in range(H):
        slope = 2.0 ** (-8.0 / H * (h + 1))
        bias[:, h] = np.where(times > 0, -slope * dist + np.log(np.maximum(times, 1)), -1e30)

    b = np.zeros((P, C_B), np.float32)
    b[:, C_IOTA2:C_IOTA2 + P] = np.tile(np.arange(SLOTS), 2)
    b[:, C_TRI:C_TRI + P] = t[:, None] < t[None, :]
    b[:, C_ONE:C_ONE + P] = 1.0
    b[:, C_IOTA32:C_IOTA32 + E] = np.arange(E)
    b[:, C_ECOL] = t
    b[:, C_J:C_J + EXTRA] = np.arange(EXTRA)
    return a, bias.reshape(P, H * SEQ), b


def program(nc, x, g_mix, w_in, mu, w0, w_dec, a0, w_icl, w_gat, k_k, k_a, r_k, gn_w, gn_b, w_out, g_ffn, w_router,
            b_router, w_gu, b_gu, w_dn, b_dn, g_fin, const_a, const_bias, const_b, out):
    with ExitStack() as ctx:
        def sb(name, shape, dt=F32):
            return ctx.enter_context(nc.sbuf_tensor(name, shape, dt))

        def sem(name):
            return ctx.enter_context(nc.semaphore(name))

        ring = sb("ring", [P, RING, CHUNK])
        resid = sb("resid", [P, NT, D])
        arena = sb("arena", [P, 12, 1024])
        attn = sb("attn", [P, 3, 1024])
        stage = sb("stage", [P, 4, 1024])
        zpad = sb("zpad", [P, 2, 2, SEQ + 1])
        lora = sb("lora", [P, 2, SEQ])
        mixT = sb("mixT", [P, KT, SEQ])
        ca = sb("ca", [P, C_A])
        cb = sb("cb", [P, C_B])
        vrow = sb("vrow", [NV, P])
        vcol = sb("vcol", [P, NV])
        gmix = sb("gmix", [P, KT])
        gffn = sb("gffn", [P, KT])
        st = sb("st", [P, 96])
        wrt = sb("wrt", [P, KT, E])
        brt = sb("brt", [P, E])

        bank = [ctx.enter_context(nc.psum_tensor(f"bank{i}", [P, 512], F32)) for i in range(8)]

        y_bank = [bank[i] for i in (6, 7, 0, 1)]
        b_g, b_u, b_x, b_d = bank[2:6]
        level_bank = [[bank[i] for i in b] for b in ((0, 1), (4, 5))]

        ident = ca[:, C_IDENT:C_IDENT + P]
        head_ones = ca[:, C_ONES:C_ONES + P]
        head_mean = ca[:, C_MEAN:C_MEAN + P]
        scan_keep = ca[:, C_SCAN:C_SCAN + SEQ]
        eye2 = ca[:, C_EYE2:C_EYE2 + HD]
        mask4 = ca[:, C_MASK4:C_MASK4 + 4 * CH]

        def level_mask(n):
            return ca[:, C_LEVEL + (n - 1) * CH:C_LEVEL + n * CH].unsqueeze(1).to_broadcast([P, H, CH])

        def blk(i, n=1):
            return arena[:, i:i + n, :].rearrange("p b c -> p (b c)")

        def tiles(ap):
            return ap.rearrange("p (f t) -> p f t", t=SEQ)

        B_R, B_S, B_I, B_X, B_KK, B_G, B_C, B_AR, B_A, B_K, B_V = 0, 1, 2, 3, 4, 5, 6, 7, 9, 10, 11
        rT, kT, vT = blk(B_R), blk(B_K), blk(B_V)
        sw = blk(B_S)
        cum = blk(B_C)
        pinv = blk(B_I)
        tmp = blk(B_X)
        kkT = blk(B_KK)
        gT = blk(B_G)
        aT = blk(B_A)
        ar = blk(B_AR, 2).rearrange("p (f w t) -> p f w t", w=2, t=SEQ)
        xn = arena[:, B_R:B_R + 2, :]
        xT = stage[:, 0:2, :].rearrange("p b c -> p (b c)").rearrange("p (k t) -> p k t", t=SEQ)
        wlo = stage[:, 2:4, :].rearrange("p b c -> p (b c)").rearrange("p (k n) -> p k n", n=LORA)
        qA, kA = tiles(attn[:, 0, :]), tiles(attn[:, 1, :])
        vA = attn[:, 2, :].rearrange("p (t n) -> p t n", n=AW)

        slot = [ring[:, i, :].rearrange("p (k n) -> p k n", k=KT) for i in range(RING)]
        work = ring[:, 2:4, :].rearrange("p b c -> p (b c)")
        amv = work[:, 0:2048].rearrange("p (t h w j) -> p t h w j", t=NT, h=H, w=2)
        btok = work[:, 2048:3072].rearrange("p (t n) -> p t n", t=NT)
        ktok = work[:, 3072:4096].rearrange("p (t n) -> p t n", t=NT)
        vtok = work[:, 4096:6144].rearrange("p (t c n) -> p t c n", t=NT, c=2)
        uu = [work[:, 6144 + 512 * g:6656 + 512 * g].rearrange("p (h s) -> p h s", h=H) for g in range(NT)]
        low = [work[:, 7168 + 512 * g:7680 + 512 * g].rearrange("p (h s) -> p h s", h=H) for g in range(NT)]
        apart = ring[:, 0:2, :].rearrange("p b c -> p (b c)")
        heads_apart = apart[:, 0:4096].rearrange("p (j a f t) -> p j a f t", j=2, a=2, f=FT)
        nzw = [apart[:, 0:4096].rearrange("p (c t h s) -> p t c h s", c=2, t=NT, h=H)[:, g] for g in range(NT)]
        lml = [apart[:, 4096 + 1024 * g:5120 + 1024 * g].rearrange("p (h c s) -> p h c s", h=H, c=2) for g in range(NT)]
        xx = [apart[:, 6144 + 1024 * g:7168 + 1024 * g].rearrange("p (h c s) -> p h c s", h=H, c=2) for g in range(NT)]
        abias = blk(B_R, 2).rearrange("p (h s) -> p h s", h=H)
        mflat = mixT[:, :, :].rearrange("p k t -> p (k t)")
        wlor_d = mflat[:, 0:RW]
        wgt = mflat[:, RW:2 * RW]
        wo = ring[:, 4:6, :].rearrange("p b c -> p (b c)").rearrange("p (m n) -> p m n", m=KT)

        sflat = stage[:, :, :].rearrange("p b c -> p (b c)")
        sc_s = [sflat[:, 384 * i:384 * i + 384] for i in range(2)]
        sc_e = [sflat[:, 768 + 384 * i:1152 + 384 * i] for i in range(2)]
        sc_t = [sflat[:, 1536 + 384 * i:1920 + 384 * i] for i in range(2)]
        nm = [sflat[:, 2048 * g:2048 * g + 2048].rearrange("p (h w s) -> p h w s", h=H, w=4) for g in range(NT)]
        t1s = [attn[:, 0, 512 * g:512 * g + 512].rearrange("p (h s) -> p h s", h=H) for g in range(NT)]
        gg = tiles(blk(B_X))
        yT = tiles(zpad[:, :, :, :].rearrange("p a b c -> p (a b c)")[:, 0:1024])
        tt = attn[:, 1, :].rearrange("p (c f j) -> p c f j", c=NCH, f=FT)
        state = attn[:, 2, :].rearrange("p (c f i) -> p c f i", c=NCH, f=FT)
        stmp = blk(B_R)[:, 0:FT * HD].rearrange("p (f i) -> p f i", f=FT)
        yc = blk(B_S)
        ysq = blk(B_R)

        xs = arena[:, B_R:B_R + 2, :]
        xsplit = attn[:, :, :].rearrange("p b c -> p (b c)").bitcast(BF16).rearrange("p (t s n) -> p t s n", t=NT, s=3)
        hT = stage[:, 0:2, :].rearrange("p b c -> p (b c)").rearrange("p (k t) -> p k t", t=SEQ)
        gfin = stage[:, 2, :]
        xrem = arena[:, B_X:B_X + 2, :]
        yout = arena[:, B_R:B_R + 2, :]
        QB = 3 * D // 4
        braw = mflat[:, 2 * RW:2 * RW + QB]
        bpart = [sflat[:, o:o + QB // 2].bitcast(BF16) for o in (3072, 3072 + QB // 2, 2304)]
        bsp = blk(B_K, 2).bitcast(BF16)[:, 0:4 * QB].rearrange("p (q n) -> p q n", q=4)
        mz = blk(B_I, 5)
        m_g, m_u, m_t, m_s, m_a, m_at, m_os, m_xg = (mz[:, 512 * i:512 * i + 512] for i in range(8))
        m_gt, m_g2 = mz[:, 4096:4352], mz[:, 4352:4608].rearrange("p (t c) -> p t c", t=NT)
        m_p = mz[:, 4608:4672].bitcast(BF16).rearrange("p (t c) -> p t c", t=NT)
        m_sel = mz[:, 4672:4704].bitcast(BF16)
        rs = stage[:, 3, :]
        rint = sb("rint", [P, 80], I32)
        idx8 = sb("idx8", [P, NT, 8], U32)
        lg = rs[:, 0:64].rearrange("p (t e) -> p t e", t=NT)
        mx8 = rs[:, 64:80].rearrange("p (t e) -> p t e", t=NT)
        idxf = rs[:, 80:96].rearrange("p (t e) -> p t e", t=NT)
        ex4 = rs[:, 96:104].rearrange("p (t e) -> p t e", t=NT)
        gt4 = rs[:, 104:112].rearrange("p (t e) -> p t e", t=NT)
        onehot = rs[:, 112:368].rearrange("p (t j e) -> p t j e", t=NT, j=TOPK)
        picked = rs[:, 368:432].rearrange("p (t e) -> p t e", t=NT)
        gates = rs[:, 432:496].rearrange("p (t e) -> p t e", t=NT)
        slotv = rs[:, 496:560].rearrange("p (t e) -> p t e", t=NT)
        extra = rs[0:E, 560:563]
        cnt = rs[0:E, 563:564]
        startc = rs[0:E, 564:565]
        dj = rs[0:E, 566:566 + EXTRA]
        oh = rs[0:E, 584:584 + ITEMS]
        back = rs[0:E, 632:632 + ITEMS]
        colv = rs[:, 680:680 + 2 * (ITEMS + 2)].rearrange("p (t i) -> p t i", t=NT)
        gcol = rs[:, 780:780 + 2 * (ITEMS + 2)].rearrange("p (t i) -> p t i", t=NT)
        oh3 = sb("oh3", [P, ITEMS + 2], BF16)
        svT = mz[0:E, 512:1024].rearrange("p (w t) -> p w t", w=2)

        names = ("id_in gm_in ca_in vec_in wlo_in up_in bias_in cb_in wo_in braw_in route_in gfin_in out_done "
                 "v_chain a_chain p_chain xn_done xt_pe xt_done vt_pe vt_done proj_pe zcopy zshift zpad0 tanh_done sgd_done "
                 "dec_pe icl_pe gat_pe sdec_done sicl_done gat_done exps_done sq_done ss_pe nrm_done bprod_done bsum_pe "
                 "bonus_done tilde_done tok_pe tok_done s_pe s_max e_done en_done et_pe et_done pv_pe attn_done "
                 "gram_pe nm_done low_done ux_done lml_done t1_pe t1_done d_pe mv_pe mv_done zw_pe zw_done gc_pe gc_done qu_pe qu_done "
                 "st_pe st_done yp_pe y_done mu_pe yc_done ysq_done var_pe sd_done mix_done wo_pe h_done "
                 "xs_done ht_pe ht_done lg_pe lg_done ex_done pick_done rank_pe slot_done extra_done start_pe oh_done svt_pe "
                 "svt_done col_pe col_done items_done split_done bsplit_done bsp_in zero_done apart_done rem_done hsq_done "
                 "p_ready ga_pe xg_ready sel_ready gu_pe gm_done sg_done act_done tr_pe at_done g2_ready gtt_pe gt_done dn_pe os_done "
                 "sc_pe scf_pe fsq_done fin_done yfin_done um_done t_done").split()
        s = {n: sem(n) for n in names}
        s_x = [sem(f"x_in{t}") for t in range(NT)]
        s_win = [sem(f"win_in{i}") for i in range(RING)]
        s_ring = [sem(f"ring_in{i}") for i in range(RING)]
        s_free = [sem(f"ring_free{i}") for i in range(RING)]

        block = ctx.enter_context(nc.Block())

        groups = [(t, q) for t in range(NT) for q in range(2)]
        VL = dict(mu=0, w0=14, a0=18, kk=22, ka=26, rk=30, gw=34, gb=38)

        def vec(name, f):
            c = VL[name] + f
            return vcol[:, c:c + 1]

        def expert_chunk(e, c):
            if c < 4:
                return w_gu[0, e].rearrange("(p c t) n -> c p (t n)", c=4, t=2)[c]
            return w_dn[0, e].rearrange("(h p t) n -> h p (t n)", h=2, t=4)[c - 4]

        @block.sync
        def _(sp):
            for t in range(NT):
                sp.dma_start(resid[:, t, :], x[0, P * t:P * t + P, :]).then_inc(s_x[t], 16)
            sp.dma_start(ca[:, 0:P], const_a[:, 0:P]).then_inc(s["id_in"], 16)
            sp.dma_start(gmix[:, :], g_mix[0].rearrange("(p k) -> p k", k=KT)).then_inc(s["gm_in"], 16)
            sp.dma_start(wlo, w_in[0].rearrange("(p k) n -> p k n", k=KT)[:, :, 3 * AW + 3 * RW:IN_W]).then_inc(s["wlo_in"], 16)
            rows = [(mu[0], 14), (w0[0], FT), (a0[0], FT), (k_k[0], FT), (k_a[0], FT),
                    (r_k[0].rearrange("h j -> (h j)"), FT), (gn_w[0], FT), (gn_b[0], FT)]
            at = 0
            for src, n in rows:
                sp.dma_start(vrow[at:at + n, :], src.rearrange("(r c) -> r c", c=P)).then_inc(s["vec_in"], 16)
                at += n
            sp.dma_start(ca[:, P:C_A], const_a[:, P:C_A]).then_inc(s["ca_in"], 16)
            order = [3, 4, 5, 0, 1, 2]
            for c in range(RING):
                cols = slice(AW * order[c], AW * order[c] + AW)
                sp.dma_start(slot[c], w_in[0].rearrange("(p k) n -> p k n", k=KT)[:, :, cols]).then_inc(s_win[c], 16)
                if c == 0:
                    sp.dma_start(wlor_d[0:64, :], w_dec[0]).then_inc(s["up_in"], 16)
                    sp.dma_start(wlor_d[64:128, :], w_icl[0]).then_inc(s["up_in"], 16)
                    sp.dma_start(wgt[:, :], w_gat[0]).then_inc(s["up_in"], 16)
            sp.dma_start(cb[:, :], const_b).then_inc(s["cb_in"], 16)
            sp.dma_start(gffn[:, :], g_ffn[0].rearrange("(p k) -> p k", k=KT)).then_inc(s["cb_in"], 16)
            sp.dma_start(wrt[:, :, :], w_router[0].rearrange("(p k) e -> p k e", k=KT)).then_inc(s["route_in"], 16)
            sp.dma_start(brt[:, :], b_router[0:1, :].to_broadcast([P, E])).then_inc(s["route_in"], 16)
            for q in range(4):
                sp.dma_start(braw[E * q:E * q + E, 0:512], b_gu[0][:, 512 * q:512 * q + 512]).then_inc(s["braw_in"], 16)
                sp.dma_start(braw[E * q:E * q + E, 512:QB], b_dn[0][:, 256 * q:256 * q + 256]).then_inc(s["braw_in"], 16)
            sp.wait_ge(s["tilde_done"], 4)
            sp.dma_start(abias, const_bias.rearrange("p (h s) -> p h s", h=H)).then_inc(s["bias_in"], 16)
            sp.wait_ge(s["proj_pe"], 13)
            sp.dma_start(wo, w_out[0].rearrange("(m p) n -> p m n", p=P)).then_inc(s["wo_in"], 16)
            sp.wait_ge(s["bsplit_done"], 1)
            sp.wait_ge(s["tok_pe"], 8)
            sp.wait_ge(s["apart_done"], 4)
            sp.wait_ge(s["bonus_done"], 1)
            for part in range(3):
                for q in range(4):
                    sp.dma_start(bsp[E * part:E * part + E, q, :], bpart[part][E * q:E * q + E, :]).then_inc(s["bsp_in"], 16)
            sp.wait_ge(s["zw_pe"], 2)
            sp.dma_start(ring[:, 1, :], expert_chunk(0, 1)).then_inc(s_ring[1], 16)
            sp.wait_ge(s["qu_done"], 2)
            for c in (0, 2, 3):
                sp.dma_start(ring[:, c, :], expert_chunk(0, c)).then_inc(s_ring[c], 16)
            sp.dma_start(gfin, g_fin.unsqueeze(0).to_broadcast([P, D])).then_inc(s["gfin_in"], 16)
            sp.wait_ge(s["wo_pe"], 4)
            for c in (4, 5):
                sp.dma_start(ring[:, c, :], expert_chunk(0, c)).then_inc(s_ring[c], 16)
            sp.wait_ge(s["items_done"], 1)
            n_items = sp.value_load(rint[0:1, ITEMS:ITEMS + 1], min_val=E, max_val=ITEMS)
            with sp.Fori(1, n_items) as i:
                e = sp.value_load(rint[0:1, bass.ds(i, 1)], min_val=0, max_val=E - 1)
                gu = w_gu[0, bass.ds(e, 1)].rearrange("e (p c t) n -> c p (e t n)", c=4, t=2)
                dn = w_dn[0, bass.ds(e, 1)].rearrange("e (h p t) n -> h p (e t n)", h=2, t=4)
                for c in range(RING):
                    sp.wait_ge(s_free[c], i)
                    sp.dma_start(ring[:, c, :], gu[c] if c < 4 else dn[c - 4]).then_inc(s_ring[c], 16)
            for t in range(NT):
                sp.wait_ge(s["fin_done"], t + 1)
                sp.dma_start(out[0, P * t:P * t + P, :], yout[:, t, :]).then_inc(s["out_done"], 16)
            sp.wait_ge(s["out_done"], 16 * NT)

        @block.tensor
        def _(pe):
            def mm(o, l, r, start=True, stop=True):
                return pe.matmul(o, l, r, start=start, stop=stop, skip_group_check=True)

            def model_transposes(src, to, t, ready, done):
                pe.wait_ge(ready, t + 1)
                v = src[:, t, :].rearrange("p (q k) -> p k q", k=KT)
                for u in range(2):
                    for k in range(4):
                        m = pe.transpose(to[2 * t + u][:, P * k:P * k + P], v[:, 4 * u + k, :], ident)
                    m.then_inc(done, 1)

            pe.wait_ge(s["id_in"], 16)
            for t in range(NT):
                model_transposes(xn, bank[4:8], t, s["xn_done"], s["xt_pe"])
            pe.wait_ge(s["vec_in"], 16 * 8)
            pe.transpose(bank[3][:, 0:NV], vrow[:, :], ident[0:NV, 0:NV]).then_inc(s["vt_pe"], 1)
            pe.wait_ge(s["xt_done"], 4)
            pe.wait_ge(s["vt_done"], 1)

            def project(u):
                if u >= 4:
                    pe.wait_ge(s["zcopy"], u - 3)
                if u == 0:
                    pe.wait_ge(s["wlo_in"], 16)
                else:
                    pe.wait_ge(s_win[(u - 1) // 2], 16)
                b = bank[u % 4]
                if u >= 11:
                    t = u - 11
                    for k in range(KT):
                        m = mm(b[:, :], xT[:, k, P * t:P * t + P], slot[5][:, k, :], k == 0, k == KT - 1)
                else:
                    w, c0 = (wlo, 0) if u == 0 else (slot[(u - 1) // 2], 2 * P * ((u - 1) % 2))
                    for j in range(2):
                        for k in range(KT):
                            m = mm(b[:, SEQ * j:SEQ * j + SEQ], w[:, k, c0 + P * j:c0 + P * j + P], xT[:, k, :],
                                   k == 0, k == KT - 1)
                m.then_inc(s["proj_pe"], 1)

            project(0)
            project(1)
            pe.wait_ge(s["up_in"], 48)
            pe.wait_ge(s["tanh_done"], 1)
            for f in range(FT):
                m = mm(bank[4 + f // 2][:, SEQ * (f % 2):SEQ * (f % 2) + SEQ], wlor_d[0:64, P * f:P * f + P], lora[0:64, 0, :])
                if f % 2:
                    m.then_inc(s["dec_pe"], 1)
            for f in range(FT):
                m = mm(bank[6 + f // 2][:, SEQ * (f % 2):SEQ * (f % 2) + SEQ], wlor_d[64:128, P * f:P * f + P], lora[64:128, 0, :])
                if f % 2:
                    m.then_inc(s["icl_pe"], 1)
            project(2)
            project(3)
            pe.wait_ge(s["sgd_done"], 1)
            pe.wait_ge(s["sdec_done"], FT)
            for f in range(FT):
                m = mm(bank[4 + f // 2][:, SEQ * (f % 2):SEQ * (f % 2) + SEQ], wgt[:, P * f:P * f + P], lora[:, 1, :])
                if f % 2:
                    m.then_inc(s["gat_pe"], 1)
            for u in range(4, 7):
                project(u)
            pe.wait_ge(s["ca_in"], 16)
            pe.wait_ge(s["sq_done"], 1)
            pe.wait_ge(s["sicl_done"], FT)
            for j in range(2):
                mm(bank[6 + j][:, :], head_ones, tmp[:, 512 * j:512 * j + 512]).then_inc(s["ss_pe"], 1)
            for u in range(7, 13):
                project(u)
            pe.wait_ge(s["bprod_done"], 1)
            pe.wait_ge(s["gat_done"], 2)
            for j in range(2):
                mm(bank[4 + j][:, :], head_ones, tmp[:, 512 * j:512 * j + 512]).then_inc(s["bsum_pe"], 1)

            pe.wait_ge(s["tilde_done"], 4)
            pe.wait_ge(s["zcopy"], 13)
            for n in range(8):
                arr, t = n // 2, n % 2
                if n >= 4:
                    pe.wait_ge(s["tok_done"], n - 3)
                for f in range(FT):
                    src = (tiles(vT)[:, f, :], ar[:, f, 0, :], tiles(aT)[:, f, :], tiles(kT)[:, f, :])[arr]
                    m = pe.transpose(bank[n % 4][:, P * f:P * f + P], src[:, P * t:P * t + P], ident)
                m.then_inc(s["tok_pe"], 1)

            def scores(f):
                b = [bank[4 + 2 * (f % 2) + hh] for hh in range(2)]
                if f >= 2:
                    pe.wait_ge(s["s_max"], f - 1)
                for c0, q, n in ((0, slice(0, P), P), (P, slice(P, SEQ), SEQ)):
                    for hh in range(2):
                        r = slice(HD * hh, HD * hh + HD)
                        m = mm(b[hh][:, c0:c0 + n], qA[r, f, q], kA[r, f, 0:n])
                m.then_inc(s["s_pe"], 1)

            def turn(f):
                for hh in range(2):
                    h = 2 * f + hh
                    pe.wait_ge(s["en_done"], h + 1)
                    if f >= 1:
                        pe.wait_ge(s["et_done"], h - 1)
                    for n in range(3):
                        m = pe.transpose(bank[hh][:, P * n:P * n + P], sc_e[h % 2][:, P * n:P * n + P], ident)
                    m.then_inc(s["et_pe"], 1)

            def values(f):
                pe.wait_ge(s["et_done"], 2 * f + 2)
                if f >= 2:
                    pe.wait_ge(s["attn_done"], f - 1)
                for t in range(NT):
                    for hh in range(2):
                        h = 2 * f + hh
                        c0 = P * t
                        m = mm(bank[2 + f % 2][HD * hh:HD * hh + HD, c0:SEQ], vA[:, t, HD * h:HD * h + HD],
                               sc_t[h % 2][:, 2 * P * t:SEQ + P * t], t == 0, t == 1)
                m.then_inc(s["pv_pe"], 1)

            pe.wait_ge(s["bonus_done"], 1)
            pe.wait_ge(s["nrm_done"], 2)
            pe.wait_ge(s["tok_done"], 8)
            scores(0)
            scores(1)
            for f in range(FT):
                turn(f)
                if f + 2 < FT:
                    scores(f + 2)
                values(f)

            pe.wait_ge(s["attn_done"], FT)
            pe.wait_ge(s["et_done"], H)
            chunk_rows = [slice(CH * c, CH * c + CH) for c in range(2)]
            head_rows = [slice(HD * j, HD * j + HD) for j in range(2)]
            pe.wait_ge(s["apart_done"], 4)

            def project_out(n, ks):
                t, half = n // 2, n % 2
                for k in ks:
                    m = mm(y_bank[n][:, :], mixT[:, k, P * t:P * t + P], wo[:, k, 512 * half:512 * half + 512], k == 0, k == KT - 1)
                return m

            for t in range(NT):
                for k in range(2):
                    if t:
                        pe.wait_ge(s["nm_done"], 2 * k + 2)
                    for f in (2 * k, 2 * k + 1):
                        ts = [slice(P * t + CH * c, P * t + CH * c + CH) for c in range(2)]
                        for a in range(2):
                            o = 4 * CH * (f % 2) + 2 * CH * a
                            for j in range(2):
                                for c, cr in enumerate(chunk_rows):
                                    mm(bank[2 * k + j][cr, o:o + 2 * CH], heads_apart[:, j, a, f, ts[c]], ar[:, f, :, ts[c]])
                        for c, cr in enumerate(chunk_rows):
                            m = mm(bank[4 + t][cr, P * f:P * f + P], ar[:, f, 0, ts[c]], heads_apart[:, :, 0, f, ts[c]])
                    m.then_inc(s["gram_pe"], 1)
            pe.wait_ge(s["wo_in"], 16)
            project_out(0, range(FT))
            for lv in range(2, LEVELS + 1):
                for t in range(NT):
                    pe.wait_ge(s["lml_done"], 2 * (lv - 2) + t + 1)
                    pe.wait_ge(s["nm_done"], 8)
                    pe.wait_ge(s["ux_done"], 2 * t + 2 if lv == 2 else 4 * (lv - 2) + 2 * t + 2)
                    for h in range(H):
                        for c, cr in enumerate(chunk_rows):
                            m = mm(bank[2 + t][cr, CH * h:CH * h + CH], lml[t][:, h, c, :], uu[t][:, h, :])
                    m.then_inc(s["t1_pe"], 1)
                if lv - 2 < FT:
                    project_out(1, [lv - 2])
                for t in range(NT):
                    pe.wait_ge(s["t1_done"], 2 * (lv - 2) + t + 1)
                    pe.wait_ge(s["low_done"], 2)
                    for h in range(H):
                        b, c0 = level_bank[t][h // 4], 2 * CH * (h % 4)
                        for c, cr in enumerate(chunk_rows):
                            m = mm(b[cr, c0:c0 + CH], xx[t][:, h, c, :], t1s[t][:, h, :])
                        if lv < LEVELS:
                            for c, cr in enumerate(chunk_rows):
                                m = mm(b[cr, c0 + CH:c0 + 2 * CH], t1s[t][:, h, :], xx[t][:, h, c, :])
                        if h % 4 == 3:
                            m.then_inc(s["d_pe"], 1)
            for t in range(NT):
                for h in range(H):
                    for c, cr in enumerate(chunk_rows):
                        m = mm(bank[2 + t][cr, HD * h:HD * h + HD], nm[t][:, h, 2, :], vtok[:, t, c, HD * h:HD * h + HD])
                m.then_inc(s["mv_pe"], 1)
            for t in range(NT):
                pe.wait_ge(s["mv_done"], t + 1)
                pe.wait_ge(s["ux_done"], 22 + 2 * t)
                for h in range(H):
                    for c, cr in enumerate(chunk_rows):
                        m = mm(level_bank[t][h // 4][cr, P * (h % 4):P * (h % 4) + P], xx[t][:, h, c, :], amv[:, t, h, :, :])
                m.then_inc(s["zw_pe"], 1)
            for t in range(NT):
                pe.wait_ge(s["zw_done"], 4 * t + 4)
                pe.wait_ge(s["mv_done"], 2)
                for c in range(2):
                    b = level_bank[t][c]
                    for f in range(FT):
                        for j, hr in enumerate(head_rows):
                            mm(b[hr, CH * f:CH * f + CH], nzw[t][:, c, 2 * f + j, 0:HD], nm[t][:, 2 * f + j, 1, :])
                        for j, hr in enumerate(head_rows):
                            h = 2 * f + j
                            mm(b[hr, SEQ + CH * f:SEQ + CH * f + CH], vtok[:, t, c, HD * h:HD * h + HD], nm[t][:, h, 3, :], True, False)
                        for j, hr in enumerate(head_rows):
                            m = mm(b[hr, SEQ + CH * f:SEQ + CH * f + CH], nzw[t][:, c, 2 * f + j, HD:2 * HD], nm[t][:, 2 * f + j, 1, :], False, True)
                m.then_inc(s["gc_pe"], 1)
                if t:
                    pe.wait_ge(s["qu_done"], t)
                for c in range(2):
                    b = bank[2 + c]
                    if 2 * t + c == NCH - 1:
                        break
                    for f in range(FT):
                        hs = [(hr, 2 * f + j, slice(HD * (2 * f + j), HD * (2 * f + j) + HD)) for j, hr in enumerate(head_rows)]
                        if 2 * t + c:
                            for hr, h, hc in hs:
                                mm(b[hr, HD * f:HD * f + HD], nzw[t][:, c, h, 0:HD], btok[:, t, hc])
                        for hr, h, hc in hs:
                            mm(b[hr, SEQ + HD * f:SEQ + HD * f + HD], ktok[:, t, hc], vtok[:, t, c, hc], True, False)
                        for hr, h, hc in hs:
                            m = mm(b[hr, SEQ + HD * f:SEQ + HD * f + HD], btok[:, t, hc], nzw[t][:, c, h, HD:2 * HD], False, True)
                m.then_inc(s["qu_pe"], 1)
            for cc in range(1, NCH):
                pe.wait_ge(s["qu_done"], cc // 2 + 1)
                pe.wait_ge(s["gc_done"], cc // 2 + 1)
                if cc >= 2:
                    pe.wait_ge(s["st_done"], cc - 1)
                if cc < NCH - 1:
                    for h in range(H):
                        f, hr = h // 2, head_rows[h % 2]
                        m = mm(bank[0][hr, HD * f:HD * f + HD], tt[hr, cc, f, :], state[hr, cc - 1, f, :])
                    m.then_inc(s["st_pe"], 1)
                if cc >= 2:
                    pe.wait_ge(s["y_done"], cc - 1)
                for h in range(H):
                    f, hr = h // 2, head_rows[h % 2]
                    m = mm(bank[1][hr, HD * f:HD * f + HD], state[hr, cc - 1, f, :], gg[hr, f, CH * cc:CH * cc + CH])
                m.then_inc(s["yp_pe"], 1)

            pe.wait_ge(s["y_done"], 3)
            yflat = yT.rearrange("p f t -> p (f t)")
            for j in range(2):
                mm(bank[2 + j][:, :], head_mean, yflat[:, 512 * j:512 * j + 512]).then_inc(s["mu_pe"], 1)
            pe.wait_ge(s["gc_done"], 2)
            project_out(2, range(FT))
            pe.wait_ge(s["ysq_done"], 1)
            for j in range(2):
                mm(bank[4 + j][:, :], head_mean, ysq[:, 512 * j:512 * j + 512]).then_inc(s["var_pe"], 1)
            project_out(3, range(FT))
            pe.wait_ge(s["mix_done"], 1)
            for n in range(3):
                project_out(n, range(FT, KT)).then_inc(s["wo_pe"], 1)

            def logits(t):
                pe.wait_ge(s["ht_done"], 2 * t + 2)
                pe.wait_ge(s["route_in"], 32)
                for k in range(KT):
                    m = mm(bank[2][:, E * t:E * t + E], hT[:, k, P * t:P * t + P], wrt[:, k, :], k == 0, k == KT - 1)
                m.then_inc(s["lg_pe"], 1)

            pe.wait_ge(s["sd_done"], 2)
            model_transposes(xs, bank[2:6], 0, s["xs_done"], s["ht_pe"])
            project_out(3, range(FT, KT)).then_inc(s["wo_pe"], 1)
            logits(0)
            model_transposes(xs, bank[2:6], 1, s["xs_done"], s["ht_pe"])
            logits(1)
            pe.wait_ge(s["cb_in"], 32)
            pe.wait_ge(s["pick_done"], 1)
            tri, ones = cb[:, C_TRI:C_TRI + P], cb[:, C_ONE:C_ONE + P]
            mm(bank[3][:, 0:E], tri, picked[:, 0, :])
            mm(bank[3][:, E:2 * E], ones, picked[:, 0, :], True, False)
            mm(bank[3][:, E:2 * E], tri, picked[:, 1, :], False, True)
            mm(bank[3][0:E, 64:65], picked[:, 0, :], ones[:, 0:1], True, False)
            mm(bank[3][0:E, 64:65], picked[:, 1, :], ones[:, 0:1], False, True).then_inc(s["rank_pe"], 1)
            pe.wait_ge(s["extra_done"], 1)
            mm(bank[4][0:E, 0:1], tri[0:E, 0:E], extra[:, 2:3])
            mm(bank[4][0:1, 64:65], extra[:, 2:3], ones[0:E, 0:1]).then_inc(s["start_pe"], 1)
            pe.wait_ge(s["slot_done"], 1)
            for t in range(NT):
                pe.transpose(bank[5][0:E, P * t:P * t + P], slotv[:, t, :], ident)
                m = pe.transpose(bank[5][0:E, SEQ + P * t:SEQ + P * t + P], gates[:, t, :], ident)
            m.then_inc(s["svt_pe"], 1)
            pe.wait_ge(s["oh_done"], 1)
            pe.wait_ge(s["svt_done"], 1)
            for t in range(NT):
                mm(bank[2][:, 64 * t:64 * t + ITEMS], svT[:, 0, P * t:P * t + P], oh, True, False)
                mm(bank[2][:, 64 * t:64 * t + ITEMS], ones[0:E, :], back, False, True)
                mm(bank[2][:, P + 64 * t:P + 64 * t + ITEMS], svT[:, 1, P * t:P * t + P], oh)
            mm(bank[2][0:1, SEQ:SEQ + ITEMS], cb[0:E, C_ECOL:C_ECOL + 1], oh).then_inc(s["col_pe"], 1)

            xg = m_xg.rearrange("p (k c) -> p k c", k=KT)
            act_v = m_a.rearrange("p (q t) -> p t q", t=4)
            actT = m_at.rearrange("p (t c) -> p t c", t=4)

            def gather():
                for k in range(KT):
                    for n in range(6):
                        t, part = n // 3, n % 3
                        w = xsplit[:, t, part, :].rearrange("p (q k) -> p k q", k=KT)[:, k, :]
                        m = mm(b_x[:, SLOTS * k:SLOTS * k + SLOTS], w, m_p[:, t, :], n == 0, n == 5)
                m.then_inc(s["ga_pe"], 1)

            def scatter(done):
                for t in range(NT):
                    for half in range(2):
                        r0 = slice(SLOTS * half, SLOTS * half + SLOTS)
                        m = mm(y_bank[2 * t + half][:, :], m_gt[r0, P * t:P * t + P], m_os[r0, :], False, False)
                m.then_inc(done, 1)

            pe.wait_ge(s["split_done"], 6)
            pe.wait_ge(s["p_ready"], 1)
            gather()
            pe.wait_ge(s["bsp_in"], 16 * 12)
            pe.wait_ge(s["items_done"], 1)
            n_items = pe.value_load(rint[0:1, ITEMS:ITEMS + 1], min_val=E, max_val=ITEMS)
            with pe.Fori(0, n_items) as i:
                pe.wait_ge(s["xg_ready"], i + 1)
                pe.wait_ge(s["gt_done"], i + 1)
                for c in range(4):
                    pe.wait_ge(s_ring[c], 16 * i + 16)
                    for k in range(2):
                        for col, b in ((0, b_g), (FF, b_u)):
                            for half in range(2):
                                c0 = 2 * FF * k + col + 512 * half
                                m = mm(b[SLOTS * half:SLOTS * half + SLOTS, :], xg[:, 2 * c + k, :], ring[:, c, c0:c0 + 512],
                                       c == 0 and k == 0, False)
                    m.then_inc(s_free[c], 1)
                pe.wait_ge(s["sel_ready"], i + 1)
                for col, b in ((0, b_g), (FF, b_u)):
                    for half in range(2):
                        m = mm(b[SLOTS * half:SLOTS * half + SLOTS, :], m_sel[0:3 * E, :],
                               bsp[0:3 * E, col // 512 + half, 0:512], False, True)
                m.then_inc(s["gu_pe"], 1)
                pe.wait_ge(s["os_done"], i + 1)
                scatter(s["sc_pe"])
                pe.wait_ge(s["p_ready"], i + 2)
                gather()
                pe.wait_ge(s["act_done"], i + 1)
                for t in range(4):
                    m = pe.transpose(b_d[:, P * t:P * t + P], act_v[:, t, :], ident)
                m.then_inc(s["tr_pe"], 1)
                pe.wait_ge(s["g2_ready"], i + 1)
                for t in range(NT):
                    m = pe.transpose(b_g[:, P * t:P * t + P], m_g2[:, t, :], ident)
                m.then_inc(s["gtt_pe"], 1)
                pe.wait_ge(s["at_done"], i + 1)
                for h in range(2):
                    pe.wait_ge(s_ring[4 + h], 16 * i + 16)
                    for t in range(4):
                        for half in range(2):
                            m = mm(b_d[SLOTS * half:SLOTS * half + SLOTS, :], actT[:, t, SLOTS * h:SLOTS * h + SLOTS],
                                   ring[:, 4 + h, FF * t + 512 * half:FF * t + 512 * half + 512], h == 0 and t == 0, False)
                    m.then_inc(s_free[4 + h], 1)
                for half in range(2):
                    m = mm(b_d[SLOTS * half:SLOTS * half + SLOTS, :], m_sel[0:3 * E, :],
                           bsp[0:3 * E, 2 * half:2 * half + 2, 512:QB], False, True)
                m.then_inc(s["dn_pe"], 1)
            pe.wait_ge(s["os_done"], n_items + 1)
            pe.wait_ge(s["gt_done"], n_items + 1)
            scatter(s["scf_pe"])

        @block.scalar
        def _(act):
            def sqrt_of(o, i, scale, bias, done=None):
                ins = nc.scalar.activation(o, i, ACT.Sqrt, bias=bias, scale=scale)
                if done is not None:
                    ins.then_inc(done, 1)
                return ins

            act.wait_ge(s["zpad0"], 1)
            for t in range(NT):
                act.wait_ge(s_x[t], 16)
                act.activation(xn[:, t, :], resid[:, t, :], ACT.Square, accum_out=st[:, t:t + 1]).then_inc(s["a_chain"], 1)
                act.wait_ge(s["a_chain"], t + 1)
                act.activation(st[:, 2 + t:3 + t], st[:, t:t + 1], ACT.Sqrt, scale=1.0 / D, bias=st[:, 6:7]).then_inc(s["hsq_done"], 1)

            def copy_unit(u):
                act.wait_ge(s["proj_pe"], u + 1)
                if 2 <= u < 7:
                    act.wait_ge(s["zshift"], 2 * (u - 1))
                src = bank[u % 4][:, :].rearrange("p (j t) -> p j t", j=2)
                if u < 7:
                    act.copy(zpad[:, u % 2, :, 1:], src).then_inc(s["zcopy"], 1)
                elif u < 9:
                    act.mul(qA[:, 2 * (u - 7):2 * (u - 7) + 2, :], src, HD ** -0.5).then_inc(s["zcopy"], 1)
                elif u < 11:
                    act.copy(kA[:, 2 * (u - 9):2 * (u - 9) + 2, :], src).then_inc(s["zcopy"], 1)
                else:
                    act.copy(vA[:, u - 11, :], bank[u % 4][:, :]).then_inc(s["zcopy"], 1)

            act.wait_ge(s["zpad0"], 1)
            copy_unit(0)
            copy_unit(1)
            act.wait_ge(s["zshift"], 2)
            act.activation(lora[0:64, 0, :], lora[0:64, 0, :], ACT.Tanh).then_inc(s["tanh_done"], 1)
            act.activation(lora[:, 1, :], lora[:, 1, :], ACT.Sigmoid).then_inc(s["sgd_done"], 1)
            for f in range(FT):
                act.wait_ge(s["dec_pe"], f // 2 + 1)
                act.activation(tiles(sw)[:, f, :], bank[4 + f // 2][:, SEQ * (f % 2):SEQ * (f % 2) + SEQ], ACT.Sigmoid,
                               bias=vec("w0", f)).then_inc(s["sdec_done"], 1)
            for f in range(FT):
                act.wait_ge(s["icl_pe"], f // 2 + 1)
                act.activation(tiles(aT)[:, f, :], bank[6 + f // 2][:, SEQ * (f % 2):SEQ * (f % 2) + SEQ], ACT.Sigmoid,
                               bias=vec("a0", f)).then_inc(s["sicl_done"], 1)
            copy_unit(2)
            copy_unit(3)
            for j in range(2):
                act.wait_ge(s["gat_pe"], j + 1)
                act.copy(gT[:, 512 * j:512 * j + 512], bank[4 + j][:, :]).then_inc(s["gat_done"], 1)
            copy_unit(4)
            copy_unit(5)
            copy_unit(6)
            act.wait_ge(s["exps_done"], 1)
            act.activation(pinv, cum, ACT.Exp, scale=DECAY_C).then_inc(s["a_chain"], 1)
            act.activation(sw, sw, ACT.Exp, scale=-DECAY_C).then_inc(s["a_chain"], 1)
            act.wait_ge(s["a_chain"], 4)
            act.activation(cum, cum, ACT.Exp, scale=-DECAY_C).then_inc(s["a_chain"], 1)
            for j in range(2):
                act.wait_ge(s["ss_pe"], j + 1)
                act.activation(tmp[:, 512 * j:512 * j + 512], bank[6 + j][:, :], ACT.Sqrt).then_inc(s["nrm_done"], 1)
            for u in range(7, 13):
                copy_unit(u)
            for n in range(8):
                arr, t = n // 2, n % 2
                act.wait_ge(s["tok_pe"], n + 1)
                src = bank[n % 4][:, :]
                if arr == 0:
                    act.wait_ge(s["zero_done"], 2)
                    for c in range(2):
                        cr = slice(CH * c, CH * c + CH)
                        ins = act.copy(vtok[cr, t, c, :], src[cr, :])
                elif arr == 1:
                    ins = act.copy(amv[:, t, :, 0, :], src.rearrange("p (h j) -> p h j", h=H))
                else:
                    ins = act.copy((btok, ktok)[arr - 2][:, t, :], src)
                ins.then_inc(s["tok_done"], 1)

            def exps(h):
                f = h // 2
                act.wait_ge(s["s_max"], f + 1)
                if f >= 1:
                    act.wait_ge(s["et_pe"], h - 1)
                for j, (c0, n) in enumerate(((0, P), (P, SEQ))):
                    c = 16 + 2 * h + j
                    act.activation(sc_e[h % 2][:, c0:c0 + n], sc_s[h % 2][:, c0:c0 + n], ACT.Exp,
                                   bias=st[:, c:c + 1], accum_out=st[:, c + 16:c + 17]).then_inc(s["e_done"], 1)

            def et_copy(h):
                act.wait_ge(s["et_pe"], h + 1)
                if h >= 2:
                    act.wait_ge(s["pv_pe"], h // 2)
                act.copy(sc_t[h % 2], bank[h % 2][:, 0:3 * P]).then_inc(s["et_done"], 1)

            exps(0)
            exps(1)
            for f in range(FT):
                et_copy(2 * f)
                et_copy(2 * f + 1)
                if f + 1 < FT:
                    exps(2 * f + 2)
                    exps(2 * f + 3)
                act.wait_ge(s["pv_pe"], f + 1)
                act.copy(mixT[:, f, :], bank[2 + f % 2][:, 0:SEQ]).then_inc(s["attn_done"], 1)

            for t in range(NT):
                act.wait_ge(s["gram_pe"], 2 * t + 2)
                act.copy(low[t], bank[4 + t][:, :].rearrange("p (h s) -> p h s", h=H)).then_inc(s["low_done"], 1)
            for lv in range(2, LEVELS + 1):
                for t in range(NT):
                    act.wait_ge(s["t1_pe"], 2 * (lv - 2) + t + 1)
                    if lv > 2:
                        act.wait_ge(s["d_pe"], 4 * (lv - 3) + 2 * t + 2)
                    act.copy(t1s[t], bank[2 + t][:, :].rearrange("p (h s) -> p h s", h=H)).then_inc(s["t1_done"], 1)
            for t in range(NT):
                act.wait_ge(s["mv_pe"], t + 1)
                act.copy(amv[:, t, :, 1, :], bank[2 + t][:, :].rearrange("p (h j) -> p h j", h=H)).then_inc(s["mv_done"], 1)
            for t in range(NT):
                act.wait_ge(s["zw_pe"], t + 1)
                for j in range(2):
                    for c in range(2):
                        cr = slice(CH * c, CH * c + CH)
                        act.mul(nzw[t][cr, c, 4 * j:4 * j + 4, :], level_bank[t][j][cr, :].rearrange("p (h s) -> p h s", h=4),
                                -1.0).then_inc(s["zw_done"], 1)
            act.wait_ge(s["yc_done"], 2)
            act.activation(ysq, yc, ACT.Square).then_inc(s["ysq_done"], 1)
            for j in range(2):
                act.wait_ge(s["var_pe"], j + 1)
                act.activation(yT.rearrange("p f t -> p (f t)")[:, 512 * j:512 * j + 512], bank[4 + j][:, :], ACT.Sqrt,
                               bias=st[:, 7:8]).then_inc(s["sd_done"], 1)
            def mean_square(t):
                act.wait_ge(s["h_done"], 2 * t + 2)
                act.activation(blk(B_I), xs[:, t, :], ACT.Square, accum_out=st[:, 8 + t:9 + t]).then_inc(s["a_chain"], 1)
                act.wait_ge(s["a_chain"], 6 + t)
                act.activation(st[:, 10 + t:11 + t], st[:, 8 + t:9 + t], ACT.Sqrt, scale=1.0 / D, bias=st[:, 6:7]).then_inc(s["hsq_done"], 1)

            def split(t, part):
                if part == 0:
                    act.wait_ge(s["xs_done"], t + 1)
                else:
                    act.wait_ge(s["rem_done"], 2 * t + part)
                act.copy(xsplit[:, t, part, :], xs[:, t, :] if part == 0 else xrem[:, t, :]).then_inc(s["split_done"], 1)

            mean_square(0)
            act.wait_ge(s["yp_pe"], 3)
            split(0, 0)
            split(0, 1)
            mean_square(1)
            split(0, 2)
            for part in range(3):
                split(1, part)
            act.wait_ge(s["lg_done"], 1)
            for t in range(NT):
                act.activation(ex4[:, t, :], mx8[:, t, 0:TOPK], ACT.Exp, bias=st[:, 48 + t:49 + t],
                               accum_out=st[:, 50 + t:51 + t]).then_inc(s["ex_done"], 1)
            act.wait_ge(s["svt_pe"], 1)
            act.copy(svT, bank[5][0:E, :].rearrange("p (w t) -> p w t", w=2)).then_inc(s["svt_done"], 1)

            act.wait_ge(s["items_done"], 1)
            n_items = act.value_load(rint[0:1, ITEMS:ITEMS + 1], min_val=E, max_val=ITEMS)
            with act.Fori(0, n_items) as i:
                act.wait_ge(s["gm_done"], i + 1)
                act.activation(m_s, m_g, ACT.Sigmoid, scale=ALPHA).then_inc(s["sg_done"], 1)
                act.wait_ge(s["tr_pe"], i + 1)
                act.copy(m_at, bank[5][:, :]).then_inc(s["at_done"], 1)
                act.wait_ge(s["gtt_pe"], i + 1)
                act.copy(m_gt, b_g[:, 0:SEQ]).then_inc(s["gt_done"], 1)
                act.wait_ge(s["dn_pe"], i + 1)
                act.copy(m_os, bank[5][:, :]).then_inc(s["os_done"], 1)
            for t in range(NT):
                act.wait_ge(s["yfin_done"], 2 * t + 2)
                act.activation(stage[:, t, :], yout[:, t, :], ACT.Square, accum_out=st[:, 56 + t:57 + t]).then_inc(s["fsq_done"], 1)
                act.wait_ge(s["fsq_done"], 2 * t + 1)
                act.activation(st[:, 58 + t:59 + t], st[:, 56 + t:57 + t], ACT.Sqrt, scale=1.0 / D, bias=st[:, 6:7]).then_inc(s["fsq_done"], 1)

        @block.gpsimd
        def _(pool):
            steps = [0]

            def link(ins):
                ins.then_inc(s["p_chain"], 1)
                steps[0] += 1
                pool.wait_ge(s["p_chain"], steps[0])

            pool.wait_ge(s["braw_in"], 16 * 8)
            pool.wait_ge(s["proj_pe"], 1)
            link(pool.tensor_copy(bpart[0], braw))
            link(pool.tensor_tensor(braw, braw, bpart[0], ALU.subtract))
            link(pool.tensor_copy(bpart[1], braw))
            link(pool.tensor_tensor(braw, braw, bpart[1], ALU.subtract))
            pool.tensor_copy(bpart[2], braw).then_inc(s["bsplit_done"], 1)
            pool.wait_ge(s["proj_pe"], 5)
            pool.memset(apart, 0.0).then_inc(s["zero_done"], 1)
            pool.wait_ge(s["proj_pe"], 9)
            pool.memset(work[:, 4096:6144], 0.0).then_inc(s["zero_done"], 1)
            pool.wait_ge(s["zero_done"], 2)
            for a, (src, ready) in enumerate(((aT, 2), (kT, 3))):
                pool.wait_ge(s["tilde_done"], ready)
                for j in range(2):
                    r = slice(HD * j, HD * j + HD)
                    pool.tensor_copy(heads_apart[r, j, a, :, :], tiles(src)[r, :, :]).then_inc(s["apart_done"], 1)
                    pool.wait_ge(s["apart_done"], 2 * a + j + 1)
            for lv in range(2, LEVELS + 1):
                for t in range(NT):
                    pool.wait_ge(s["low_done"], t + 1)
                    n = 2 * (lv - 2) + t
                    if n >= 2:
                        pool.wait_ge(s["t1_pe"], n - 1)
                    for c in range(2):
                        cr = slice(CH * c, CH * c + CH)
                        ins = pool.tensor_tensor(lml[t][cr, :, c, :], low[t][cr, :, :],
                                                 ca[cr, C_LEVEL + (lv - 1) * CH:C_LEVEL + lv * CH].unsqueeze(1).to_broadcast(
                                                     [CH, H, CH]), ALU.mult)
                        if c == 0:
                            link(ins)
                    ins.then_inc(s["lml_done"], 1)
                    pool.wait_ge(s["lml_done"], n + 1)
            pool.wait_ge(s["mix_done"], 1)
            for t in range(NT):
                for part in range(2):
                    pool.wait_ge(s["split_done"], 3 * t + part + 1)
                    if part:
                        pool.wait_ge(s["rem_done"], 2 * t + 1)
                    pool.tensor_tensor(xrem[:, t, :], xs[:, t, :] if part == 0 else xrem[:, t, :], xsplit[:, t, part, :],
                                       ALU.subtract).then_inc(s["rem_done"], 1)

        @block.vector
        def _(v):
            steps = [0]

            def link(ins):
                ins.then_inc(s["v_chain"], 1)
                steps[0] += 1
                v.wait_ge(s["v_chain"], steps[0])

            def bc(col, n):
                return col.unsqueeze(2).to_broadcast([P, col.shape[1], n])

            def rows(ap):
                return ap.rearrange("p f t -> p (f t)")

            v.memset(st[:, 6:7], RMS_EPS)
            v.memset(st[:, 7:8], GN_EPS)
            v.memset(oh3[:, :], 0.0)
            v.memset(zpad[:, :, :, 0:1], 0.0).then_inc(s["zpad0"], 1)
            for t in range(NT):
                v.wait_ge(s["hsq_done"], t + 1)
                link(v.reciprocal(st[:, 4 + t:5 + t], st[:, 2 + t:3 + t]))
                v.tensor_scalar(xn[:, t, :], resid[:, t, :], st[:, 4 + t:5 + t], None, ALU.mult).then_inc(s["xn_done"], 1)

            def feature_major(dst, src, g, t, ready, done):
                for u in range(2):
                    v.wait_ge(ready, 2 * t + u + 1)
                    v.tensor_tensor(dst[:, 4 * u:4 * u + 4, P * t:P * t + P], src[2 * t + u][:, :].rearrange("p (k t) -> p k t", k=4),
                                    bc(g[:, 4 * u:4 * u + 4], P), ALU.mult).then_inc(done, 1)

            v.wait_ge(s["gm_in"], 16)
            for t in range(NT):
                feature_major(xT, bank[4:8], gmix, t, s["xt_pe"], s["xt_done"])
            v.wait_ge(s["vt_pe"], 1)
            v.tensor_copy(vcol[:, :], bank[3][:, 0:NV]).then_inc(s["vt_done"], 1)
            v.wait_ge(s["vt_done"], 1)

            def shift(u):
                v.wait_ge(s["zcopy"], u + 1)
                z = zpad[:, u % 2, :, :]
                if u == 0:
                    dst, m0 = lora[:, :, :], 12
                else:
                    dst = tiles((rT, kT, vT)[(u - 1) // 2])[:, 2 * ((u - 1) % 2):2 * ((u - 1) % 2) + 2, :]
                    m0 = 2 * (u - 1)
                if u == 1:
                    v.wait_ge(s["xt_pe"], 4)
                v.tensor_tensor(dst, z[:, :, 0:SEQ], z[:, :, 1:SEQ + 1], ALU.subtract).then_inc(s["zshift"], 1)
                v.wait_ge(s["zshift"], 2 * u + 1)
                for j in range(2):
                    ins = v.scalar_tensor_tensor(out=dst[:, j, :], in0=dst[:, j, :], scalar=vcol[:, m0 + j:m0 + j + 1],
                                                 in1=z[:, j, 1:SEQ + 1], op0=ALU.mult, op1=ALU.add)
                ins.then_inc(s["zshift"], 1)

            for u in range(3):
                shift(u)
            v.wait_ge(s["ca_in"], 16)
            v.wait_ge(s["sdec_done"], FT)
            for f in range(FT):
                ins = v.tensor_tensor_scan(tiles(cum)[:, f, :], scan_keep, tiles(sw)[:, f, :], 0.0, ALU.mult, ALU.add)
            link(ins)
            v.tensor_tensor(sw, cum, sw, ALU.subtract).then_inc(s["exps_done"], 1)
            shift(3)
            shift(4)
            v.wait_ge(s["zshift"], 10)
            for f in range(FT):
                ins = v.tensor_scalar(tiles(kkT)[:, f, :], tiles(kT)[:, f, :], vec("kk", f), None, ALU.mult)
            link(ins)
            v.tensor_tensor(tmp, kkT, kkT, ALU.mult).then_inc(s["sq_done"], 1)
            shift(5)
            shift(6)
            v.wait_ge(s["nrm_done"], 2)
            link(v.tensor_scalar(tmp, tmp, 1e-12, None, ALU.max))
            link(v.reciprocal(tmp, tmp))
            link(v.tensor_tensor(kkT, kkT, tmp, ALU.mult))
            v.wait_ge(s["sicl_done"], FT)
            for f in range(FT):
                ins = v.tensor_scalar(tiles(tmp)[:, f, :], tiles(aT)[:, f, :], -1.0, vec("ka", f), ALU.add, ALU.mult)
            link(ins)
            link(v.scalar_tensor_tensor(out=kT, in0=tmp, scalar=1.0, in1=kT, op0=ALU.add, op1=ALU.mult))
            v.wait_ge(s["zshift"], 14)
            for f in range(FT):
                ins = v.scalar_tensor_tensor(out=tiles(tmp)[:, f, :], in0=tiles(rT)[:, f, :], scalar=vec("rk", f),
                                             in1=tiles(kT)[:, f, :], op0=ALU.mult, op1=ALU.mult)
            ins.then_inc(s["bprod_done"], 1)
            v.wait_ge(s["a_chain"], 5)
            link(v.tensor_tensor(aT, aT, kkT, ALU.mult))
            v.tensor_tensor(ar[:, :, 0, :], tiles(kkT), tiles(sw), ALU.mult).then_inc(s["tilde_done"], 1)
            v.tensor_tensor(aT, aT, pinv, ALU.mult).then_inc(s["tilde_done"], 1)
            v.wait_ge(s["bprod_done"], 1)
            v.tensor_tensor(kT, kT, pinv, ALU.mult).then_inc(s["tilde_done"], 1)
            v.tensor_tensor(ar[:, :, 1, :], tiles(rT), tiles(cum), ALU.mult).then_inc(s["tilde_done"], 1)
            v.wait_ge(s["bsum_pe"], 2)
            v.wait_ge(s["tilde_done"], 4)
            for j in range(2):
                ins = v.tensor_tensor(kkT[:, 512 * j:512 * j + 512], bank[4 + j][:, :], vT[:, 512 * j:512 * j + 512], ALU.mult)
            ins.then_inc(s["bonus_done"], 1)

            v.wait_ge(s["bias_in"], 16)

            def biased(f):
                v.wait_ge(s["s_pe"], f + 1)
                if f >= 1:
                    v.wait_ge(s["e_done"], 4 * f)
                for hh in range(2):
                    b, h = bank[4 + 2 * (f % 2) + hh], 2 * f + hh
                    v.tensor_tensor_reduce(sc_s[hh][:, 0:P], b[:, 0:P], abias[:, h, P:SEQ], 1.0, -3e38,
                                           ALU.add, ALU.max, st[:, 60 + 2 * hh:61 + 2 * hh])
                    ins = v.tensor_tensor_reduce(sc_s[hh][:, P:3 * P], b[:, P:3 * P], abias[:, h, :], 1.0, -3e38,
                                                 ALU.add, ALU.max, st[:, 61 + 2 * hh:62 + 2 * hh])
                link(ins)
                v.tensor_scalar(st[:, 16 + 4 * f:20 + 4 * f], st[:, 60:64], -1.0, None, ALU.mult).then_inc(s["s_max"], 1)
                v.wait_ge(s["s_max"], f + 1)

            def normalise(f):
                for hh in range(2):
                    h = 2 * f + hh
                    v.wait_ge(s["e_done"], 2 * h + 2)
                    link(v.reciprocal(st[:, 66 + 2 * hh:68 + 2 * hh], st[:, 32 + 2 * h:34 + 2 * h]))
                    v.tensor_scalar(sc_e[hh][:, 0:P], sc_e[hh][:, 0:P], st[:, 66 + 2 * hh:67 + 2 * hh], None, ALU.mult)
                    v.tensor_scalar(sc_e[hh][:, P:3 * P], sc_e[hh][:, P:3 * P], st[:, 67 + 2 * hh:68 + 2 * hh], None,
                                    ALU.mult).then_inc(s["en_done"], 1)
                v.wait_ge(s["en_done"], 2 * f + 2)

            for f in range(FT):
                biased(f)
                normalise(f)

            v.wait_ge(s["attn_done"], FT)
            v.wait_ge(s["pv_pe"], FT)
            v.wait_ge(s["bsp_in"], 16 * 12)
            v.wait_ge(s["zero_done"], 1)
            for t in range(NT):
                for k in range(2):
                    v.wait_ge(s["gram_pe"], 2 * t + k + 1)
                    for j in range(2):
                        o = nm[t].rearrange("p (k r j) w s -> p k j r (w s)", k=2, j=2)[:, k, j]
                        v.tensor_tensor(o, bank[2 * k + j][:, :].rearrange("p (r x) -> p r x", r=2),
                                        mask4.unsqueeze(1).to_broadcast([P, 2, 4 * CH]), ALU.mult).then_inc(s["nm_done"], 1)
                v.wait_ge(s["nm_done"], 4 * t + 4)
                v.wait_ge(s["low_done"], t + 1)
                link(v.tensor_tensor(uu[t], low[t], level_mask(1), ALU.mult))
                for c in range(2):
                    cr = slice(CH * c, CH * c + CH)
                    ins = v.tensor_tensor(xx[t][cr, :, c, :], eye2[cr, :].unsqueeze(1).to_broadcast([CH, H, CH]), uu[t][cr, :, :],
                                          ALU.subtract)
                ins.then_inc(s["ux_done"], 1)
                v.wait_ge(s["ux_done"], 2 * t + 1)
                v.tensor_tensor(uu[t], eye2.unsqueeze(1).to_broadcast([P, H, CH]), nm[t][:, :, 0, :], ALU.subtract).then_inc(s["ux_done"], 1)
            for lv in range(2, LEVELS + 1):
                for t in range(NT):
                    v.wait_ge(s["ux_done"], 4 if lv == 2 else 4 * (lv - 2) + 2 * t + 2)
                    v.wait_ge(s["d_pe"], 4 * (lv - 2) + 2 * t + 2)
                    for j in range(2):
                        hs = slice(4 * j, 4 * j + 4)
                        d2 = level_bank[t][j][:, :].rearrange("p (h w s) -> p h w s", h=4, w=2)
                        if lv < LEVELS:
                            v.tensor_tensor(uu[t][:, hs, :], uu[t][:, hs, :], d2[:, :, 0, :], ALU.subtract)
                        for c in range(2):
                            cr, w = slice(CH * c, CH * c + CH), 1
                            old = xx[t][cr, hs, c, :]
                            if lv == LEVELS:
                                old, w = uu[t][cr, hs, :], 0
                            ins = v.tensor_tensor(xx[t][cr, hs, c, :], old, d2[cr, :, w, :], ALU.subtract)
                        ins.then_inc(s["ux_done"], 1)

            def heads(ap):
                return ap.rearrange("p (f t) -> p f t", f=FT)

            for t in range(NT):
                v.wait_ge(s["gc_pe"], t + 1)
                for c in range(2):
                    ts = slice(P * t + CH * c, P * t + CH * c + CH)
                    b = level_bank[t][c]
                    v.tensor_tensor(gg[:, :, ts], heads(b[:, 0:SEQ]), ar[:, :, 1, ts], ALU.add)
                    ins = v.tensor_copy(yT[:, :, ts], heads(b[:, SEQ:2 * SEQ]))
                ins.then_inc(s["gc_done"], 1)
                v.wait_ge(s["qu_pe"], t + 1)
                for c in range(2):
                    cc, b = 2 * t + c, bank[2 + c]
                    if 0 < cc < NCH - 1:
                        v.tensor_tensor(tt[:, cc, :, :], heads(b[:, 0:SEQ]), eye2.unsqueeze(1).to_broadcast([P, FT, HD]), ALU.add)
                    if cc < NCH - 1:
                        ins = v.tensor_tensor(state[:, cc, :, :], heads(b[:, SEQ:2 * SEQ]),
                                              bc(tiles(cum)[:, :, CH * cc + CH - 1], HD), ALU.mult)
                ins.then_inc(s["qu_done"], 1)
            for cc in range(1, NCH):
                if cc < NCH - 1:
                    v.wait_ge(s["st_pe"], cc)
                    link(v.tensor_tensor(stmp, heads(bank[0][:, 0:SEQ]), bc(tiles(cum)[:, :, CH * cc + CH - 1], HD), ALU.mult))
                    v.wait_ge(s["qu_done"], cc // 2 + 1)
                    v.tensor_tensor(state[:, cc, :, :], state[:, cc, :, :], stmp, ALU.add).then_inc(s["st_done"], 1)
                v.wait_ge(s["yp_pe"], cc)
                v.wait_ge(s["gc_done"], 2)
                o = yT[:, :, CH * cc:CH * cc + CH]
                v.tensor_tensor(o, heads(bank[1][:, 0:SEQ]), o, ALU.add).then_inc(s["y_done"], 1)

            v.wait_ge(s["y_done"], 3)
            for j in range(2):
                v.wait_ge(s["mu_pe"], j + 1)
                v.tensor_tensor(yc[:, 512 * j:512 * j + 512], rows(yT)[:, 512 * j:512 * j + 512], bank[2 + j][:, :],
                                ALU.subtract).then_inc(s["yc_done"], 1)
            v.wait_ge(s["sd_done"], 2)
            link(v.reciprocal(rows(yT), rows(yT)))
            link(v.tensor_tensor(yc, yc, rows(yT), ALU.mult))
            for f in range(FT):
                ins = v.tensor_scalar(tiles(yc)[:, f, :], tiles(yc)[:, f, :], vec("gw", f), vec("gb", f), ALU.mult, ALU.add)
            link(ins)
            link(v.tensor_tensor(yc, yc, kkT, ALU.add))
            v.tensor_tensor(rows(mixT[:, FT:KT, :]), yc, gT, ALU.mult).then_inc(s["mix_done"], 1)
            def block_sum(t, half):
                o = slice(512 * half, 512 * half + 512)
                v.wait_ge(s["wo_pe"], 2 * t + half + 1)
                v.tensor_tensor(xs[:, t, o], y_bank[2 * t + half][:, :], resid[:, t, o], ALU.add).then_inc(s["h_done"], 1)

            def unit(t):
                v.wait_ge(s["hsq_done"], 3 + t)
                link(v.reciprocal(st[:, 12 + t:13 + t], st[:, 10 + t:11 + t]))
                v.tensor_scalar(xs[:, t, :], xs[:, t, :], st[:, 12 + t:13 + t], None, ALU.mult).then_inc(s["xs_done"], 1)

            v.wait_ge(s["cb_in"], 32)
            block_sum(0, 0)
            block_sum(0, 1)
            unit(0)
            block_sum(1, 0)
            feature_major(hT, bank[2:6], gffn, 0, s["ht_pe"], s["ht_done"])
            block_sum(1, 1)
            unit(1)
            feature_major(hT, bank[2:6], gffn, 1, s["ht_pe"], s["ht_done"])
            v.wait_ge(s["lg_pe"], 2)
            v.wait_ge(s["route_in"], 32)
            link(v.tensor_tensor(lg, bank[2][:, 0:2 * E].rearrange("p (t e) -> p t e", t=NT),
                                 brt[:, :].unsqueeze(1).to_broadcast([P, NT, E]), ALU.add))
            for t in range(NT):
                link(v.max(mx8[:, t, :], lg[:, t, :]))
            v.tensor_scalar(st[:, 48:50], mx8[:, :, 0], -1.0, None, ALU.mult).then_inc(s["lg_done"], 1)
            for t in range(NT):
                link(v.max_index(idx8[:, t, :], mx8[:, t, :], lg[:, t, :]))
            link(v.tensor_copy(idxf, idx8[:, :, :]))
            iota = cb[:, C_IOTA32:C_IOTA32 + E]
            for t in range(NT):
                ins = v.tensor_tensor(onehot[:, t, :, :], iota.unsqueeze(1).to_broadcast([P, TOPK, E]),
                                      bc(idxf[:, t, 0:TOPK], E), ALU.is_equal)
            link(ins)
            for t in range(NT):
                ins = v.tensor_reduce(picked[:, t, :], onehot[:, t, :, :].rearrange("p j e -> p e j"), AX.X, ALU.add)
            ins.then_inc(s["pick_done"], 1)
            v.wait_ge(s["ex_done"], 2)
            link(v.reciprocal(st[:, 54:56], st[:, 50:52]))
            link(v.tensor_tensor(gt4, ex4, bc(st[:, 54:56], TOPK), ALU.mult))
            for t in range(NT):
                ins = v.tensor_tensor(onehot[:, t, :, :], onehot[:, t, :, :], bc(gt4[:, t, :], E), ALU.mult)
            link(ins)
            for t in range(NT):
                ins = v.tensor_reduce(gates[:, t, :], onehot[:, t, :, :].rearrange("p j e -> p e j"), AX.X, ALU.add)
            link(ins)
            v.wait_ge(s["rank_pe"], 1)
            v.wait_ge(s["pick_done"], 1)
            link(v.tensor_copy(cnt, bank[3][0:E, 64:65]))
            link(v.tensor_scalar(extra[:, 0:1], cnt, 1.0 * SLOTS, None, ALU.is_gt))
            link(v.scalar_tensor_tensor(out=extra[:, 1:2], in0=cnt, scalar=2.0 * SLOTS, in1=extra[:, 0:1], op0=ALU.is_gt, op1=ALU.add))
            v.scalar_tensor_tensor(out=extra[:, 2:3], in0=cnt, scalar=3.0 * SLOTS, in1=extra[:, 1:2], op0=ALU.is_gt,
                                   op1=ALU.add).then_inc(s["extra_done"], 1)
            link(v.scalar_tensor_tensor(out=slotv, in0=bank[3][:, 0:2 * E].rearrange("p (t e) -> p t e", t=NT), scalar=1.0,
                                        in1=picked, op0=ALU.add, op1=ALU.mult))
            v.tensor_scalar(slotv, slotv, -1.0, None, ALU.add).then_inc(s["slot_done"], 1)
            v.memset(back, 0.0)
            v.memset(colv, 0.0)
            v.memset(gcol, 0.0)
            v.tensor_copy(oh[:, 0:E], ident[0:E, 0:E])
            v.wait_ge(s["extra_done"], 1)
            v.wait_ge(s["start_pe"], 1)
            link(v.tensor_copy(startc, bank[4][0:E, 0:1]))
            link(v.tensor_scalar(dj, cb[0:E, C_J:C_J + EXTRA], startc, None, ALU.subtract))
            link(v.tensor_scalar(oh[:, E:ITEMS], dj, 0.0, None, ALU.is_ge))
            link(v.scalar_tensor_tensor(out=oh[:, E:ITEMS], in0=dj, scalar=extra[:, 2:3], in1=oh[:, E:ITEMS],
                                        op0=ALU.is_lt, op1=ALU.mult))
            link(v.tensor_scalar(dj, dj, 1.0, -1.0 * SLOTS, ALU.add, ALU.mult))
            link(v.tensor_tensor(back[:, E:ITEMS], dj, oh[:, E:ITEMS], ALU.mult))
            for part in range(3):
                ins = v.tensor_copy(oh3[E * part:E * part + E, 0:ITEMS], oh)
            ins.then_inc(s["oh_done"], 1)
            v.wait_ge(s["split_done"], 6)
            v.memset(m_os, 0.0).then_inc(s["os_done"], 1)
            v.memset(m_gt, 0.0).then_inc(s["gt_done"], 1)
            v.wait_ge(s["col_pe"], 1)
            v.tensor_copy(colv[:, :, 0:ITEMS], bank[2][:, 0:P].rearrange("p (t i) -> p t i", t=NT)[:, :, 0:ITEMS])
            v.tensor_copy(gcol[:, :, 0:ITEMS], bank[2][:, P:2 * P].rearrange("p (t i) -> p t i", t=NT)[:, :, 0:ITEMS])
            v.tensor_copy(rint[0:1, 0:ITEMS], bank[2][0:1, SEQ:SEQ + ITEMS])
            v.tensor_scalar(rint[0:1, ITEMS:ITEMS + 1], bank[4][0:1, 64:65], float(E), None, ALU.add).then_inc(s["items_done"], 1)
            v.wait_ge(s["items_done"], 1)
            n_items = v.value_load(rint[0:1, ITEMS:ITEMS + 1], min_val=E, max_val=ITEMS)

            iota2 = cb[:, C_IOTA2:C_IOTA2 + P]

            def one_hot(i):
                for t in range(NT):
                    ins = v.tensor_scalar(m_p[:, t, :], iota2[:, 0:SLOTS], colv[:, t, bass.ds(i, 1)], None, ALU.is_equal)
                ins.then_inc(s["p_ready"], 1)

            def gate_matrix(i):
                for t in range(NT):
                    ins = v.tensor_scalar(m_g2[:, t, :], iota2, colv[:, t, bass.ds(i, 1)], gcol[:, t, bass.ds(i, 1)],
                                          ALU.is_equal, ALU.mult)
                ins.then_inc(s["g2_ready"], 1)

            def select(i):
                v.tensor_copy(m_sel[0:3 * E, :], oh3[0:3 * E, bass.ds(i, 1)].to_broadcast([3 * E, SLOTS])).then_inc(s["sel_ready"], 1)

            def gathered():
                v.tensor_tensor(m_xg.rearrange("p (k c) -> p k c", k=KT), b_x[:, :].rearrange("p (k c) -> p k c", k=KT),
                                bc(gffn[:, :], SLOTS), ALU.mult).then_inc(s["xg_ready"], 1)

            one_hot(0)
            gate_matrix(0)
            select(0)
            v.wait_ge(s["ga_pe"], 1)
            gathered()
            one_hot(1)
            with v.Fori(0, n_items) as i:
                v.wait_ge(s["gu_pe"], i + 1)
                v.tensor_scalar(m_g, b_g[:, :], LIMIT, None, ALU.min).then_inc(s["gm_done"], 1)
                v.tensor_scalar(m_u, b_u[:, :], LIMIT, -LIMIT, ALU.min, ALU.max).then_inc(s["um_done"], 1)
                v.wait_ge(s["gm_done"], i + 1)
                v.wait_ge(s["um_done"], i + 1)
                v.scalar_tensor_tensor(out=m_t, in0=m_u, scalar=1.0, in1=m_g, op0=ALU.add, op1=ALU.mult).then_inc(s["t_done"], 1)
                v.wait_ge(s["t_done"], i + 1)
                v.wait_ge(s["sg_done"], i + 1)
                v.tensor_tensor(m_a, m_t, m_s, ALU.mult).then_inc(s["act_done"], 1)
                v.wait_ge(s["ga_pe"], i + 2)
                gathered()
                one_hot(i + 2)
                v.wait_ge(s["gtt_pe"], i + 1)
                gate_matrix(i + 1)
                v.wait_ge(s["dn_pe"], i + 1)
                select(i + 1)
            v.wait_ge(s["scf_pe"], 1)
            for n in range(4):
                o = slice(512 * (n % 2), 512 * (n % 2) + 512)
                v.tensor_tensor(yout[:, n // 2, o], y_bank[n][:, :], resid[:, n // 2, o], ALU.add).then_inc(s["yfin_done"], 1)
            v.wait_ge(s["gfin_in"], 16)
            for t in range(NT):
                v.wait_ge(s["fsq_done"], 2 * t + 2)
                link(v.reciprocal(st[:, 64 + t:65 + t], st[:, 58 + t:59 + t]))
                v.scalar_tensor_tensor(out=yout[:, t, :], in0=yout[:, t, :], scalar=st[:, 64 + t:65 + t],
                                       in1=gfin, op0=ALU.mult, op1=ALU.mult).then_inc(s["fin_done"], 1)


_INS = ["x", "norm_mix_g", "w_in", "shift_mu", "decay_w0", "w_decay_up", "iclr_a0", "w_iclr_up", "w_gate_lr_up", "k_k", "k_a",
        "r_k", "gn_w", "gn_b", "w_out", "norm_ffn_g", "w_router", "b_router", "w_gate_up", "b_gate_up", "w_down", "b_down",
        "norm_final_g"]


def kernel(**inputs):
    import concourse.bacc as _bacc
    from concourse.bass_utils import run_bass_kernel_spmd as _run

    nc = _bacc.Bacc("TRN2", target_bir_lowering=False, num_devices=1)
    arrays, args = {}, []
    named = [(n, np.ascontiguousarray(inputs[n])) for n in _INS]
    named += list(zip(("const_a", "const_bias", "const_b"), shape_constants()))
    for name, a in named:
        arrays[f"in_{name}"] = a
        args.append(nc.dram_tensor(f"in_{name}", a.shape, mybir.dt.from_np(a.dtype), kind="ExternalInput").ap())
    args.append(nc.dram_tensor("out_0", (1, SEQ, D), F32, kind="ExternalOutput").ap())
    program(nc, *args)
    r = _run(nc, [arrays], core_ids=[0])
    return r.results[0]["out_0"]
```

```python
from contextlib import ExitStack

import numpy as np
import concourse.bass as bass
from concourse import mybir

F32 = mybir.dt.float32
BF16 = mybir.dt.bfloat16
I32 = mybir.dt.int32
U32 = mybir.dt.uint32
ALU = mybir.AluOpType
ACT = mybir.ActivationFunctionType
AX = mybir.AxisListType

P = 128
D = 1024
SEQ = 256
NT = SEQ // P
KT = D // P
AW = 512
RW = 512
HD = 64
H = 8
FT = RW // P
LORA = 256
IN_W = 3 * AW + 3 * RW + LORA
CH = 64
NCH = SEQ // CH
LEVELS = 6
E = 32
TOPK = 4
FF = 1024
SLOTS = 64
EXTRA = 16
ITEMS = E + EXTRA
CHUNK = 4096
HALF = CHUNK // 2
RING = 6
LIMIT = 7.0
ALPHA = 1.702
RMS_EPS = 1e-5
GN_EPS = 64e-5
DECAY_C = float(np.exp(-0.5))
NV = 14 + 7 * FT
PATTERNS = ((128, 1), (512, 4), (2048, 16))

C_IDENT, C_ONES, C_MEAN, C_SCAN = 0, 128, 256, 384
C_EYE2 = 640
C_MASK4 = 704
C_LEVEL = C_MASK4 + 4 * CH
C_A = C_LEVEL + LEVELS * CH
C_IOTA2, C_TRI, C_ONE, C_IOTA32, C_ECOL, C_J = 0, 128, 256, 384, 416, 417
C_B = 440


def shape_constants():
    a = np.zeros((P, C_A), np.float32)
    t = np.arange(P)
    a[:, C_IDENT:C_IDENT + P] = np.eye(P)
    a[:, C_ONES:C_ONES + P] = (t[:, None] // HD) == (t[None, :] // HD)
    a[:, C_MEAN:C_MEAN + P] = a[:, C_ONES:C_ONES + P] / HD
    a[:, C_SCAN:C_SCAN + SEQ] = (np.arange(SEQ) % CH) != 0
    a[:, C_EYE2:C_EYE2 + HD] = np.tile(np.eye(HD), (2, 1))

    c = np.arange(CH)

    def level(n):
        return ((c[:, None] >> n) == (c[None, :] >> n)) & (((c[:, None] >> (n - 1)) & 1) == 1) & (((c[None, :] >> (n - 1)) & 1) == 0)

    masks = [level(1).T, c[:, None] <= c[None, :], c[:, None] < c[None, :], c[:, None] <= c[None, :]]
    masks += [level(n + 1) for n in range(LEVELS)]
    for n, m in enumerate(masks):
        a[:, C_MASK4 + n * CH:C_MASK4 + (n + 1) * CH] = np.tile(m, (2, 1))

    dist = P + t[:, None] - np.arange(SEQ)[None, :]
    times = np.zeros(dist.shape, np.float64)
    for window, dil in PATTERNS:
        times += (dist >= 0) & (dist <= window) & (dist % dil == 0)
    bias = np.empty((P, H, SEQ), np.float32)
    for h in range(H):
        slope = 2.0 ** (-8.0 / H * (h + 1))
        bias[:, h] = np.where(times > 0, -slope * dist + np.log(np.maximum(times, 1)), -1e30)

    b = np.zeros((P, C_B), np.float32)
    b[:, C_IOTA2:C_IOTA2 + P] = np.tile(np.arange(SLOTS), 2)
    b[:, C_TRI:C_TRI + P] = t[:, None] < t[None, :]
    b[:, C_ONE:C_ONE + P] = 1.0
    b[:, C_IOTA32:C_IOTA32 + E] = np.arange(E)
    b[:, C_ECOL] = t
    b[:, C_J:C_J + EXTRA] = np.arange(EXTRA)
    return a, bias.reshape(P, H * SEQ), b


def program(nc, x, g_mix, w_in, mu, w0, w_dec, a0, w_icl, w_gat, k_k, k_a, r_k, gn_w, gn_b, w_out, g_ffn, w_router,
            b_router, w_gu, b_gu, w_dn, b_dn, g_fin, const_a, const_bias, const_b, out):
    with ExitStack() as ctx:
        def sb(name, shape, dt=F32):
            return ctx.enter_context(nc.sbuf_tensor(name, shape, dt))

        def sem(name):
            return ctx.enter_context(nc.semaphore(name))

        ring = sb("ring", [P, RING, CHUNK])
        resid = sb("resid", [P, NT, D])
        arena = sb("arena", [P, 12, 1024])
        attn = sb("attn", [P, 3, 1024])
        stage = sb("stage", [P, 4, 1024])
        zpad = sb("zpad", [P, 2, 2, SEQ + 1])
        lora = sb("lora", [P, 2, SEQ])
        mixT = sb("mixT", [P, KT, SEQ])
        ca = sb("ca", [P, C_A])
        cb = sb("cb", [P, C_B])
        vrow = sb("vrow", [NV, P])
        vcol = sb("vcol", [P, NV])
        gmix = sb("gmix", [P, KT])
        gffn = sb("gffn", [P, KT])
        st = sb("st", [P, 96])
        wrt = sb("wrt", [P, KT, E])
        brt = sb("brt", [P, E])

        bank = [ctx.enter_context(nc.psum_tensor(f"bank{i}", [P, 512], F32)) for i in range(8)]

        y_bank = [bank[i] for i in (6, 7, 0, 1)]
        b_g, b_u, b_x, b_d = bank[2:6]
        level_bank = [[bank[i] for i in b] for b in ((0, 1), (4, 5))]

        ident = ca[:, C_IDENT:C_IDENT + P]
        head_ones = ca[:, C_ONES:C_ONES + P]
        head_mean = ca[:, C_MEAN:C_MEAN + P]
        scan_keep = ca[:, C_SCAN:C_SCAN + SEQ]
        eye2 = ca[:, C_EYE2:C_EYE2 + HD]
        mask4 = ca[:, C_MASK4:C_MASK4 + 4 * CH]

        def level_mask(n):
            return ca[:, C_LEVEL + (n - 1) * CH:C_LEVEL + n * CH].unsqueeze(1).to_broadcast([P, H, CH])

        def blk(i, n=1):
            return arena[:, i:i + n, :].rearrange("p b c -> p (b c)")

        def tiles(ap):
            return ap.rearrange("p (f t) -> p f t", t=SEQ)

        B_R, B_S, B_I, B_X, B_KK, B_G, B_C, B_AR, B_A, B_K, B_V = 0, 1, 2, 3, 4, 5, 6, 7, 9, 10, 11
        rT, kT, vT = blk(B_R), blk(B_K), blk(B_V)
        sw = blk(B_S)
        cum = blk(B_C)
        pinv = blk(B_I)
        tmp = blk(B_X)
        kkT = blk(B_KK)
        gT = blk(B_G)
        aT = blk(B_A)
        ar = blk(B_AR, 2).rearrange("p (f w t) -> p f w t", w=2, t=SEQ)
        xn = arena[:, B_R:B_R + 2, :]
        xT = stage[:, 0:2, :].rearrange("p b c -> p (b c)").rearrange("p (k t) -> p k t", t=SEQ)
        wlo = stage[:, 2:4, :].rearrange("p b c -> p (b c)").rearrange("p (k n) -> p k n", n=LORA)
        qA, kA = tiles(attn[:, 0, :]), tiles(attn[:, 1, :])
        vA = attn[:, 2, :].rearrange("p (t n) -> p t n", n=AW)

        slot = [ring[:, i, :].rearrange("p (k n) -> p k n", k=KT) for i in range(RING)]
        work = ring[:, 2:4, :].rearrange("p b c -> p (b c)")
        amv = work[:, 0:2048].rearrange("p (t h w j) -> p t h w j", t=NT, h=H, w=2)
        btok = work[:, 2048:3072].rearrange("p (t n) -> p t n", t=NT)
        ktok = work[:, 3072:4096].rearrange("p (t n) -> p t n", t=NT)
        vtok = work[:, 4096:6144].rearrange("p (t c n) -> p t c n", t=NT, c=2)
        uu = [work[:, 6144 + 512 * g:6656 + 512 * g].rearrange("p (h s) -> p h s", h=H) for g in range(NT)]
        low = [work[:, 7168 + 512 * g:7680 + 512 * g].rearrange("p (h s) -> p h s", h=H) for g in range(NT)]
        apart = ring[:, 0:2, :].rearrange("p b c -> p (b c)")
        heads_apart = apart[:, 0:4096].rearrange("p (j a f t) -> p j a f t", j=2, a=2, f=FT)
        nzw = [apart[:, 0:4096].rearrange("p (c t h s) -> p t c h s", c=2, t=NT, h=H)[:, g] for g in range(NT)]
        lml = [apart[:, 4096 + 1024 * g:5120 + 1024 * g].rearrange("p (h c s) -> p h c s", h=H, c=2) for g in range(NT)]
        xx = [apart[:, 6144 + 1024 * g:7168 + 1024 * g].rearrange("p (h c s) -> p h c s", h=H, c=2) for g in range(NT)]
        abias = blk(B_R, 2).rearrange("p (h s) -> p h s", h=H)
        mflat = mixT[:, :, :].rearrange("p k t -> p (k t)")
        wlor_d = mflat[:, 0:RW]
        wgt = mflat[:, RW:2 * RW]
        wo = ring[:, 4:6, :].rearrange("p b c -> p (b c)").rearrange("p (m n) -> p m n", m=KT)

        sflat = stage[:, :, :].rearrange("p b c -> p (b c)")
        sc_s = [sflat[:, 384 * i:384 * i + 384] for i in range(2)]
        sc_e = [sflat[:, 768 + 384 * i:1152 + 384 * i] for i in range(2)]
        sc_t = [sflat[:, 1536 + 384 * i:1920 + 384 * i] for i in range(2)]
        nm = [sflat[:, 2048 * g:2048 * g + 2048].rearrange("p (h w s) -> p h w s", h=H, w=4) for g in range(NT)]
        t1s = [attn[:, 0, 512 * g:512 * g + 512].rearrange("p (h s) -> p h s", h=H) for g in range(NT)]
        gg = tiles(blk(B_X))
        yT = tiles(zpad[:, :, :, :].rearrange("p a b c -> p (a b c)")[:, 0:1024])
        tt = attn[:, 1, :].rearrange("p (c f j) -> p c f j", c=NCH, f=FT)
        state = attn[:, 2, :].rearrange("p (c f i) -> p c f i", c=NCH, f=FT)
        stmp = blk(B_R)[:, 0:FT * HD].rearrange("p (f i) -> p f i", f=FT)
        yc = blk(B_S)
        ysq = blk(B_R)

        hidden = arena[:, B_AR:B_AR + 2, :]
        xs = arena[:, B_R:B_R + 2, :]
        xsplit = attn[:, :, :].rearrange("p b c -> p (b c)").bitcast(BF16).rearrange("p (t s n) -> p t s n", t=NT, s=3)
        hT = stage[:, 0:2, :].rearrange("p b c -> p (b c)").rearrange("p (k t) -> p k t", t=SEQ)
        gfin = stage[:, 2, :]
        xrem = arena[:, B_X:B_X + 2, :]
        yout = arena[:, B_R:B_R + 2, :]
        QB = 3 * D // 4
        braw = mflat[:, 2 * RW:2 * RW + QB]
        bpart = [sflat[:, o:o + QB // 2].bitcast(BF16) for o in (3072, 3072 + QB // 2, 2304)]
        bsp = blk(B_K, 2).bitcast(BF16)[:, 0:4 * QB].rearrange("p (q n) -> p q n", q=4)
        mz = blk(B_I, 5)
        m_g, m_u, m_t, m_s, m_a, m_at, m_os, m_xg = (mz[:, 512 * i:512 * i + 512] for i in range(8))
        m_gt, m_g2 = mz[:, 4096:4352], mz[:, 4352:4608].rearrange("p (t c) -> p t c", t=NT)
        m_p = mz[:, 4608:4672].bitcast(BF16).rearrange("p (t c) -> p t c", t=NT)
        m_sel = mz[:, 4672:4704].bitcast(BF16)
        rs = stage[:, 3, :]
        rint = sb("rint", [P, 80], I32)
        idx8 = sb("idx8", [P, NT, 8], U32)
        lg = rs[:, 0:64].rearrange("p (t e) -> p t e", t=NT)
        mx8 = rs[:, 64:80].rearrange("p (t e) -> p t e", t=NT)
        idxf = rs[:, 80:96].rearrange("p (t e) -> p t e", t=NT)
        ex4 = rs[:, 96:104].rearrange("p (t e) -> p t e", t=NT)
        gt4 = rs[:, 104:112].rearrange("p (t e) -> p t e", t=NT)
        onehot = rs[:, 112:368].rearrange("p (t j e) -> p t j e", t=NT, j=TOPK)
        picked = rs[:, 368:432].rearrange("p (t e) -> p t e", t=NT)
        gates = rs[:, 432:496].rearrange("p (t e) -> p t e", t=NT)
        slotv = rs[:, 496:560].rearrange("p (t e) -> p t e", t=NT)
        extra = rs[0:E, 560:563]
        cnt = rs[0:E, 563:564]
        startc = rs[0:E, 564:565]
        dj = rs[0:E, 566:566 + EXTRA]
        oh = rs[0:E, 584:584 + ITEMS]
        back = rs[0:E, 632:632 + ITEMS]
        colv = rs[:, 680:680 + 2 * (ITEMS + 2)].rearrange("p (t i) -> p t i", t=NT)
        gcol = rs[:, 780:780 + 2 * (ITEMS + 2)].rearrange("p (t i) -> p t i", t=NT)
        oh3 = sb("oh3", [P, ITEMS + 2], BF16)
        svT = mz[0:E, 512:1024].rearrange("p (w t) -> p w t", w=2)

        names = ("id_in gm_in ca_in vec_in wlo_in up_in bias_in cb_in wo_in braw_in route_in gfin_in out_done "
                 "v_chain a_chain p_chain xn_done xt_pe xt_done vt_pe vt_done proj_pe zcopy zshift zpad0 tanh_done sgd_done "
                 "dec_pe icl_pe gat_pe sdec_done sicl_done gat_done exps_done sq_done ss_pe nrm_done bprod_done bsum_pe "
                 "bonus_done tilde_done tok_pe tok_done s_pe s_max e_done en_done et_pe et_done pv_pe attn_done "
                 "gram_pe nm_done low_done ux_done lml_done t1_pe t1_done d_pe mv_pe mv_done zw_pe zw_done gc_pe gc_done qu_pe qu_done "
                 "st_pe st_done yp_pe y_done mu_pe yc_done ysq_done var_pe sd_done mix_done wo_pe h_done "
                 "xs_done ht_pe ht_done lg_pe lg_done ex_done pick_done rank_pe slot_done extra_done start_pe oh_done svt_pe "
                 "svt_done col_pe items_done count_done split_done bsplit_done bsp_in zero_done apart_done rem0_done rem1_done hsq_done "
                 "p_ready ga_pe xg_ready sel_ready gu_pe gm_done sg_done act_done tr_pe at_done g2_ready gtt_pe gt_done dn_pe os_done "
                 "scf_pe fsq_done fsum_done frt_done fin_done yfin_done um_done t_done").split()
        s = {n: sem(n) for n in names}
        s_x = [sem(f"x_in{t}") for t in range(NT)]
        s_win = [sem(f"win_in{i}") for i in range(RING)]
        s_ring = [[sem(f"ring_in{i}{u}") for u in "ab"] for i in range(RING)]
        s_free = sem("ring_free")

        block = ctx.enter_context(nc.Block())

        VL = dict(mu=0, w0=14, a0=18, kk=22, ka=26, rk=30, gw=34, gb=38)

        def vec(name, f):
            c = VL[name] + f
            return vcol[:, c:c + 1]

        def expert_views(gu, dn):
            gu = gu.rearrange("e (p c u) n -> c u p (e n)", c=4, u=2)
            dn = dn.rearrange("e (h p u t) n -> h u p (e t n)", h=2, u=2, t=2)
            return [[gu[c, u] for u in range(2)] for c in range(4)] + [[dn[h, u] for u in range(2)] for h in range(2)]

        @block.sync
        def _(sp):
            for t in range(NT):
                sp.dma_start(resid[:, t, :], x[0, P * t:P * t + P, :]).then_inc(s_x[t], 16)
            sp.dma_start(ca[:, 0:P], const_a[:, 0:P]).then_inc(s["id_in"], 16)
            sp.dma_start(gmix[:, :], g_mix[0].rearrange("(p k) -> p k", k=KT)).then_inc(s["gm_in"], 16)
            sp.dma_start(wlo, w_in[0].rearrange("(p k) n -> p k n", k=KT)[:, :, 3 * AW + 3 * RW:IN_W]).then_inc(s["wlo_in"], 16)
            rows = [(mu[0], 14), (w0[0], FT), (a0[0], FT), (k_k[0], FT), (k_a[0], FT),
                    (r_k[0].rearrange("h j -> (h j)"), FT), (gn_w[0], FT), (gn_b[0], FT)]
            at = 0
            for src, n in rows:
                sp.dma_start(vrow[at:at + n, :], src.rearrange("(r c) -> r c", c=P)).then_inc(s["vec_in"], 16)
                at += n
            sp.dma_start(ca[:, P:C_A], const_a[:, P:C_A]).then_inc(s["ca_in"], 16)
            order = [3, 4, 5, 0, 1, 2]
            for c in range(RING):
                cols = slice(AW * order[c], AW * order[c] + AW)
                sp.dma_start(slot[c], w_in[0].rearrange("(p k) n -> p k n", k=KT)[:, :, cols]).then_inc(s_win[c], 16)
                if c == 0:
                    sp.dma_start(wlor_d[0:64, :], w_dec[0]).then_inc(s["up_in"], 16)
                    sp.dma_start(wlor_d[64:128, :], w_icl[0]).then_inc(s["up_in"], 16)
                    sp.dma_start(wgt[:, :], w_gat[0]).then_inc(s["up_in"], 16)
            sp.dma_start(cb[:, :], const_b).then_inc(s["cb_in"], 16)
            sp.dma_start(gffn[:, :], g_ffn[0].rearrange("(p k) -> p k", k=KT)).then_inc(s["cb_in"], 16)
            sp.dma_start(wrt[:, :, :], w_router[0].rearrange("(p k) e -> p k e", k=KT)).then_inc(s["route_in"], 16)
            sp.dma_start(brt[:, :], b_router[0:1, :].to_broadcast([P, E])).then_inc(s["route_in"], 16)
            for q in range(4):
                sp.dma_start(braw[E * q:E * q + E, 0:512], b_gu[0][:, 512 * q:512 * q + 512]).then_inc(s["braw_in"], 16)
                sp.dma_start(braw[E * q:E * q + E, 512:QB], b_dn[0][:, 256 * q:256 * q + 256]).then_inc(s["braw_in"], 16)
            sp.wait_ge(s["tilde_done"], 4)
            sp.dma_start(abias, const_bias.rearrange("p (h s) -> p h s", h=H)).then_inc(s["bias_in"], 16)
            sp.wait_ge(s["proj_pe"], 13)
            sp.dma_start(wo, w_out[0].rearrange("(m p) n -> p m n", p=P)).then_inc(s["wo_in"], 16)
            sp.wait_ge(s["bsplit_done"], 1)
            sp.wait_ge(s["tok_pe"], 8)
            sp.wait_ge(s["apart_done"], 4)
            sp.wait_ge(s["bonus_done"], 1)
            for part in range(3):
                for q in range(4):
                    sp.dma_start(bsp[E * part:E * part + E, q, :], bpart[part][E * q:E * q + E, :]).then_inc(s["bsp_in"], 16)
            sp.wait_ge(s["zw_pe"], 2)
            first = expert_views(w_gu[0, 0:1], w_dn[0, 0:1])

            def load(views, c):
                for u in range(2):
                    sp.dma_start(ring[:, c, HALF * u:HALF * u + HALF], views[c][u]).then_inc(s_ring[c][u], 16)

            load(first, 1)
            sp.wait_ge(s["qu_done"], 2)
            for c in (0, 2, 3):
                load(first, c)
            sp.dma_start(gfin, g_fin.unsqueeze(0).to_broadcast([P, D])).then_inc(s["gfin_in"], 16)
            sp.wait_ge(s["wo_pe"], 4)
            for c in (4, 5):
                load(first, c)
            sp.wait_ge(s["items_done"], 1)
            n_items = sp.value_load(rint[0:1, ITEMS:ITEMS + 1], min_val=E, max_val=ITEMS)
            with sp.Fori(1, n_items) as i:
                e = sp.value_load(rint[0:1, bass.ds(i, 1)], min_val=0, max_val=E - 1)
                views = expert_views(w_gu[0, bass.ds(e, 1)], w_dn[0, bass.ds(e, 1)])
                for c in range(RING):
                    for u in range(2):
                        sp.wait_ge(s_free, 12 * i + (2 * c + u - 11))
                        sp.dma_start(ring[:, c, HALF * u:HALF * u + HALF], views[c][u]).then_inc(s_ring[c][u], 16)
            for n in range(4):
                t, o = n // 2, slice(512 * (n % 2), 512 * (n % 2) + 512)
                sp.wait_ge(s["fin_done"], n + 1)
                sp.dma_start(out[0, P * t:P * t + P, o], yout[:, t, o]).then_inc(s["out_done"], 16)
            sp.wait_ge(s["out_done"], 16 * 4)

        @block.tensor
        def _(pe):
            def mm(o, l, r, start=True, stop=True):
                return pe.matmul(o, l, r, start=start, stop=stop, skip_group_check=True)

            def model_transposes(src, to, t, done):
                v = src[:, t, :].rearrange("p (q k) -> p k q", k=KT)
                for u in range(2):
                    for k in range(4):
                        m = pe.transpose(to[2 * t + u][:, P * k:P * k + P], v[:, 4 * u + k, :], ident)
                    m.then_inc(done, 1)

            pe.wait_ge(s["id_in"], 16)
            for t in range(NT):
                pe.wait_ge(s["xn_done"], t + 1)
                model_transposes(xn, bank[4:8], t, s["xt_pe"])
            pe.wait_ge(s["vec_in"], 16 * 8)
            pe.transpose(bank[3][:, 0:NV], vrow[:, :], ident[0:NV, 0:NV]).then_inc(s["vt_pe"], 1)
            pe.wait_ge(s["xt_done"], 4)
            pe.wait_ge(s["vt_done"], 1)

            def project(u):
                if u >= 4:
                    pe.wait_ge(s["zcopy"], u - 3)
                if u == 0:
                    pe.wait_ge(s["wlo_in"], 16)
                else:
                    pe.wait_ge(s_win[(u - 1) // 2], 16)
                b = bank[u % 4]
                if u >= 11:
                    t = u - 11
                    for k in range(KT):
                        m = mm(b[:, :], xT[:, k, P * t:P * t + P], slot[5][:, k, :], k == 0, k == KT - 1)
                else:
                    w, c0 = (wlo, 0) if u == 0 else (slot[(u - 1) // 2], 2 * P * ((u - 1) % 2))
                    for j in range(2):
                        for k in range(KT):
                            m = mm(b[:, SEQ * j:SEQ * j + SEQ], w[:, k, c0 + P * j:c0 + P * j + P], xT[:, k, :],
                                   k == 0, k == KT - 1)
                m.then_inc(s["proj_pe"], 1)

            project(0)
            project(1)
            project(2)
            pe.wait_ge(s["up_in"], 48)
            pe.wait_ge(s["tanh_done"], 1)
            for f in range(FT):
                m = mm(bank[4 + f // 2][:, SEQ * (f % 2):SEQ * (f % 2) + SEQ], wlor_d[0:64, P * f:P * f + P], lora[0:64, 0, :])
                if f % 2:
                    m.then_inc(s["dec_pe"], 1)
            for f in range(FT):
                m = mm(bank[6 + f // 2][:, SEQ * (f % 2):SEQ * (f % 2) + SEQ], wlor_d[64:128, P * f:P * f + P], lora[64:128, 0, :])
                if f % 2:
                    m.then_inc(s["icl_pe"], 1)
            project(3)
            pe.wait_ge(s["sgd_done"], 1)
            pe.wait_ge(s["sdec_done"], FT)
            for f in range(FT):
                m = mm(bank[4 + f // 2][:, SEQ * (f % 2):SEQ * (f % 2) + SEQ], wgt[:, P * f:P * f + P], lora[:, 1, :])
                if f % 2:
                    m.then_inc(s["gat_pe"], 1)
            for u in range(4, 7):
                project(u)
            pe.wait_ge(s["ca_in"], 16)
            pe.wait_ge(s["sq_done"], 1)
            pe.wait_ge(s["sicl_done"], FT)
            for j in range(2):
                mm(bank[6 + j][:, :], head_ones, tmp[:, 512 * j:512 * j + 512]).then_inc(s["ss_pe"], 1)
            for u in range(7, 13):
                project(u)
            pe.wait_ge(s["bprod_done"], 1)
            pe.wait_ge(s["gat_done"], 2)
            for j in range(2):
                mm(bank[4 + j][:, :], head_ones, tmp[:, 512 * j:512 * j + 512]).then_inc(s["bsum_pe"], 1)

            def scores(f):
                b = [bank[6 - 2 * (f % 2) + hh] for hh in range(2)]
                if f >= 2:
                    pe.wait_ge(s["s_max"], f - 1)
                for c0, q, n in ((0, slice(0, P), P), (P, slice(P, SEQ), SEQ)):
                    for hh in range(2):
                        r = slice(HD * hh, HD * hh + HD)
                        m = mm(b[hh][:, c0:c0 + n], qA[r, f, q], kA[r, f, 0:n])
                m.then_inc(s["s_pe"], 1)

            def token_major(n):
                arr, t = n // 2, n % 2
                if n >= 4:
                    pe.wait_ge(s["tok_done"], n - 3)
                for f in range(FT):
                    src = (tiles(vT)[:, f, :], ar[:, f, 0, :], tiles(aT)[:, f, :], tiles(kT)[:, f, :])[arr]
                    m = pe.transpose(bank[n % 4][:, P * f:P * f + P], src[:, P * t:P * t + P], ident)
                m.then_inc(s["tok_pe"], 1)

            pe.wait_ge(s["zcopy"], 13)
            pe.wait_ge(s["nrm_done"], 2)
            scores(0)
            pe.wait_ge(s["tilde_done"], 4)
            for n in range(4):
                token_major(n)
            pe.wait_ge(s["bonus_done"], 1)
            scores(1)
            for n in range(4, 8):
                token_major(n)

            def turn(f):
                for hh in range(2):
                    h = 2 * f + hh
                    pe.wait_ge(s["en_done"], h + 1)
                    if f >= 1:
                        pe.wait_ge(s["et_done"], h - 1)
                    for n in range(3):
                        m = pe.transpose(bank[hh][:, P * n:P * n + P], sc_e[h % 2][:, P * n:P * n + P], ident)
                    m.then_inc(s["et_pe"], 1)

            def values(f):
                pe.wait_ge(s["tok_done"], 8)
                pe.wait_ge(s["et_done"], 2 * f + 2)
                if f >= 2:
                    pe.wait_ge(s["attn_done"], f - 1)
                for t in range(NT):
                    for hh in range(2):
                        h = 2 * f + hh
                        c0 = P * t
                        m = mm(bank[2 + f % 2][HD * hh:HD * hh + HD, c0:SEQ], vA[:, t, HD * h:HD * h + HD],
                               sc_t[h % 2][:, 2 * P * t:SEQ + P * t], t == 0, t == 1)
                m.then_inc(s["pv_pe"], 1)

            pe.wait_ge(s["tok_done"], 6)
            for f in range(FT):
                turn(f)
                if f + 2 < FT:
                    scores(f + 2)
                values(f)

            pe.wait_ge(s["attn_done"], FT)
            pe.wait_ge(s["et_done"], H)
            chunk_rows = [slice(CH * c, CH * c + CH) for c in range(2)]
            head_rows = [slice(HD * j, HD * j + HD) for j in range(2)]
            pe.wait_ge(s["apart_done"], 4)

            def project_out(n, ks):
                t, half = n // 2, n % 2
                for k in ks:
                    m = mm(y_bank[n][:, :], mixT[:, k, P * t:P * t + P], wo[:, k, 512 * half:512 * half + 512], k == 0, k == KT - 1)
                return m

            for t in range(NT):
                for k in range(2):
                    if t:
                        pe.wait_ge(s["nm_done"], 2 * k + 2)
                    for f in (2 * k, 2 * k + 1):
                        ts = [slice(P * t + CH * c, P * t + CH * c + CH) for c in range(2)]
                        for a in range(2):
                            o = 4 * CH * (f % 2) + 2 * CH * a
                            for j in range(2):
                                for c, cr in enumerate(chunk_rows):
                                    mm(bank[2 * k + j][cr, o:o + 2 * CH], heads_apart[:, j, a, f, ts[c]], ar[:, f, :, ts[c]])
                        for c, cr in enumerate(chunk_rows):
                            m = mm(bank[4 + t][cr, P * f:P * f + P], ar[:, f, 0, ts[c]], heads_apart[:, :, 0, f, ts[c]])
                    m.then_inc(s["gram_pe"], 1)
            pe.wait_ge(s["wo_in"], 16)
            project_out(0, range(FT))
            for lv in range(2, LEVELS + 1):
                for t in range(NT):
                    pe.wait_ge(s["lml_done"], 2 * (lv - 2) + t + 1)
                    pe.wait_ge(s["nm_done"], 8)
                    pe.wait_ge(s["ux_done"], 2 * t + 2 if lv == 2 else 4 * (lv - 2) + 2 * t + 2)
                    for h in range(H):
                        for c, cr in enumerate(chunk_rows):
                            m = mm(bank[2 + t][cr, CH * h:CH * h + CH], lml[t][:, h, c, :], uu[t][:, h, :])
                    m.then_inc(s["t1_pe"], 1)
                if lv - 2 < FT:
                    project_out(1, [lv - 2])
                for t in range(NT):
                    pe.wait_ge(s["t1_done"], 2 * (lv - 2) + t + 1)
                    pe.wait_ge(s["low_done"], 2)
                    for h in range(H):
                        b, c0 = level_bank[t][h // 4], 2 * CH * (h % 4)
                        for c, cr in enumerate(chunk_rows):
                            m = mm(b[cr, c0:c0 + CH], xx[t][:, h, c, :], t1s[t][:, h, :])
                        if lv < LEVELS:
                            for c, cr in enumerate(chunk_rows):
                                m = mm(b[cr, c0 + CH:c0 + 2 * CH], t1s[t][:, h, :], xx[t][:, h, c, :])
                        if h % 4 == 3:
                            m.then_inc(s["d_pe"], 1)
            for t in range(NT):
                for h in range(H):
                    for c, cr in enumerate(chunk_rows):
                        m = mm(bank[2 + t][cr, HD * h:HD * h + HD], nm[t][:, h, 2, :], vtok[:, t, c, HD * h:HD * h + HD])
                m.then_inc(s["mv_pe"], 1)
            for t in range(NT):
                pe.wait_ge(s["mv_done"], t + 1)
                pe.wait_ge(s["ux_done"], 22 + 2 * t)
                for h in range(H):
                    for c, cr in enumerate(chunk_rows):
                        m = mm(level_bank[t][h // 4][cr, P * (h % 4):P * (h % 4) + P], xx[t][:, h, c, :], amv[:, t, h, :, :])
                m.then_inc(s["zw_pe"], 1)
            for t in range(NT):
                pe.wait_ge(s["zw_done"], 4 * t + 4)
                pe.wait_ge(s["mv_done"], 2)
                for c in range(2):
                    b = level_bank[t][c]
                    for f in range(FT):
                        for j, hr in enumerate(head_rows):
                            mm(b[hr, CH * f:CH * f + CH], nzw[t][:, c, 2 * f + j, 0:HD], nm[t][:, 2 * f + j, 1, :])
                        for j, hr in enumerate(head_rows):
                            h = 2 * f + j
                            mm(b[hr, SEQ + CH * f:SEQ + CH * f + CH], vtok[:, t, c, HD * h:HD * h + HD], nm[t][:, h, 3, :], True, False)
                        for j, hr in enumerate(head_rows):
                            m = mm(b[hr, SEQ + CH * f:SEQ + CH * f + CH], nzw[t][:, c, 2 * f + j, HD:2 * HD], nm[t][:, 2 * f + j, 1, :], False, True)
                m.then_inc(s["gc_pe"], 1)
                if t:
                    pe.wait_ge(s["qu_done"], t)
                for c in range(2):
                    b = bank[2 + c]
                    if 2 * t + c == NCH - 1:
                        break
                    for f in range(FT):
                        hs = [(hr, 2 * f + j, slice(HD * (2 * f + j), HD * (2 * f + j) + HD)) for j, hr in enumerate(head_rows)]
                        if 2 * t + c:
                            for hr, h, hc in hs:
                                mm(b[hr, HD * f:HD * f + HD], nzw[t][:, c, h, 0:HD], btok[:, t, hc])
                        for hr, h, hc in hs:
                            mm(b[hr, SEQ + HD * f:SEQ + HD * f + HD], ktok[:, t, hc], vtok[:, t, c, hc], True, False)
                        for hr, h, hc in hs:
                            m = mm(b[hr, SEQ + HD * f:SEQ + HD * f + HD], btok[:, t, hc], nzw[t][:, c, h, HD:2 * HD], False, True)
                m.then_inc(s["qu_pe"], 1)
            for cc in range(1, NCH):
                pe.wait_ge(s["qu_done"], cc // 2 + 1)
                pe.wait_ge(s["gc_done"], 2)
                if cc >= 2:
                    project_out(2, [cc - 2])
                    pe.wait_ge(s["st_done"], cc - 1)
                if cc < NCH - 1:
                    for h in range(H):
                        f, hr = h // 2, head_rows[h % 2]
                        m = mm(bank[4][hr, HD * f:HD * f + HD], tt[hr, cc, f, :], state[hr, cc - 1, f, :])
                    m.then_inc(s["st_pe"], 1)
                if cc >= 2:
                    pe.wait_ge(s["y_done"], cc - 1)
                for h in range(H):
                    f, hr = h // 2, head_rows[h % 2]
                    m = mm(bank[5][hr, HD * f:HD * f + HD], state[hr, cc - 1, f, :], gg[hr, f, CH * cc:CH * cc + CH])
                m.then_inc(s["yp_pe"], 1)

            pe.wait_ge(s["y_done"], 3)
            yflat = yT.rearrange("p f t -> p (f t)")
            for j in range(2):
                mm(bank[2 + j][:, :], head_mean, yflat[:, 512 * j:512 * j + 512]).then_inc(s["mu_pe"], 1)
            project_out(2, [2, 3])
            for j in range(2):
                pe.wait_ge(s["ysq_done"], j + 1)
                mm(bank[4 + j][:, :], head_mean, ysq[:, 512 * j:512 * j + 512]).then_inc(s["var_pe"], 1)
            project_out(3, range(FT))
            for f in range(FT):
                pe.wait_ge(s["mix_done"], f + 1)
                for n in range(3 if f == FT - 1 else 4):
                    m = project_out(n, [FT + f])
                    if f == FT - 1:
                        m.then_inc(s["wo_pe"], 1)

            def logits(t):
                pe.wait_ge(s["ht_done"], 2 * t + 2)
                pe.wait_ge(s["route_in"], 32)
                for k in range(KT):
                    m = mm(bank[2][:, E * t:E * t + E], hT[:, k, P * t:P * t + P], wrt[:, k, :], k == 0, k == KT - 1)
                m.then_inc(s["lg_pe"], 1)

            pe.wait_ge(s["sd_done"], 2)
            pe.wait_ge(s["h_done"], 2)
            model_transposes(hidden, bank[2:6], 0, s["ht_pe"])
            project_out(3, [KT - 1]).then_inc(s["wo_pe"], 1)
            logits(0)
            pe.wait_ge(s["h_done"], 4)
            model_transposes(hidden, bank[2:6], 1, s["ht_pe"])
            logits(1)
            pe.wait_ge(s["cb_in"], 32)
            pe.wait_ge(s["pick_done"], 1)
            tri, ones = cb[:, C_TRI:C_TRI + P], cb[:, C_ONE:C_ONE + P]
            mm(bank[3][:, 0:E], tri, picked[:, 0, :])
            mm(bank[3][:, E:2 * E], ones, picked[:, 0, :], True, False)
            mm(bank[3][:, E:2 * E], tri, picked[:, 1, :], False, True)
            mm(bank[3][0:E, 64:65], picked[:, 0, :], ones[:, 0:1], True, False)
            mm(bank[3][0:E, 64:65], picked[:, 1, :], ones[:, 0:1], False, True).then_inc(s["rank_pe"], 1)
            pe.wait_ge(s["extra_done"], 1)
            mm(bank[2][0:E, 0:1], tri[0:E, 0:E], extra[:, 2:3])
            mm(bank[2][0:1, 64:65], extra[:, 2:3], ones[0:E, 0:1]).then_inc(s["start_pe"], 1)
            pe.wait_ge(s["slot_done"], 1)
            for t in range(NT):
                pe.transpose(bank[5][0:E, P * t:P * t + P], slotv[:, t, :], ident)
                m = pe.transpose(bank[5][0:E, SEQ + P * t:SEQ + P * t + P], gates[:, t, :], ident)
            m.then_inc(s["svt_pe"], 1)
            xg = m_xg.rearrange("p (k c) -> p k c", k=KT)
            act_v = m_a.rearrange("p (q t) -> p t q", t=4)
            actT = m_at.rearrange("p (t c) -> p t c", t=4)

            def gather():
                for k in range(KT):
                    for n in range(6):
                        t, part = n // 3, n % 3
                        w = xsplit[:, t, part, :].rearrange("p (q k) -> p k q", k=KT)[:, k, :]
                        m = mm(b_x[:, SLOTS * k:SLOTS * k + SLOTS], w, m_p[:, t, :], n == 0, n == 5)
                m.then_inc(s["ga_pe"], 1)

            def scatter(t):
                for half in range(2):
                    r0 = slice(SLOTS * half, SLOTS * half + SLOTS)
                    m = mm(y_bank[2 * t + half][:, :], m_gt[r0, P * t:P * t + P], m_os[r0, :], False, False)
                return m

            pe.wait_ge(s["split_done"], 6)
            pe.wait_ge(s["count_done"], 1)
            n_items = pe.value_load(rint[0:1, ITEMS:ITEMS + 1], min_val=E, max_val=ITEMS)
            pe.wait_ge(s["p_ready"], 1)
            gather()
            pe.wait_ge(s["oh_done"], 1)
            pe.wait_ge(s["svt_done"], 1)
            for t in range(NT):
                mm(b_d[:, 64 * t:64 * t + ITEMS], svT[:, 0, P * t:P * t + P], oh, True, False)
                mm(b_d[:, 64 * t:64 * t + ITEMS], ones[0:E, :], back, False, True)
                mm(b_d[:, P + 64 * t:P + 64 * t + ITEMS], svT[:, 1, P * t:P * t + P], oh)
            mm(b_d[0:1, SEQ:SEQ + ITEMS], cb[0:E, C_ECOL:C_ECOL + 1], oh).then_inc(s["col_pe"], 1)
            pe.wait_ge(s["bsp_in"], 16 * 12)
            with pe.Fori(0, n_items) as i:
                pe.wait_ge(s["xg_ready"], i + 1)
                pe.wait_ge(s["gt_done"], i + 1)
                for c in range(4):
                    if c == 1:
                        pe.wait_ge(s["os_done"], i + 1)
                        scatter(0)
                    for k in range(2):
                        pe.wait_ge(s_ring[c][k], 16 * i + 16)
                        for col, b in ((0, b_g), (FF, b_u)):
                            for half in range(2):
                                c0 = 2 * FF * k + col + 512 * half
                                m = mm(b[SLOTS * half:SLOTS * half + SLOTS, :], xg[:, 2 * c + k, :], ring[:, c, c0:c0 + 512],
                                       c == 0 and k == 0, False)
                        m.then_inc(s_free, 1)
                pe.wait_ge(s["sel_ready"], i + 1)
                for col, b in ((0, b_g), (FF, b_u)):
                    for half in range(2):
                        m = mm(b[SLOTS * half:SLOTS * half + SLOTS, :], m_sel[0:3 * E, :],
                               bsp[0:3 * E, col // 512 + half, 0:512], False, True)
                m.then_inc(s["gu_pe"], 1)
                scatter(1)
                pe.wait_ge(s["p_ready"], i + 2)
                gather()
                pe.wait_ge(s["act_done"], i + 1)
                pe.wait_ge(s["items_done"], 1)
                for t in range(4):
                    m = pe.transpose(b_d[:, P * t:P * t + P], act_v[:, t, :], ident)
                m.then_inc(s["tr_pe"], 1)
                pe.wait_ge(s["g2_ready"], i + 1)
                for t in range(NT):
                    m = pe.transpose(b_g[:, P * t:P * t + P], m_g2[:, t, :], ident)
                m.then_inc(s["gtt_pe"], 1)
                pe.wait_ge(s["at_done"], i + 1)
                for h in range(2):
                    for t in range(4):
                        if t % 2 == 0:
                            pe.wait_ge(s_ring[4 + h][t // 2], 16 * i + 16)
                        for half in range(2):
                            m = mm(b_d[SLOTS * half:SLOTS * half + SLOTS, :], actT[:, t, SLOTS * h:SLOTS * h + SLOTS],
                                   ring[:, 4 + h, FF * t + 512 * half:FF * t + 512 * half + 512], h == 0 and t == 0, False)
                        if t % 2:
                            m.then_inc(s_free, 1)
                for half in range(2):
                    m = mm(b_d[SLOTS * half:SLOTS * half + SLOTS, :], m_sel[0:3 * E, :],
                           bsp[0:3 * E, 2 * half:2 * half + 2, 512:QB], False, True)
                m.then_inc(s["dn_pe"], 1)
            pe.wait_ge(s["os_done"], n_items + 1)
            pe.wait_ge(s["gt_done"], n_items + 1)
            for t in range(NT):
                scatter(t).then_inc(s["scf_pe"], 1)

        @block.scalar
        def _(act):
            def load_table(n, func):
                act.activation(st[:, 80 + n:81 + n], st[:, 6:7], func)

            act.wait_ge(s["zpad0"], 1)
            load_table(4, ACT.Sqrt)
            for t in range(NT):
                act.wait_ge(s_x[t], 16)
                act.activation(xn[:, t, :], resid[:, t, :], ACT.Square, accum_out=st[:, t:t + 1]).then_inc(s["a_chain"], 1)
                act.wait_ge(s["a_chain"], t + 1)
                act.activation(st[:, 2 + t:3 + t], st[:, t:t + 1], ACT.Sqrt, scale=1.0 / D, bias=st[:, 6:7]).then_inc(s["hsq_done"], 1)

            def copy_unit(u):
                act.wait_ge(s["proj_pe"], u + 1)
                if 2 <= u < 7:
                    act.wait_ge(s["zshift"], 2 * (u - 1))
                src = bank[u % 4][:, :].rearrange("p (j t) -> p j t", j=2)
                if u < 7:
                    act.copy(zpad[:, u % 2, :, 1:], src).then_inc(s["zcopy"], 1)
                elif u < 9:
                    act.mul(qA[:, 2 * (u - 7):2 * (u - 7) + 2, :], src, HD ** -0.5).then_inc(s["zcopy"], 1)
                elif u < 11:
                    act.copy(kA[:, 2 * (u - 9):2 * (u - 9) + 2, :], src).then_inc(s["zcopy"], 1)
                else:
                    act.copy(vA[:, u - 11, :], bank[u % 4][:, :]).then_inc(s["zcopy"], 1)

            act.wait_ge(s["zpad0"], 1)
            copy_unit(0)
            copy_unit(1)
            act.wait_ge(s["zshift"], 2)
            act.activation(lora[0:64, 0, :], lora[0:64, 0, :], ACT.Tanh).then_inc(s["tanh_done"], 1)
            act.activation(lora[:, 1, :], lora[:, 1, :], ACT.Sigmoid).then_inc(s["sgd_done"], 1)
            for f in range(FT):
                act.wait_ge(s["dec_pe"], f // 2 + 1)
                act.activation(tiles(sw)[:, f, :], bank[4 + f // 2][:, SEQ * (f % 2):SEQ * (f % 2) + SEQ], ACT.Sigmoid,
                               bias=vec("w0", f)).then_inc(s["sdec_done"], 1)
            for f in range(FT):
                act.wait_ge(s["icl_pe"], f // 2 + 1)
                act.activation(tiles(aT)[:, f, :], bank[6 + f // 2][:, SEQ * (f % 2):SEQ * (f % 2) + SEQ], ACT.Sigmoid,
                               bias=vec("a0", f)).then_inc(s["sicl_done"], 1)
            copy_unit(2)
            copy_unit(3)
            for j in range(2):
                act.wait_ge(s["gat_pe"], j + 1)
                act.copy(gT[:, 512 * j:512 * j + 512], bank[4 + j][:, :]).then_inc(s["gat_done"], 1)
            copy_unit(4)
            copy_unit(5)
            copy_unit(6)
            act.wait_ge(s["exps_done"], 1)
            act.activation(pinv, cum, ACT.Exp, scale=DECAY_C).then_inc(s["a_chain"], 1)
            act.activation(sw, sw, ACT.Exp, scale=-DECAY_C).then_inc(s["a_chain"], 1)
            act.wait_ge(s["a_chain"], 4)
            act.activation(cum, cum, ACT.Exp, scale=-DECAY_C).then_inc(s["a_chain"], 1)
            for j in range(2):
                act.wait_ge(s["ss_pe"], j + 1)
                act.activation(tmp[:, 512 * j:512 * j + 512], bank[6 + j][:, :], ACT.Sqrt).then_inc(s["nrm_done"], 1)
            for u in range(7, 13):
                copy_unit(u)
            def tok_copy(n):
                arr, t = n // 2, n % 2
                act.wait_ge(s["tok_pe"], n + 1)
                src = bank[n % 4][:, :]
                if arr == 0:
                    act.wait_ge(s["zero_done"], 2)
                    for c in range(2):
                        cr = slice(CH * c, CH * c + CH)
                        ins = act.copy(vtok[cr, t, c, :], src[cr, :])
                elif arr == 1:
                    ins = act.copy(amv[:, t, :, 0, :], src.rearrange("p (h j) -> p h j", h=H))
                else:
                    ins = act.copy((btok, ktok)[arr - 2][:, t, :], src)
                ins.then_inc(s["tok_done"], 1)

            load_table(0, ACT.Exp)
            tok_copy(0)
            tok_copy(1)

            def exps(h):
                f = h // 2
                act.wait_ge(s["s_max"], f + 1)
                if f >= 1:
                    act.wait_ge(s["et_pe"], h - 1)
                for j, (c0, n) in enumerate(((0, P), (P, SEQ))):
                    c = 16 + 2 * h + j
                    act.activation(sc_e[h % 2][:, c0:c0 + n], sc_s[h % 2][:, c0:c0 + n], ACT.Exp,
                                   bias=st[:, c:c + 1], accum_out=st[:, c + 16:c + 17]).then_inc(s["e_done"], 1)

            def et_copy(h):
                act.wait_ge(s["et_pe"], h + 1)
                if h >= 2:
                    act.wait_ge(s["pv_pe"], h // 2)
                act.copy(sc_t[h % 2], bank[h % 2][:, 0:3 * P]).then_inc(s["et_done"], 1)

            exps(0)
            exps(1)
            for n in range(2, 8):
                tok_copy(n)
            for f in range(FT):
                et_copy(2 * f)
                et_copy(2 * f + 1)
                if f + 1 < FT:
                    exps(2 * f + 2)
                    exps(2 * f + 3)
                act.wait_ge(s["pv_pe"], f + 1)
                act.copy(mixT[:, f, :], bank[2 + f % 2][:, 0:SEQ]).then_inc(s["attn_done"], 1)

            for t in range(NT):
                act.wait_ge(s["gram_pe"], 2 * t + 2)
                act.copy(low[t], bank[4 + t][:, :].rearrange("p (h s) -> p h s", h=H)).then_inc(s["low_done"], 1)
            for lv in range(2, LEVELS + 1):
                for t in range(NT):
                    act.wait_ge(s["t1_pe"], 2 * (lv - 2) + t + 1)
                    if lv > 2:
                        act.wait_ge(s["d_pe"], 4 * (lv - 3) + 2 * t + 2)
                    act.copy(t1s[t], bank[2 + t][:, :].rearrange("p (h s) -> p h s", h=H)).then_inc(s["t1_done"], 1)
            for t in range(NT):
                act.wait_ge(s["mv_pe"], t + 1)
                act.copy(amv[:, t, :, 1, :], bank[2 + t][:, :].rearrange("p (h j) -> p h j", h=H)).then_inc(s["mv_done"], 1)
            for t in range(NT):
                act.wait_ge(s["zw_pe"], t + 1)
                for j in range(2):
                    for c in range(2):
                        cr = slice(CH * c, CH * c + CH)
                        act.mul(nzw[t][cr, c, 4 * j:4 * j + 4, :], level_bank[t][j][cr, :].rearrange("p (h s) -> p h s", h=4),
                                -1.0).then_inc(s["zw_done"], 1)
            load_table(1, ACT.Sqrt)
            for j in range(2):
                act.wait_ge(s["yc_done"], j + 1)
                act.activation(ysq[:, 512 * j:512 * j + 512], yc[:, 512 * j:512 * j + 512], ACT.Square).then_inc(s["ysq_done"], 1)
            for j in range(2):
                act.wait_ge(s["var_pe"], j + 1)
                act.activation(yT.rearrange("p f t -> p (f t)")[:, 512 * j:512 * j + 512], bank[4 + j][:, :], ACT.Sqrt,
                               bias=st[:, 7:8]).then_inc(s["sd_done"], 1)
            def mean_square(t):
                act.wait_ge(s["h_done"], 2 * t + 2)
                act.activation(blk(B_I), hidden[:, t, :], ACT.Square, accum_out=st[:, 8 + t:9 + t]).then_inc(s["a_chain"], 1)
                act.wait_ge(s["a_chain"], 6 + t)
                act.activation(st[:, 10 + t:11 + t], st[:, 8 + t:9 + t], ACT.Sqrt, scale=1.0 / D, bias=st[:, 6:7]).then_inc(s["hsq_done"], 1)

            def split(t, part):
                if part == 0:
                    act.wait_ge(s["xs_done"], t + 1)
                else:
                    act.wait_ge(s[f"rem{t}_done"], part)
                act.copy(xsplit[:, t, part, :], xs[:, t, :] if part == 0 else xrem[:, t, :]).then_inc(s["split_done"], 1)

            mean_square(0)
            act.wait_ge(s["yp_pe"], 3)
            split(0, 0)
            mean_square(1)
            load_table(2, ACT.Exp)
            split(1, 0)
            split(0, 1)
            split(1, 1)
            act.wait_ge(s["lg_done"], 1)
            for t in range(NT):
                act.activation(ex4[:, t, :], mx8[:, t, 0:TOPK], ACT.Exp, bias=st[:, 48 + t:49 + t],
                               accum_out=st[:, 50 + t:51 + t]).then_inc(s["ex_done"], 1)
            split(0, 2)
            split(1, 2)
            act.wait_ge(s["svt_pe"], 1)
            act.copy(svT, bank[5][0:E, :].rearrange("p (w t) -> p w t", w=2)).then_inc(s["svt_done"], 1)

            act.wait_ge(s["count_done"], 1)
            n_items = act.value_load(rint[0:1, ITEMS:ITEMS + 1], min_val=E, max_val=ITEMS)
            with act.Fori(0, n_items) as i:
                act.wait_ge(s["gm_done"], i + 1)
                act.activation(m_s, m_g, ACT.Sigmoid, scale=ALPHA).then_inc(s["sg_done"], 1)
                act.wait_ge(s["tr_pe"], i + 1)
                act.copy(m_at, bank[5][:, :]).then_inc(s["at_done"], 1)
                act.wait_ge(s["gtt_pe"], i + 1)
                act.copy(m_gt, b_g[:, 0:SEQ]).then_inc(s["gt_done"], 1)
                act.wait_ge(s["dn_pe"], i + 1)
                act.copy(m_os, bank[5][:, :]).then_inc(s["os_done"], 1)
            load_table(3, ACT.Sqrt)
            for t in range(NT):
                for half in range(2):
                    n, o = 2 * t + half, slice(512 * half, 512 * half + 512)
                    act.wait_ge(s["yfin_done"], n + 1)
                    act.activation(stage[:, t, o], yout[:, t, o], ACT.Square, accum_out=st[:, 56 + n:57 + n]).then_inc(s["fsq_done"], 1)
                act.wait_ge(s["fsum_done"], t + 1)
                act.activation(st[:, 90 + t:91 + t], st[:, 88 + t:89 + t], ACT.Sqrt, scale=1.0 / D, bias=st[:, 6:7]).then_inc(s["frt_done"], 1)

        @block.gpsimd
        def _(pool):
            steps = [0]

            def link(ins):
                ins.then_inc(s["p_chain"], 1)
                steps[0] += 1
                pool.wait_ge(s["p_chain"], steps[0])

            pool.wait_ge(s["braw_in"], 16 * 8)
            pool.wait_ge(s["proj_pe"], 1)
            link(pool.tensor_copy(bpart[0], braw))
            link(pool.tensor_tensor(braw, braw, bpart[0], ALU.subtract))
            link(pool.tensor_copy(bpart[1], braw))
            link(pool.tensor_tensor(braw, braw, bpart[1], ALU.subtract))
            pool.tensor_copy(bpart[2], braw).then_inc(s["bsplit_done"], 1)
            pool.wait_ge(s["proj_pe"], 5)
            pool.memset(apart, 0.0).then_inc(s["zero_done"], 1)
            pool.wait_ge(s["proj_pe"], 9)
            pool.memset(work[:, 4096:6144], 0.0).then_inc(s["zero_done"], 1)
            pool.wait_ge(s["zero_done"], 2)
            for a, (src, ready) in enumerate(((aT, 2), (kT, 3))):
                pool.wait_ge(s["tilde_done"], ready)
                for j in range(2):
                    r = slice(HD * j, HD * j + HD)
                    pool.tensor_copy(heads_apart[r, j, a, :, :], tiles(src)[r, :, :]).then_inc(s["apart_done"], 1)
                    pool.wait_ge(s["apart_done"], 2 * a + j + 1)
            for lv in range(2, LEVELS + 1):
                for t in range(NT):
                    pool.wait_ge(s["low_done"], t + 1)
                    n = 2 * (lv - 2) + t
                    if n >= 2:
                        pool.wait_ge(s["t1_pe"], n - 1)
                    for c in range(2):
                        cr = slice(CH * c, CH * c + CH)
                        ins = pool.tensor_tensor(lml[t][cr, :, c, :], low[t][cr, :, :],
                                                 ca[cr, C_LEVEL + (lv - 1) * CH:C_LEVEL + lv * CH].unsqueeze(1).to_broadcast(
                                                     [CH, H, CH]), ALU.mult)
                        if c == 0:
                            link(ins)
                    ins.then_inc(s["lml_done"], 1)
                    pool.wait_ge(s["lml_done"], n + 1)
            pool.wait_ge(s["mix_done"], FT)
            for part in range(2):
                pool.wait_ge(s["split_done"], 2 * part + 1)
                if part:
                    pool.wait_ge(s["rem0_done"], 1)
                pool.tensor_tensor(xrem[:, 0, :], xs[:, 0, :] if part == 0 else xrem[:, 0, :], xsplit[:, 0, part, :],
                                   ALU.subtract).then_inc(s["rem0_done"], 1)

        @block.vector
        def _(v):
            steps = [0]

            def link(ins):
                ins.then_inc(s["v_chain"], 1)
                steps[0] += 1
                v.wait_ge(s["v_chain"], steps[0])

            def bc(col, n):
                return col.unsqueeze(2).to_broadcast([P, col.shape[1], n])

            def rows(ap):
                return ap.rearrange("p f t -> p (f t)")

            v.memset(st[:, 6:7], RMS_EPS)
            v.memset(st[:, 7:8], GN_EPS)
            v.memset(oh3[:, :], 0.0)
            v.memset(zpad[:, :, :, 0:1], 0.0).then_inc(s["zpad0"], 1)
            for t in range(NT):
                v.wait_ge(s["hsq_done"], t + 1)
                link(v.reciprocal(st[:, 4 + t:5 + t], st[:, 2 + t:3 + t]))
                v.tensor_scalar(xn[:, t, :], resid[:, t, :], st[:, 4 + t:5 + t], None, ALU.mult).then_inc(s["xn_done"], 1)

            def feature_major(dst, src, g, t, ready, done):
                for u in range(2):
                    v.wait_ge(ready, 2 * t + u + 1)
                    v.tensor_tensor(dst[:, 4 * u:4 * u + 4, P * t:P * t + P], src[2 * t + u][:, :].rearrange("p (k t) -> p k t", k=4),
                                    bc(g[:, 4 * u:4 * u + 4], P), ALU.mult).then_inc(done, 1)

            v.wait_ge(s["gm_in"], 16)
            for t in range(NT):
                feature_major(xT, bank[4:8], gmix, t, s["xt_pe"], s["xt_done"])
            v.wait_ge(s["vt_pe"], 1)
            v.tensor_copy(vcol[:, :], bank[3][:, 0:NV]).then_inc(s["vt_done"], 1)
            v.wait_ge(s["vt_done"], 1)

            def shift(u):
                v.wait_ge(s["zcopy"], u + 1)
                z = zpad[:, u % 2, :, :]
                if u == 0:
                    dst, m0 = lora[:, :, :], 12
                else:
                    dst = tiles((rT, kT, vT)[(u - 1) // 2])[:, 2 * ((u - 1) % 2):2 * ((u - 1) % 2) + 2, :]
                    m0 = 2 * (u - 1)
                if u == 1:
                    v.wait_ge(s["xt_pe"], 4)
                v.tensor_tensor(dst, z[:, :, 0:SEQ], z[:, :, 1:SEQ + 1], ALU.subtract).then_inc(s["zshift"], 1)
                v.wait_ge(s["zshift"], 2 * u + 1)
                for j in range(2):
                    ins = v.scalar_tensor_tensor(out=dst[:, j, :], in0=dst[:, j, :], scalar=vcol[:, m0 + j:m0 + j + 1],
                                                 in1=z[:, j, 1:SEQ + 1], op0=ALU.mult, op1=ALU.add)
                ins.then_inc(s["zshift"], 1)

            for u in range(3):
                shift(u)
            v.wait_ge(s["ca_in"], 16)
            v.wait_ge(s["sdec_done"], FT)
            for f in range(FT):
                ins = v.tensor_tensor_scan(tiles(cum)[:, f, :], scan_keep, tiles(sw)[:, f, :], 0.0, ALU.mult, ALU.add)
            link(ins)
            v.tensor_tensor(sw, cum, sw, ALU.subtract).then_inc(s["exps_done"], 1)
            shift(3)
            shift(4)
            v.wait_ge(s["zshift"], 10)
            for f in range(FT):
                ins = v.tensor_scalar(tiles(kkT)[:, f, :], tiles(kT)[:, f, :], vec("kk", f), None, ALU.mult)
            link(ins)
            v.tensor_tensor(tmp, kkT, kkT, ALU.mult).then_inc(s["sq_done"], 1)
            shift(5)
            shift(6)
            v.wait_ge(s["nrm_done"], 2)
            link(v.tensor_scalar(tmp, tmp, 1e-12, None, ALU.max))
            link(v.reciprocal(tmp, tmp))
            link(v.tensor_tensor(kkT, kkT, tmp, ALU.mult))
            v.wait_ge(s["sicl_done"], FT)
            for f in range(FT):
                ins = v.tensor_scalar(tiles(tmp)[:, f, :], tiles(aT)[:, f, :], -1.0, vec("ka", f), ALU.add, ALU.mult)
            link(ins)
            link(v.scalar_tensor_tensor(out=kT, in0=tmp, scalar=1.0, in1=kT, op0=ALU.add, op1=ALU.mult))
            v.wait_ge(s["zshift"], 14)
            for f in range(FT):
                ins = v.scalar_tensor_tensor(out=tiles(tmp)[:, f, :], in0=tiles(rT)[:, f, :], scalar=vec("rk", f),
                                             in1=tiles(kT)[:, f, :], op0=ALU.mult, op1=ALU.mult)
            ins.then_inc(s["bprod_done"], 1)
            v.wait_ge(s["a_chain"], 5)
            link(v.tensor_tensor(aT, aT, kkT, ALU.mult))
            v.tensor_tensor(ar[:, :, 0, :], tiles(kkT), tiles(sw), ALU.mult).then_inc(s["tilde_done"], 1)
            v.tensor_tensor(aT, aT, pinv, ALU.mult).then_inc(s["tilde_done"], 1)
            v.wait_ge(s["bprod_done"], 1)
            v.tensor_tensor(kT, kT, pinv, ALU.mult).then_inc(s["tilde_done"], 1)
            v.tensor_tensor(ar[:, :, 1, :], tiles(rT), tiles(cum), ALU.mult).then_inc(s["tilde_done"], 1)
            v.wait_ge(s["bsum_pe"], 2)
            v.wait_ge(s["tilde_done"], 4)
            for j in range(2):
                ins = v.tensor_tensor(kkT[:, 512 * j:512 * j + 512], bank[4 + j][:, :], vT[:, 512 * j:512 * j + 512], ALU.mult)
            ins.then_inc(s["bonus_done"], 1)

            v.wait_ge(s["bias_in"], 16)

            def biased(f):
                v.wait_ge(s["s_pe"], f + 1)
                if f >= 1:
                    v.wait_ge(s["e_done"], 4 * f)
                for hh in range(2):
                    b, h = bank[6 - 2 * (f % 2) + hh], 2 * f + hh
                    v.tensor_tensor_reduce(sc_s[hh][:, 0:P], b[:, 0:P], abias[:, h, P:SEQ], 1.0, -3e38,
                                           ALU.add, ALU.max, st[:, 60 + 2 * hh:61 + 2 * hh])
                    ins = v.tensor_tensor_reduce(sc_s[hh][:, P:3 * P], b[:, P:3 * P], abias[:, h, :], 1.0, -3e38,
                                                 ALU.add, ALU.max, st[:, 61 + 2 * hh:62 + 2 * hh])
                link(ins)
                v.tensor_scalar(st[:, 16 + 4 * f:20 + 4 * f], st[:, 60:64], -1.0, None, ALU.mult).then_inc(s["s_max"], 1)
                v.wait_ge(s["s_max"], f + 1)

            def normalise(f):
                for hh in range(2):
                    h = 2 * f + hh
                    v.wait_ge(s["e_done"], 2 * h + 2)
                    link(v.reciprocal(st[:, 66 + 2 * hh:68 + 2 * hh], st[:, 32 + 2 * h:34 + 2 * h]))
                    v.tensor_scalar(sc_e[hh][:, 0:P], sc_e[hh][:, 0:P], st[:, 66 + 2 * hh:67 + 2 * hh], None, ALU.mult)
                    v.tensor_scalar(sc_e[hh][:, P:3 * P], sc_e[hh][:, P:3 * P], st[:, 67 + 2 * hh:68 + 2 * hh], None,
                                    ALU.mult).then_inc(s["en_done"], 1)
                v.wait_ge(s["en_done"], 2 * f + 2)

            for f in range(FT):
                biased(f)
                normalise(f)

            v.wait_ge(s["attn_done"], FT)
            v.wait_ge(s["pv_pe"], FT)
            v.wait_ge(s["bsp_in"], 16 * 12)
            v.wait_ge(s["zero_done"], 1)
            for t in range(NT):
                for k in range(2):
                    v.wait_ge(s["gram_pe"], 2 * t + k + 1)
                    for j in range(2):
                        o = nm[t].rearrange("p (k r j) w s -> p k j r (w s)", k=2, j=2)[:, k, j]
                        v.tensor_tensor(o, bank[2 * k + j][:, :].rearrange("p (r x) -> p r x", r=2),
                                        mask4.unsqueeze(1).to_broadcast([P, 2, 4 * CH]), ALU.mult).then_inc(s["nm_done"], 1)
                v.wait_ge(s["nm_done"], 4 * t + 4)
                v.wait_ge(s["low_done"], t + 1)
                link(v.tensor_tensor(uu[t], low[t], level_mask(1), ALU.mult))
                for c in range(2):
                    cr = slice(CH * c, CH * c + CH)
                    ins = v.tensor_tensor(xx[t][cr, :, c, :], eye2[cr, :].unsqueeze(1).to_broadcast([CH, H, CH]), uu[t][cr, :, :],
                                          ALU.subtract)
                ins.then_inc(s["ux_done"], 1)
                v.wait_ge(s["ux_done"], 2 * t + 1)
                v.tensor_tensor(uu[t], eye2.unsqueeze(1).to_broadcast([P, H, CH]), nm[t][:, :, 0, :], ALU.subtract).then_inc(s["ux_done"], 1)
            for lv in range(2, LEVELS + 1):
                for t in range(NT):
                    v.wait_ge(s["ux_done"], 4 if lv == 2 else 4 * (lv - 2) + 2 * t + 2)
                    for j in range(2):
                        v.wait_ge(s["d_pe"], 4 * (lv - 2) + 2 * t + j + 1)
                        hs = slice(4 * j, 4 * j + 4)
                        d2 = level_bank[t][j][:, :].rearrange("p (h w s) -> p h w s", h=4, w=2)
                        if lv < LEVELS:
                            v.tensor_tensor(uu[t][:, hs, :], uu[t][:, hs, :], d2[:, :, 0, :], ALU.subtract)
                        for c in range(2):
                            cr, w = slice(CH * c, CH * c + CH), 1
                            old = xx[t][cr, hs, c, :]
                            if lv == LEVELS:
                                old, w = uu[t][cr, hs, :], 0
                            ins = v.tensor_tensor(xx[t][cr, hs, c, :], old, d2[cr, :, w, :], ALU.subtract)
                        ins.then_inc(s["ux_done"], 1)

            def heads(ap):
                return ap.rearrange("p (f t) -> p f t", f=FT)

            for t in range(NT):
                v.wait_ge(s["gc_pe"], t + 1)
                for c in range(2):
                    ts = slice(P * t + CH * c, P * t + CH * c + CH)
                    b = level_bank[t][c]
                    v.tensor_tensor(gg[:, :, ts], heads(b[:, 0:SEQ]), ar[:, :, 1, ts], ALU.add)
                    ins = v.tensor_copy(yT[:, :, ts], heads(b[:, SEQ:2 * SEQ]))
                ins.then_inc(s["gc_done"], 1)
                v.wait_ge(s["qu_pe"], t + 1)
                for c in range(2):
                    cc, b = 2 * t + c, bank[2 + c]
                    if 0 < cc < NCH - 1:
                        v.tensor_tensor(tt[:, cc, :, :], heads(b[:, 0:SEQ]), eye2.unsqueeze(1).to_broadcast([P, FT, HD]), ALU.add)
                    if cc < NCH - 1:
                        ins = v.tensor_tensor(state[:, cc, :, :], heads(b[:, SEQ:2 * SEQ]),
                                              bc(tiles(cum)[:, :, CH * cc + CH - 1], HD), ALU.mult)
                ins.then_inc(s["qu_done"], 1)
            for cc in range(1, NCH):
                if cc < NCH - 1:
                    v.wait_ge(s["st_pe"], cc)
                    link(v.tensor_tensor(stmp, heads(bank[4][:, 0:SEQ]), bc(tiles(cum)[:, :, CH * cc + CH - 1], HD), ALU.mult))
                    v.wait_ge(s["qu_done"], cc // 2 + 1)
                    v.tensor_tensor(state[:, cc, :, :], state[:, cc, :, :], stmp, ALU.add).then_inc(s["st_done"], 1)
                v.wait_ge(s["yp_pe"], cc)
                v.wait_ge(s["gc_done"], 2)
                o = yT[:, :, CH * cc:CH * cc + CH]
                v.tensor_tensor(o, heads(bank[5][:, 0:SEQ]), o, ALU.add).then_inc(s["y_done"], 1)

            v.wait_ge(s["y_done"], 3)
            for j in range(2):
                v.wait_ge(s["mu_pe"], j + 1)
                v.tensor_tensor(yc[:, 512 * j:512 * j + 512], rows(yT)[:, 512 * j:512 * j + 512], bank[2 + j][:, :],
                                ALU.subtract).then_inc(s["yc_done"], 1)
            for f in range(FT):
                y1, d1, o1 = tiles(yc)[:, f, :], yT[:, f, :], mixT[:, FT + f, :]
                v.wait_ge(s["sd_done"], f // 2 + 1)
                link(v.reciprocal(d1, d1))
                link(v.tensor_tensor(y1, y1, d1, ALU.mult))
                link(v.tensor_scalar(y1, y1, vec("gw", f), vec("gb", f), ALU.mult, ALU.add))
                link(v.tensor_tensor(y1, y1, tiles(kkT)[:, f, :], ALU.add))
                v.tensor_tensor(o1, y1, tiles(gT)[:, f, :], ALU.mult).then_inc(s["mix_done"], 1)
            def block_sum(t, half):
                o = slice(512 * half, 512 * half + 512)
                v.wait_ge(s["wo_pe"], 2 * t + half + 1)
                v.tensor_tensor(hidden[:, t, o], y_bank[2 * t + half][:, :], resid[:, t, o], ALU.add).then_inc(s["h_done"], 1)

            def unit(t):
                v.wait_ge(s["hsq_done"], 3 + t)
                link(v.reciprocal(st[:, 12 + t:13 + t], st[:, 10 + t:11 + t]))
                v.tensor_scalar(xs[:, t, :], hidden[:, t, :], st[:, 12 + t:13 + t], None, ALU.mult).then_inc(s["xs_done"], 1)

            v.wait_ge(s["cb_in"], 32)
            block_sum(0, 0)
            block_sum(0, 1)
            block_sum(1, 0)
            feature_major(hT, bank[2:6], gffn, 0, s["ht_pe"], s["ht_done"])
            block_sum(1, 1)
            unit(0)
            feature_major(hT, bank[2:6], gffn, 1, s["ht_pe"], s["ht_done"])
            unit(1)

            def remainder(part):
                v.wait_ge(s["split_done"], 2 * part + 2)
                if part:
                    v.wait_ge(s["rem1_done"], 1)
                v.tensor_tensor(xrem[:, 1, :], xs[:, 1, :] if part == 0 else xrem[:, 1, :], xsplit[:, 1, part, :],
                                ALU.subtract).then_inc(s["rem1_done"], 1)

            remainder(0)
            v.wait_ge(s["lg_pe"], 2)
            v.wait_ge(s["route_in"], 32)
            for t in range(NT):
                ins = v.scalar_tensor_tensor(out=lg[:, t, :], in0=bank[2][:, E * t:E * t + E], scalar=st[:, 12 + t:13 + t],
                                             in1=brt[:, :], op0=ALU.mult, op1=ALU.add)
            link(ins)
            for t in range(NT):
                link(v.max(mx8[:, t, :], lg[:, t, :]))
            v.tensor_scalar(st[:, 48:50], mx8[:, :, 0], -1.0, None, ALU.mult).then_inc(s["lg_done"], 1)
            for t in range(NT):
                link(v.max_index(idx8[:, t, :], mx8[:, t, :], lg[:, t, :]))
            link(v.tensor_copy(idxf, idx8[:, :, :]))
            iota = cb[:, C_IOTA32:C_IOTA32 + E]
            for t in range(NT):
                ins = v.tensor_tensor(onehot[:, t, :, :], iota.unsqueeze(1).to_broadcast([P, TOPK, E]),
                                      bc(idxf[:, t, 0:TOPK], E), ALU.is_equal)
            link(ins)
            for t in range(NT):
                ins = v.tensor_reduce(picked[:, t, :], onehot[:, t, :, :].rearrange("p j e -> p e j"), AX.X, ALU.add)
            ins.then_inc(s["pick_done"], 1)
            remainder(1)
            v.wait_ge(s["ex_done"], 2)
            link(v.reciprocal(st[:, 54:56], st[:, 50:52]))
            link(v.tensor_tensor(gt4, ex4, bc(st[:, 54:56], TOPK), ALU.mult))
            for t in range(NT):
                ins = v.tensor_tensor(onehot[:, t, :, :], onehot[:, t, :, :], bc(gt4[:, t, :], E), ALU.mult)
            link(ins)
            for t in range(NT):
                ins = v.tensor_reduce(gates[:, t, :], onehot[:, t, :, :].rearrange("p j e -> p e j"), AX.X, ALU.add)
            link(ins)
            v.wait_ge(s["rank_pe"], 1)
            v.wait_ge(s["pick_done"], 1)
            link(v.tensor_copy(cnt, bank[3][0:E, 64:65]))
            link(v.tensor_scalar(extra[:, 0:1], cnt, 1.0 * SLOTS, None, ALU.is_gt))
            link(v.scalar_tensor_tensor(out=extra[:, 1:2], in0=cnt, scalar=2.0 * SLOTS, in1=extra[:, 0:1], op0=ALU.is_gt, op1=ALU.add))
            v.scalar_tensor_tensor(out=extra[:, 2:3], in0=cnt, scalar=3.0 * SLOTS, in1=extra[:, 1:2], op0=ALU.is_gt,
                                   op1=ALU.add).then_inc(s["extra_done"], 1)
            link(v.scalar_tensor_tensor(out=slotv, in0=bank[3][:, 0:2 * E].rearrange("p (t e) -> p t e", t=NT), scalar=1.0,
                                        in1=picked, op0=ALU.add, op1=ALU.mult))
            v.tensor_scalar(slotv, slotv, -1.0, None, ALU.add).then_inc(s["slot_done"], 1)
            v.wait_ge(s["slot_done"], 1)
            v.tensor_copy(gcol[:, :, 0:E], gates)
            link(v.tensor_copy(colv[:, :, 0:E], slotv))

            iota2 = cb[:, C_IOTA2:C_IOTA2 + P]

            def one_hot(i):
                for t in range(NT):
                    ins = v.tensor_scalar(m_p[:, t, :], iota2[:, 0:SLOTS], colv[:, t, bass.ds(i, 1)], None, ALU.is_equal)
                ins.then_inc(s["p_ready"], 1)

            one_hot(0)
            v.memset(back, 0.0)
            v.tensor_copy(oh[:, 0:E], ident[0:E, 0:E])
            v.wait_ge(s["extra_done"], 1)
            v.wait_ge(s["start_pe"], 1)
            v.tensor_scalar(rint[0:1, ITEMS:ITEMS + 1], bank[2][0:1, 64:65], float(E), None, ALU.add).then_inc(s["count_done"], 1)
            link(v.tensor_copy(startc, bank[2][0:E, 0:1]))
            link(v.tensor_scalar(dj, cb[0:E, C_J:C_J + EXTRA], startc, None, ALU.subtract))
            link(v.tensor_scalar(oh[:, E:ITEMS], dj, 0.0, None, ALU.is_ge))
            link(v.scalar_tensor_tensor(out=oh[:, E:ITEMS], in0=dj, scalar=extra[:, 2:3], in1=oh[:, E:ITEMS],
                                        op0=ALU.is_lt, op1=ALU.mult))
            link(v.tensor_scalar(dj, dj, 1.0, -1.0 * SLOTS, ALU.add, ALU.mult))
            link(v.tensor_tensor(back[:, E:ITEMS], dj, oh[:, E:ITEMS], ALU.mult))
            for part in range(3):
                ins = v.tensor_copy(oh3[E * part:E * part + E, 0:ITEMS], oh)
            ins.then_inc(s["oh_done"], 1)
            v.wait_ge(s["split_done"], 6)
            v.memset(m_os, 0.0).then_inc(s["os_done"], 1)
            v.memset(m_gt, 0.0).then_inc(s["gt_done"], 1)
            v.wait_ge(s["count_done"], 1)
            n_items = v.value_load(rint[0:1, ITEMS:ITEMS + 1], min_val=E, max_val=ITEMS)

            def gate_matrix(i):
                for t in range(NT):
                    ins = v.tensor_scalar(m_g2[:, t, :], iota2, colv[:, t, bass.ds(i, 1)], gcol[:, t, bass.ds(i, 1)],
                                          ALU.is_equal, ALU.mult)
                ins.then_inc(s["g2_ready"], 1)

            def select(i):
                v.tensor_copy(m_sel[0:3 * E, :], oh3[0:3 * E, bass.ds(i, 1)].to_broadcast([3 * E, SLOTS])).then_inc(s["sel_ready"], 1)

            def gathered():
                v.tensor_tensor(m_xg.rearrange("p (k c) -> p k c", k=KT), b_x[:, :].rearrange("p (k c) -> p k c", k=KT),
                                bc(gffn[:, :], SLOTS), ALU.mult).then_inc(s["xg_ready"], 1)

            gate_matrix(0)
            v.wait_ge(s["oh_done"], 1)
            select(0)
            v.wait_ge(s["ga_pe"], 1)
            gathered()
            one_hot(1)
            v.wait_ge(s["col_pe"], 1)
            v.memset(colv[:, :, ITEMS:], 0.0)
            v.memset(gcol[:, :, ITEMS:], 0.0)
            v.tensor_copy(colv[:, :, E:ITEMS], b_d[:, 0:P].rearrange("p (t i) -> p t i", t=NT)[:, :, E:ITEMS])
            v.tensor_copy(gcol[:, :, E:ITEMS], b_d[:, P:2 * P].rearrange("p (t i) -> p t i", t=NT)[:, :, E:ITEMS])
            v.tensor_copy(rint[0:1, 0:ITEMS], b_d[0:1, SEQ:SEQ + ITEMS]).then_inc(s["items_done"], 1)
            v.wait_ge(s["items_done"], 1)
            with v.Fori(0, n_items) as i:
                v.wait_ge(s["gu_pe"], i + 1)
                v.tensor_scalar(m_g, b_g[:, :], LIMIT, None, ALU.min).then_inc(s["gm_done"], 1)
                v.tensor_scalar(m_u, b_u[:, :], LIMIT, -LIMIT, ALU.min, ALU.max).then_inc(s["um_done"], 1)
                v.wait_ge(s["gm_done"], i + 1)
                v.wait_ge(s["um_done"], i + 1)
                v.scalar_tensor_tensor(out=m_t, in0=m_u, scalar=1.0, in1=m_g, op0=ALU.add, op1=ALU.mult).then_inc(s["t_done"], 1)
                v.wait_ge(s["t_done"], i + 1)
                v.wait_ge(s["sg_done"], i + 1)
                v.tensor_tensor(m_a, m_t, m_s, ALU.mult).then_inc(s["act_done"], 1)
                v.wait_ge(s["ga_pe"], i + 2)
                gathered()
                one_hot(i + 2)
                v.wait_ge(s["gtt_pe"], i + 1)
                gate_matrix(i + 1)
                v.wait_ge(s["dn_pe"], i + 1)
                select(i + 1)
            v.wait_ge(s["gfin_in"], 16)
            def total(n):
                t, o = n // 2, slice(512 * (n % 2), 512 * (n % 2) + 512)
                v.wait_ge(s["scf_pe"], t + 1)
                v.tensor_tensor(yout[:, t, o], y_bank[n][:, :], resid[:, t, o], ALU.add).then_inc(s["yfin_done"], 1)

            def finish(t):
                v.wait_ge(s["frt_done"], t + 1)
                link(v.reciprocal(st[:, 64 + t:65 + t], st[:, 90 + t:91 + t]))
                for half in range(2):
                    o = slice(512 * half, 512 * half + 512)
                    v.scalar_tensor_tensor(out=yout[:, t, o], in0=yout[:, t, o], scalar=st[:, 64 + t:65 + t],
                                           in1=gfin[:, o], op0=ALU.mult, op1=ALU.mult).then_inc(s["fin_done"], 1)

            def sum_halves(t):
                v.wait_ge(s["fsq_done"], 2 * t + 2)
                v.tensor_tensor(st[:, 88 + t:89 + t], st[:, 56 + 2 * t:57 + 2 * t], st[:, 57 + 2 * t:58 + 2 * t], ALU.add).then_inc(s["fsum_done"], 1)

            total(0)
            total(1)
            total(2)
            sum_halves(0)
            total(3)
            finish(0)
            sum_halves(1)
            finish(1)


_INS = ["x", "norm_mix_g", "w_in", "shift_mu", "decay_w0", "w_decay_up", "iclr_a0", "w_iclr_up", "w_gate_lr_up", "k_k", "k_a",
        "r_k", "gn_w", "gn_b", "w_out", "norm_ffn_g", "w_router", "b_router", "w_gate_up", "b_gate_up", "w_down", "b_down",
        "norm_final_g"]


def kernel(**inputs):
    import concourse.bacc as _bacc
    from concourse.bass_utils import run_bass_kernel_spmd as _run

    nc = _bacc.Bacc("TRN2", target_bir_lowering=False, num_devices=1)
    arrays, args = {}, []
    named = [(n, np.ascontiguousarray(inputs[n])) for n in _INS]
    named += list(zip(("const_a", "const_bias", "const_b"), shape_constants()))
    for name, a in named:
        arrays[f"in_{name}"] = a
        args.append(nc.dram_tensor(f"in_{name}", a.shape, mybir.dt.from_np(a.dtype), kind="ExternalInput").ap())
    args.append(nc.dram_tensor("out_0", (1, SEQ, D), F32, kind="ExternalOutput").ap())
    program(nc, *args)
    r = _run(nc, [arrays], core_ids=[0])
    return r.results[0]["out_0"]
```
